# Optimizing a Trainium2 kernel written in Bass

```python
import math
import jax, jax.numpy as jnp
from jax import lax
import numpy as np

D_MODEL = 1024
BATCH = 1
SEQ = 256
DEPTH = 1

PLE_DIM = 256
EPS = 1e-6
SSD_HEADS = 16
SSD_HEAD_DIM = 64
SSD_INNER = SSD_HEADS * SSD_HEAD_DIM
SSD_GROUPS = 2
SSD_STATE = 64
SSD_CONV = 4
SSD_CHUNK = 128
SSD_CONV_CH = SSD_INNER + 2 * SSD_GROUPS * SSD_STATE
ATT_HEADS = 16
ATT_HEAD_DIM = 64
ATT_INNER = ATT_HEADS * ATT_HEAD_DIM
MOBA_BLOCK = 256
MOBA_TOPK = 3
MOBA_QCHUNK = 16
ROPE_THETA = 10000.0
IN_SPLITS = (SSD_INNER, SSD_CONV_CH, SSD_HEADS, ATT_INNER, ATT_INNER, ATT_INNER, D_MODEL, D_MODEL)
IN_WIDTH = 7440
N_GROUPS = 4
EXPERTS_PER_GROUP = 8
TOPK_IN_GROUP = 2
D_EXPERT = 256


def rms_norm(x, w):
    xf = x.astype(jnp.float32)
    inv = lax.rsqrt(jnp.mean(xf * xf, axis=-1, keepdims=True) + EPS)
    return (xf * inv).astype(x.dtype) * w

def split_columns(proj):
    offs = np.cumsum(IN_SPLITS)[:-1].tolist()
    return jnp.split(proj, offs, axis=-1)

def rope(x, positions):
    half = x.shape[-1] // 2
    inv_freq = ROPE_THETA ** (-jnp.arange(half, dtype=jnp.float32) / half)
    ang = positions.astype(jnp.float32)[..., None] * inv_freq
    cos = jnp.cos(ang)[:, :, None, :].astype(x.dtype)
    sin = jnp.sin(ang)[:, :, None, :].astype(x.dtype)
    x1, x2 = x[..., :half], x[..., half:]
    return jnp.concatenate([x1 * cos - x2 * sin, x2 * cos + x1 * sin], axis=-1)

def causal_dwconv(u, w, b):
    out = lax.conv_general_dilated(
        u, w[:, None, :].astype(u.dtype), window_strides=(1,),
        padding=((SSD_CONV - 1, 0),), dimension_numbers=("NWC", "WIO", "NWC"),
        feature_group_count=u.shape[-1])
    return out + b

def ssd_mixer(z, xbc, dt_raw, conv_w, conv_b, dt_bias, a_log, d_skip, norm_w):
    b, L, _ = z.shape
    nc = L // SSD_CHUNK
    E = SSD_HEADS // SSD_GROUPS
    xbc = jax.nn.silu(causal_dwconv(xbc, conv_w, conv_b))
    xs, Bm, Cm = jnp.split(xbc, [SSD_INNER, SSD_INNER + SSD_GROUPS * SSD_STATE], axis=-1)
    dt = jax.nn.softplus(dt_raw.astype(jnp.float32) + dt_bias.astype(jnp.float32))
    A = -jnp.exp(a_log.astype(jnp.float32)).reshape(SSD_GROUPS, E)
    X = xs.reshape(b, nc, SSD_CHUNK, SSD_GROUPS, E, SSD_HEAD_DIM)
    Bc = Bm.reshape(b, nc, SSD_CHUNK, SSD_GROUPS, SSD_STATE)
    Cc = Cm.reshape(b, nc, SSD_CHUNK, SSD_GROUPS, SSD_STATE)
    dtc = dt.reshape(b, nc, SSD_CHUNK, SSD_GROUPS, E)
    Xdt = X * dtc[..., None].astype(X.dtype)
    dA = jnp.transpose(dtc * A, (0, 1, 3, 4, 2))
    A_cum = jnp.cumsum(dA, axis=-1)
    idx = jnp.arange(SSD_CHUNK)
    causal = idx[:, None] >= idx[None, :]
    Lmat = jnp.exp(jnp.where(causal, A_cum[..., :, None] - A_cum[..., None, :], -jnp.inf))
    CB = jnp.einsum("bclgn,bcsgn->bcgls", Cc, Bc)
    M = (CB[:, :, :, None] * Lmat).astype(X.dtype)
    y_diag = jnp.einsum("bcgels,bcsgep->bclgep", M, Xdt)
    decay_states = jnp.exp(A_cum[..., -1:] - A_cum).astype(X.dtype)
    states = jnp.einsum("bclgn,bcgel,bclgep->bcgepn", Bc, decay_states, Xdt)
    chunk_decay = jnp.exp(A_cum[..., -1])

    def step(h, inp):
        s_c, d_c = inp
        return h * d_c[..., None, None] + s_c, h

    h0 = jnp.zeros((b, SSD_GROUPS, E, SSD_HEAD_DIM, SSD_STATE), jnp.float32)
    _, prev = lax.scan(step, h0, (jnp.moveaxis(states, 1, 0).astype(jnp.float32),
                                  jnp.moveaxis(chunk_decay, 1, 0)))
    prev = jnp.moveaxis(prev, 0, 1).astype(X.dtype)
    y_off = jnp.einsum("bclgn,bcgepn,bcgel->bclgep", Cc, prev, jnp.exp(A_cum).astype(X.dtype))
    y = y_diag + y_off + X * d_skip.reshape(SSD_GROUPS, E)[:, :, None].astype(X.dtype)
    y = y.reshape(b, L, SSD_INNER)
    yg = (y * jax.nn.silu(z)).reshape(b, L, SSD_GROUPS, SSD_INNER // SSD_GROUPS)
    return rms_norm(yg, norm_w.reshape(SSD_GROUPS, -1)).reshape(b, L, SSD_INNER)

def moba_attention(q, k, v):
    b, L, H, Dh = q.shape
    Lp = -(-L // MOBA_BLOCK) * MOBA_BLOCK
    nb = Lp // MOBA_BLOCK
    n_sel = min(MOBA_TOPK, nb - 1)
    pad = ((0, 0), (0, Lp - L), (0, 0), (0, 0))
    qh = jnp.pad(q, pad).transpose(0, 2, 1, 3)
    k_blocks = jnp.pad(k, pad).transpose(0, 2, 1, 3).reshape(b, H, nb, MOBA_BLOCK, Dh)
    v_blocks = jnp.pad(v, pad).transpose(0, 2, 1, 3).reshape(b, H, nb, MOBA_BLOCK, Dh)
    k_mean = jnp.mean(k_blocks.astype(jnp.float32), axis=3).astype(q.dtype)
    scale = Dh ** -0.5
    bi = jnp.arange(b)[:, None, None, None]
    hi = jnp.arange(H)[None, :, None, None]
    kpos_in_blk = jnp.arange(MOBA_BLOCK)

    def chunk(c):
        q0 = c * MOBA_QCHUNK
        qc = lax.dynamic_slice_in_dim(qh, q0, MOBA_QCHUNK, axis=2)
        qpos = q0 + jnp.arange(MOBA_QCHUNK)
        own = q0 // MOBA_BLOCK
        own_idx = jnp.broadcast_to(own, (b, H, MOBA_QCHUNK, 1)).astype(jnp.int32)
        if n_sel > 0:
            gate = jnp.einsum("bhqd,bhnd->bhqn", qc, k_mean).astype(jnp.float32)
            gate = jnp.where(jnp.arange(nb) < own, gate, -jnp.inf)
            _, sel = lax.top_k(gate, n_sel)
            sel = sel.astype(jnp.int32)
            blk_idx = jnp.concatenate([sel, own_idx], axis=-1)
            slot_ok = jnp.concatenate([sel < own, jnp.ones(own_idx.shape, bool)], axis=-1)
        else:
            blk_idx = own_idx
            slot_ok = jnp.ones(own_idx.shape, bool)
        kg = k_blocks[bi, hi, blk_idx]
        vg = v_blocks[bi, hi, blk_idx]
        s = jnp.einsum("bhqd,bhqjkd->bhqjk", qc, kg).astype(jnp.float32) * scale
        kpos = blk_idx[..., None] * MOBA_BLOCK + kpos_in_blk
        mask = slot_ok[..., None] & (kpos <= qpos[:, None, None])
        s = jnp.where(mask, s, -jnp.inf)
        pr = jax.nn.softmax(s.reshape(b, H, MOBA_QCHUNK, -1), axis=-1).reshape(s.shape)
        return jnp.einsum("bhqjk,bhqjkd->bhqd", pr.astype(vg.dtype), vg)

    out = lax.map(chunk, jnp.arange(Lp // MOBA_QCHUNK))
    out = out.transpose(1, 0, 3, 2, 4).reshape(b, Lp, H, Dh)
    return out[:, :L]

def hybrid_mixer(h, positions, w_in, conv_w, conv_b, dt_bias, a_log, d_skip, ssd_norm_w,
                 w_ssd_out, w_attn_out, w_out):
    b, L, _ = h.shape
    z, xbc, dt_raw, q, k, v, g_ssd, g_att = split_columns(h @ w_in)
    y_ssd = ssd_mixer(z, xbc, dt_raw, conv_w, conv_b, dt_bias, a_log, d_skip, ssd_norm_w) @ w_ssd_out
    q = rope(q.reshape(b, L, ATT_HEADS, ATT_HEAD_DIM), positions)
    k = rope(k.reshape(b, L, ATT_HEADS, ATT_HEAD_DIM), positions)
    v = v.reshape(b, L, ATT_HEADS, ATT_HEAD_DIM)
    y_att = moba_attention(q, k, v).reshape(b, L, ATT_INNER) @ w_attn_out
    merged = jax.nn.sigmoid(g_ssd) * y_ssd + jax.nn.sigmoid(g_att) * y_att
    return merged @ w_out

def hier_moe(h, w_rg, b_rg, w_re, b_re, w_gate, w_up, w_down):
    b, L, _ = h.shape
    gl = (h @ w_rg).astype(jnp.float32) + b_rg.astype(jnp.float32)
    gp = jax.nn.softmax(gl, axis=-1)
    _, gi = lax.top_k(gl, 1)
    g_oh = jax.nn.one_hot(gi[..., 0], N_GROUPS, dtype=jnp.float32)
    g_w = jnp.sum(gp * g_oh, axis=-1)
    el = ((h @ w_re).astype(jnp.float32) + b_re.astype(jnp.float32)).reshape(b, L, N_GROUPS, EXPERTS_PER_GROUP)
    el_sel = jnp.einsum("blge,blg->ble", el, g_oh)
    top_v, top_i = lax.top_k(el_sel, TOPK_IN_GROUP)
    top_w = jax.nn.softmax(top_v, axis=-1) * g_w[..., None]
    e_w = jnp.sum(jax.nn.one_hot(top_i, EXPERTS_PER_GROUP, dtype=jnp.float32) * top_w[..., None], axis=-2)
    comb = (g_oh[..., None] * e_w[..., None, :]).astype(h.dtype)
    out = jnp.zeros_like(h)
    for g in range(N_GROUPS):
        hid = jax.nn.silu(jnp.einsum("bld,edf->blef", h, w_gate[g])) * jnp.einsum("bld,edf->blef", h, w_up[g])
        out = out + jnp.einsum("blef,ble,efd->bld", hid, comb[:, :, g], w_down[g])
    return out

def first_inputs(seed: int = 0) -> dict:
    key = jax.random.key(seed)
    ks = jax.random.split(key, 32)
    f32 = jnp.float32

    def nrm(k, shape, fan_in):
        return jax.random.normal(k, shape, f32) * (fan_in ** -0.5)

    def gain(k, shape):
        return 1.0 + 0.05 * jax.random.normal(k, shape, f32)

    dt0 = jnp.exp(jax.random.uniform(ks[5], (DEPTH, SSD_HEADS), f32, math.log(1e-3), math.log(1e-1)))
    dt_bias = dt0 + jnp.log(-jnp.expm1(-dt0))
    return {
        "x": jax.random.normal(ks[0], (BATCH, SEQ, D_MODEL), f32),
        "p": jax.random.normal(ks[1], (DEPTH, BATCH, SEQ, PLE_DIM), f32),
        "positions": (jnp.arange(SEQ, dtype=jnp.int32)[None, :]
                      + jax.random.randint(ks[2], (BATCH, 1), 0, 1024, dtype=jnp.int32)),
        "attn_norm_w": gain(ks[3], (DEPTH, D_MODEL)),
        "w_in": nrm(ks[4], (DEPTH, D_MODEL, IN_WIDTH), D_MODEL),
        "conv_w": nrm(ks[6], (DEPTH, SSD_CONV, SSD_CONV_CH), SSD_CONV),
        "conv_b": 0.02 * jax.random.normal(ks[7], (DEPTH, SSD_CONV_CH), f32),
        "dt_bias": dt_bias,
        "a_log": jnp.log(jax.random.uniform(ks[8], (DEPTH, SSD_HEADS), f32, 1.0, 16.0)),
        "d_skip": 1.0 + 0.1 * jax.random.normal(ks[9], (DEPTH, SSD_HEADS), f32),
        "ssd_norm_w": gain(ks[10], (DEPTH, SSD_INNER)),
        "w_ssd_out": nrm(ks[11], (DEPTH, SSD_INNER, D_MODEL), SSD_INNER),
        "w_attn_out": nrm(ks[12], (DEPTH, ATT_INNER, D_MODEL), ATT_INNER),
        "w_out": nrm(ks[13], (DEPTH, D_MODEL, D_MODEL), D_MODEL),
        "moe_norm_w": gain(ks[14], (DEPTH, D_MODEL)),
        "w_router_group": nrm(ks[15], (DEPTH, D_MODEL, N_GROUPS), D_MODEL),
        "b_router_group": 0.01 * jax.random.normal(ks[16], (DEPTH, N_GROUPS), f32),
        "w_router_expert": nrm(ks[17], (DEPTH, D_MODEL, N_GROUPS * EXPERTS_PER_GROUP), D_MODEL),
        "b_router_expert": 0.01 * jax.random.normal(ks[18], (DEPTH, N_GROUPS * EXPERTS_PER_GROUP), f32),
        "w_exp_gate": nrm(ks[19], (DEPTH, N_GROUPS, EXPERTS_PER_GROUP, D_MODEL, D_EXPERT), D_MODEL),
        "w_exp_up": nrm(ks[20], (DEPTH, N_GROUPS, EXPERTS_PER_GROUP, D_MODEL, D_EXPERT), D_MODEL),
        "w_exp_down": nrm(ks[21], (DEPTH, N_GROUPS, EXPERTS_PER_GROUP, D_EXPERT, D_MODEL), D_EXPERT),
        "ple_norm_w": gain(ks[22], (DEPTH, D_MODEL)),
        "w_ple": nrm(ks[23], (DEPTH, PLE_DIM, D_MODEL), PLE_DIM),
        "w_ple_gate": nrm(ks[24], (DEPTH, D_MODEL, D_MODEL), D_MODEL),
        "final_norm_w": gain(ks[25], (D_MODEL,)),
    }

def first_block(x, p, positions, attn_norm_w, w_in, conv_w, conv_b, dt_bias, a_log, d_skip,
              ssd_norm_w, w_ssd_out, w_attn_out, w_out, moe_norm_w, w_router_group,
              b_router_group, w_router_expert, b_router_expert, w_exp_gate, w_exp_up,
              w_exp_down, ple_norm_w, w_ple, w_ple_gate, final_norm_w):
    for i in range(DEPTH):
        h = rms_norm(x, attn_norm_w[i])
        x = x + hybrid_mixer(h, positions, w_in[i], conv_w[i], conv_b[i], dt_bias[i], a_log[i],
                             d_skip[i], ssd_norm_w[i], w_ssd_out[i], w_attn_out[i], w_out[i])
        h = rms_norm(x, moe_norm_w[i])
        x = x + hier_moe(h, w_router_group[i], b_router_group[i], w_router_expert[i],
                         b_router_expert[i], w_exp_gate[i], w_exp_up[i], w_exp_down[i])
        gate = jax.nn.sigmoid(rms_norm(x, ple_norm_w[i]) @ w_ple_gate[i])
        x = x + gate * (p[i] @ w_ple[i])
    return rms_norm(x, final_norm_w)


DEPTH_2 = 4

N_MIXERS = 3
N_A_LAYERS = (DEPTH_2 + 2) // 3
N_B_LAYERS = (DEPTH_2 + 1) // 3
N_C_LAYERS = DEPTH_2 // 3

RMS_EPS = 1e-6
CONV_W = 3

NA_HEAD_DIM = 64
NA_HEADS = D_MODEL // NA_HEAD_DIM
GRID_W = 64
NA_MAX_ROWS = 8
NA_COLS = 16
NA_QCOLS = 16
NA_SPAN = NA_QCOLS + NA_COLS

HYENA_ORDER = 2
HYENA_BANDS = 16
HYENA_EMB = 1 + 2 * HYENA_BANDS
HYENA_FILTER_HIDDEN = 64
HYENA_DECAY_TARGET = 1e-2
HYENA_FAST_DECAY = 0.3
HYENA_SLOW_DECAY = 1.5

FFN_HIDDEN = ((8 * D_MODEL + 3 * 256 - 1) // (3 * 256)) * 256


def rmsnorm(x, g):
    xf = x.astype(jnp.float32)
    y = xf * lax.rsqrt(jnp.mean(xf * xf, axis=-1, keepdims=True) + RMS_EPS)
    return (y * g.astype(jnp.float32)).astype(x.dtype)

def depthwise_conv3(x, w, b=None):
    c = x.shape[-1]
    y = lax.conv_general_dilated(
        x, w.astype(x.dtype)[:, None, :], (1,), ((CONV_W // 2, CONV_W // 2),),
        dimension_numbers=('NWC', 'WIO', 'NWC'), feature_group_count=c)
    return y if b is None else y + b.astype(x.dtype)

def short_conv_mixer(h, w_in, conv_w, w_out):
    b_gate, c_gate, u = jnp.split(h @ w_in, 3, axis=-1)
    return (b_gate * depthwise_conv3(c_gate * u, conv_w)) @ w_out

def na_column_tables():
    cb = np.arange(GRID_W // NA_QCOLS)
    starts = np.clip(cb * NA_QCOLS - NA_COLS // 2, 0, GRID_W - NA_SPAN)
    key_col = starts[:, None] + np.arange(NA_SPAN)
    q_col = cb[:, None] * NA_QCOLS + np.arange(NA_QCOLS)
    col_start = np.clip(q_col - NA_COLS // 2, 0, GRID_W - NA_COLS)
    kc = key_col[:, None, :]
    valid = (kc >= col_start[:, :, None]) & (kc < col_start[:, :, None] + NA_COLS)
    dc_idx = np.clip(kc - q_col[:, :, None] + NA_COLS - 1, 0, 2 * NA_COLS - 2)
    return key_col, valid, dc_idx

def neighborhood_attention(h, w_qkv, q_g, k_g, rpb, w_out):
    bsz, seq, d = h.shape
    rows = seq // GRID_W
    wr = min(NA_MAX_ROWS, rows)
    q, k, v = jnp.split(h @ w_qkv, 3, axis=-1)
    grid = (bsz, rows, GRID_W, NA_HEADS, NA_HEAD_DIM)
    q = rmsnorm(q.reshape(grid), q_g)
    k = rmsnorm(k.reshape(grid), k_g)
    v = v.reshape(grid)
    key_col, valid, dc_idx = na_column_tables()
    ncb = key_col.shape[0]
    scale = NA_HEAD_DIM ** -0.5
    neg = jnp.finfo(jnp.float32).min
    mask = valid[None, None, :, :, None, :]

    def row_block(r):
        rs = jnp.clip(r - wr // 2, 0, rows - wr)
        q_r = lax.dynamic_index_in_dim(q, r, axis=1, keepdims=False)
        q_r = q_r.reshape(bsz, ncb, NA_QCOLS, NA_HEADS, NA_HEAD_DIM)
        k_r = lax.dynamic_slice_in_dim(k, rs, wr, axis=1)[:, :, key_col]
        v_r = lax.dynamic_slice_in_dim(v, rs, wr, axis=1)[:, :, key_col]
        s = jnp.einsum('bnqhd,brnkhd->bhnqrk', q_r, k_r).astype(jnp.float32) * scale
        dr_idx = rs + jnp.arange(wr) - r + NA_MAX_ROWS - 1
        bias = rpb[:, dr_idx[None, None, :, None], dc_idx[:, :, None, :]]
        s = jnp.where(mask, s + bias.astype(jnp.float32)[None], neg)
        p = jax.nn.softmax(s.reshape(s.shape[:4] + (wr * NA_SPAN,)), axis=-1)
        p = p.reshape(s.shape).astype(v.dtype)
        o = jnp.einsum('bhnqrk,brnkhd->bnqhd', p, v_r)
        return o.reshape(bsz, GRID_W, d)

    o = lax.map(row_block, jnp.arange(rows))
    return o.transpose(1, 0, 2, 3).reshape(bsz, seq, d) @ w_out

def hyena_filters(seq, w1, b1, w2, b2, w3, freq):
    f32 = jnp.float32
    t = jnp.linspace(0.0, 1.0, seq, dtype=f32)[:, None]
    bands = jnp.linspace(1e-4, HYENA_BANDS - 1, HYENA_BANDS, dtype=f32)
    ang = (2.0 * math.pi) * jnp.arange(seq, dtype=f32)[:, None] / seq * bands
    z = jnp.concatenate([t, jnp.cos(ang), -jnp.sin(ang)], axis=-1)
    fr = freq.astype(f32)
    hid = jnp.sin(fr * (z @ w1.astype(f32) + b1.astype(f32)))
    hid = jnp.sin(fr * (hid @ w2.astype(f32) + b2.astype(f32)))
    filt = (hid @ w3.astype(f32)).reshape(seq, HYENA_ORDER, 2, D_MODEL)
    lt = math.log(HYENA_DECAY_TARGET)
    deltas = jnp.abs(jnp.linspace(lt / HYENA_SLOW_DECAY, lt / HYENA_FAST_DECAY, D_MODEL, dtype=f32))
    filt = filt * jnp.exp(-t * deltas)[:, None, None, :]
    fwd, rev = filt[:, :, 0], filt[:, :, 1]
    h_full = jnp.concatenate([fwd[:1] + rev[:1], fwd[1:], jnp.zeros_like(fwd[:1]), rev[:0:-1]], axis=0)
    h_full = h_full / jnp.sum(jnp.abs(h_full), axis=0, keepdims=True)
    return jnp.fft.rfft(h_full, axis=0)

def hyena_mixer(h, w_in, short_w, short_b, f_w1, f_b1, f_w2, f_b2, f_w3, f_freq, f_skip, w_out):
    seq = h.shape[1]
    v, x1, x2 = jnp.split(depthwise_conv3(h @ w_in, short_w, short_b), 3, axis=-1)
    h_freq = hyena_filters(seq, f_w1, f_b1, f_w2, f_b2, f_w3, f_freq)

    def long_conv(u, n):
        uf = u.astype(jnp.float32)
        y = jnp.fft.irfft(jnp.fft.rfft(uf, n=2 * seq, axis=1) * h_freq[:, n], n=2 * seq, axis=1)[:, :seq]
        return (y + uf * f_skip[n].astype(jnp.float32)).astype(u.dtype)

    z = x1 * long_conv(v, 0)
    z = x2 * long_conv(z, 1)
    return z @ w_out

def swiglu(h, w13, w2):
    g, u = jnp.split(h @ w13, 2, axis=-1)
    return (jax.nn.silu(g) * u) @ w2

def second_inputs(seed: int = 0) -> dict:
    key = jax.random.key(seed)
    ks = jax.random.split(key, 24)
    f32 = jnp.float32

    def nrm(k, shape, fan_in):
        return jax.random.normal(k, shape, f32) * (fan_in ** -0.5)

    def gain(k, shape):
        return 1.0 + 0.02 * jax.random.normal(k, shape, f32)

    def small(k, shape, s=0.02):
        return s * jax.random.normal(k, shape, f32)

    D = D_MODEL
    return {
        'x': jax.random.normal(ks[0], (BATCH, SEQ, D), f32),
        'norm_mix_g': gain(ks[1], (DEPTH_2, D)),
        'norm_ffn_g': gain(ks[2], (DEPTH_2, D)),
        'a_w_in': nrm(ks[3], (N_A_LAYERS, D, 3 * D), D),
        'a_conv_w': nrm(ks[4], (N_A_LAYERS, CONV_W, D), CONV_W),
        'a_w_out': nrm(ks[5], (N_A_LAYERS, D, D), D),
        'b_w_qkv': nrm(ks[6], (N_B_LAYERS, D, 3 * D), D),
        'b_q_norm_g': gain(ks[7], (N_B_LAYERS, NA_HEAD_DIM)),
        'b_k_norm_g': gain(ks[8], (N_B_LAYERS, NA_HEAD_DIM)),
        'b_rpb': small(ks[9], (N_B_LAYERS, NA_HEADS, 2 * NA_MAX_ROWS - 1, 2 * NA_COLS - 1)),
        'b_w_out': nrm(ks[10], (N_B_LAYERS, D, D), D),
        'c_w_in': nrm(ks[11], (N_C_LAYERS, D, 3 * D), D),
        'c_short_w': nrm(ks[12], (N_C_LAYERS, CONV_W, 3 * D), CONV_W),
        'c_short_b': small(ks[13], (N_C_LAYERS, 3 * D)),
        'c_f_w1': nrm(ks[14], (N_C_LAYERS, HYENA_EMB, HYENA_FILTER_HIDDEN), HYENA_EMB),
        'c_f_b1': small(ks[15], (N_C_LAYERS, HYENA_FILTER_HIDDEN)),
        'c_f_w2': nrm(ks[16], (N_C_LAYERS, HYENA_FILTER_HIDDEN, HYENA_FILTER_HIDDEN), HYENA_FILTER_HIDDEN),
        'c_f_b2': small(ks[17], (N_C_LAYERS, HYENA_FILTER_HIDDEN)),
        'c_f_w3': nrm(ks[18], (N_C_LAYERS, HYENA_FILTER_HIDDEN, HYENA_ORDER * 2 * D), HYENA_FILTER_HIDDEN),
        'c_f_freq': gain(ks[19], (N_C_LAYERS, HYENA_FILTER_HIDDEN)),
        'c_f_skip': small(ks[20], (N_C_LAYERS, HYENA_ORDER, D), 0.5),
        'c_w_out': nrm(ks[21], (N_C_LAYERS, D, D), D),
        'f_w13': nrm(ks[22], (DEPTH_2, D, 2 * FFN_HIDDEN), D),
        'f_w2': nrm(ks[23], (DEPTH_2, FFN_HIDDEN, D), FFN_HIDDEN),
    }

def second_block(x, norm_mix_g, norm_ffn_g, a_w_in, a_conv_w, a_w_out,
              b_w_qkv, b_q_norm_g, b_k_norm_g, b_rpb, b_w_out,
              c_w_in, c_short_w, c_short_b, c_f_w1, c_f_b1, c_f_w2, c_f_b2,
              c_f_w3, c_f_freq, c_f_skip, c_w_out, f_w13, f_w2):
    ia = ib = ic = 0
    for i in range(DEPTH_2):
        h = rmsnorm(x, norm_mix_g[i])
        kind = i % N_MIXERS
        if kind == 0:
            y = short_conv_mixer(h, a_w_in[ia], a_conv_w[ia], a_w_out[ia])
            ia += 1
        elif kind == 1:
            y = neighborhood_attention(h, b_w_qkv[ib], b_q_norm_g[ib], b_k_norm_g[ib], b_rpb[ib], b_w_out[ib])
            ib += 1
        else:
            y = hyena_mixer(h, c_w_in[ic], c_short_w[ic], c_short_b[ic], c_f_w1[ic], c_f_b1[ic],
                            c_f_w2[ic], c_f_b2[ic], c_f_w3[ic], c_f_freq[ic], c_f_skip[ic], c_w_out[ic])
            ic += 1
        x = x + y
        x = x + swiglu(rmsnorm(x, norm_ffn_g[i]), f_w13[i], f_w2[i])
    return x


def setup_inputs(seed=0):
    out = dict(first_inputs(seed))
    for name, value in second_inputs(seed + 1).items():
        if name != "x":
            out[name + "_2"] = value
    return out


def reference(
    x, p, positions, attn_norm_w, w_in, conv_w, conv_b, dt_bias, a_log, d_skip, ssd_norm_w,
    w_ssd_out, w_attn_out, w_out, moe_norm_w, w_router_group, b_router_group, w_router_expert,
    b_router_expert, w_exp_gate, w_exp_up, w_exp_down, ple_norm_w, w_ple, w_ple_gate,
    final_norm_w, norm_mix_g_2, norm_ffn_g_2, a_w_in_2, a_conv_w_2, a_w_out_2, b_w_qkv_2,
    b_q_norm_g_2, b_k_norm_g_2, b_rpb_2, b_w_out_2, c_w_in_2, c_short_w_2, c_short_b_2,
    c_f_w1_2, c_f_b1_2, c_f_w2_2, c_f_b2_2, c_f_w3_2, c_f_freq_2, c_f_skip_2, c_w_out_2,
    f_w13_2, f_w2_2,
):
    x = first_block(
        x, p, positions, attn_norm_w, w_in, conv_w, conv_b, dt_bias, a_log, d_skip, ssd_norm_w,
        w_ssd_out, w_attn_out, w_out, moe_norm_w, w_router_group, b_router_group,
        w_router_expert, b_router_expert, w_exp_gate, w_exp_up, w_exp_down, ple_norm_w, w_ple,
        w_ple_gate, final_norm_w,
    )
    return second_block(
        x, norm_mix_g_2, norm_ffn_g_2, a_w_in_2, a_conv_w_2, a_w_out_2, b_w_qkv_2, b_q_norm_g_2,
        b_k_norm_g_2, b_rpb_2, b_w_out_2, c_w_in_2, c_short_w_2, c_short_b_2, c_f_w1_2,
        c_f_b1_2, c_f_w2_2, c_f_b2_2, c_f_w3_2, c_f_freq_2, c_f_skip_2, c_w_out_2, f_w13_2,
        f_w2_2,
    )


_drawn_inputs = setup_inputs


def setup_inputs(seed=0):
    import zlib

    import numpy as np

    out = dict(_drawn_inputs(seed))
    spreads = {}
    factors = {'b_router_group': 8.0,
     'ple_norm_w': 3.024,
     'b_q_norm_g_2': 8.0,
     'b_k_norm_g_2': 8.0,
     'b_rpb_2': 34.069,
     'c_short_b_2': 6.837,
     'c_f_b1_2': 8.0,
     'c_f_b2_2': 8.0,
     'c_f_freq_2': 8.0}
    for name, (base, spread) in spreads.items():
        noise = np.random.default_rng([zlib.crc32(name.encode()), seed]).standard_normal(out[name].shape)
        drawn = base * np.exp(spread * noise) if base else spread * noise
        out[name] = __import__('jax').numpy.asarray(drawn.astype(out[name].dtype))
    for name, factor in factors.items():
        out[name] = (out[name] * factor).astype(out[name].dtype)
    return out
```

```python
import math
from contextlib import ExitStack

import numpy as np
import concourse.bass as bass
from concourse import mybir

P = 128
SEQ, D = 256, 1024
TT = SEQ // P
KT = D // P
COLS = 256
RING = 3
POOL_SLOT = 0
CHUNK = KT * COLS
HEADS, HD = 16, 64
PAIRS = HEADS // 2
SSD_GROUPS, SSD_STATE, SSD_TAPS = 2, 64, 4
SSD_INNER = HEADS * HD
SSD_CHANNELS = SSD_INNER + 2 * SSD_GROUPS * SSD_STATE
XBC_TILES = SSD_CHANNELS // P
DT_COL = SSD_INNER + SSD_CHANNELS
MIXER_DMAS = 11
N_GROUPS, GROUP_EXPERTS = 4, 8
EXPERTS = N_GROUPS * GROUP_EXPERTS
D_EXPERT = 256
FFN = ((8 * D + 3 * 256 - 1) // (3 * 256)) * 256
LAYERS = 4
HALF = 512
GRID_W, NA_ROWS, NA_COLS = 64, 8, 16
ORDER, BANDS, EMB, HIDDEN = 2, 16, 33, 64
EPS = 1e-6
NEG = -1e30
TRI = P + SEQ

MLP_CHUNKS = 3 * (FFN // COLS)
STREAM = [("in_zx", 9), ("in_qk", 8), ("in_v", 4), ("in_g", 8), ("ssd_out", 4), ("attn_out", 4), ("mix_out", 4), ("experts", 3 * EXPERTS),
          ("ple", 1), ("ple_gate", 4),
          ("a_in0", 12), ("a_out0", 4), ("ffn0", MLP_CHUNKS),
          ("b_qk", 8), ("b_v", 4), ("na_out", 4), ("ffn1", MLP_CHUNKS),
          ("hy_in", 12), ("hy_out", 4), ("ffn2", MLP_CHUNKS),
          ("a_in1", 12), ("a_out1", 4), ("ffn3", MLP_CHUNKS)]
FIRST = {}
_c = 0
for _name, _n in STREAM:
    FIRST[_name] = (_c, _n)
    _c += _n
TOTAL = _c
BANKED = [n for n, _ in STREAM if n not in ("experts", "ple") and not n.startswith("ffn")]
DRAINED = {}
_c = 0
for _name in BANKED:
    DRAINED[_name] = _c
    _c += dict(STREAM)[_name]
LATE_DMAS, ROUTER_DMAS, HYENA_DMAS = 9, 5, 10
X_STATES = ["input", "mix_out", "experts", "ple", "final", "a_out0", "ffn0", "na_out", "ffn1", "hy_out",
            "ffn2", "a_out1", "ffn3"]
OPERANDS = ["attn", "ssd", "attention", "merged", "moe", "ple", "mix0", "conv0", "ffn0", "mix1", "na",
            "ffn1", "mix2", "hyena", "ffn2", "mix3", "conv1", "ffn3"]
NORMS = [("attn", "input", "attn_norm_w", 0), ("moe", "mix_out", "moe_norm_w", 0),
         ("ple", "experts", "ple_norm_w", 0)]
for _i, _a, _b in ((0, "final", "a_out0"), (1, "ffn0", "na_out"), (2, "ffn1", "hy_out"), (3, "ffn2", "a_out1")):
    NORMS += [(f"mix{_i}", _a, "norm_mix_g_2", 8 * _i), (f"ffn{_i}", _b, "norm_ffn_g_2", 8 * _i)]
NORM_OF = {_o: _k for _k, (_o, *_r) in enumerate(NORMS)}
SQUARED = [_o for _o, *_r in NORMS]
SQUARED.insert(3, "final")
ROUNDS = {"experts": 0}
for _i in range(LAYERS):
    ROUNDS[f"ffn{_i}"] = EXPERTS + _i * (FFN // COLS)

PARAMS = [("attn_norm_w", 8), ("moe_norm_w", 8), ("ple_norm_w", 8), ("ssd_norm_w", 8),
          ("conv_w", 40), ("conv_b", 10), ("norm_mix_g_2", 32), ("norm_ffn_g_2", 32),
          ("a_conv_w_2", 48), ("c_short_w_2", 72), ("c_short_b_2", 24), ("c_f_skip_2", 16)]
ROW = {}
_c = 0
for _name, _n in PARAMS:
    ROW[_name] = _c
    _c += _n
PARAM_ROWS = _c
PARAM_TILES = -(-PARAM_ROWS // P)


TWO_PI_1 = 6.28125
TWO_PI_2 = float(np.float32(np.round((2 * math.pi - TWO_PI_1) * 2 ** 20) / 2 ** 20))
TWO_PI_3 = float(np.float32(2 * math.pi - TWO_PI_1 - TWO_PI_2))
ROUND = 1.5 * 2 ** 23


def constants():
    f32 = np.float32
    c = {}
    c["ident"] = np.eye(P, dtype=f32)
    tri = np.zeros((P, TT, SEQ), f32)
    for t in range(TT):
        tri[:, t] = (np.arange(P)[:, None] + P * t) <= np.arange(SEQ)[None]
    c["tri"] = tri.reshape(P, TT * SEQ)
    q = np.arange(P)[:, None]
    c["causal"] = np.concatenate([np.where(np.arange(P)[None] <= q, 0, NEG),
                                  np.where(np.arange(SEQ)[None] <= q + P, 0, NEG)], 1).astype(f32)
    half = HD // 2
    rot = np.zeros((P, P), f32)
    for m in range(P):
        if m % HD < half:
            rot[m + half, m] = -1
        else:
            rot[m - half, m] = 1
    c["rot"] = rot
    inv = f32(10000.0) ** (-np.arange(half, dtype=f32) / f32(half))
    c["inv_freq"] = np.tile(inv, P // half).reshape(P, 1).astype(f32)
    c["diag16"] = np.eye(HEADS, dtype=f32)
    c["iota8"] = np.tile(np.arange(8, dtype=f32), (P, 1))
    c["headones"] = np.kron(np.eye(2, dtype=f32), np.ones((HD, HD), f32))
    c["flip"] = np.kron(np.eye(2, dtype=f32), np.eye(GRID_W, dtype=f32)[::-1])
    col = np.arange(SEQ) % GRID_W
    start = np.clip(col - NA_COLS // 2, 0, GRID_W - NA_COLS)
    ok = (col[None] >= start[:, None]) & (col[None] < start[:, None] + NA_COLS)
    c["na_mask"] = np.where(ok, 0, NEG).astype(f32).reshape(TT, P, SEQ).transpose(1, 0, 2).reshape(P, -1)
    t = np.linspace(0.0, 1.0, SEQ, dtype=f32)[:, None]
    bands = np.linspace(1e-4, BANDS - 1, BANDS, dtype=f32)
    ang = (f32(2.0 * math.pi) * np.arange(SEQ, dtype=f32)[:, None] / f32(SEQ) * bands).astype(f32)
    z = np.concatenate([t, np.cos(ang), -np.sin(ang)], -1).astype(f32)
    c["embed"] = np.ascontiguousarray(z.T)
    lt = math.log(1e-2)
    deltas = np.abs(np.linspace(lt / 1.5, lt / 0.3, D, dtype=f32))
    c["decay"] = np.exp(-t * deltas).astype(f32)
    n = 2 * SEQ
    tt = np.arange(SEQ)[:, None]
    f = np.arange(SEQ)[None]
    cos, sin = np.cos(2 * np.pi * tt * f / n), -np.sin(2 * np.pi * tt * f / n)
    nyq = np.cos(np.pi * np.arange(SEQ))
    sinn = sin.copy()
    sinn[:, 0] = nyq
    cosn = cos.copy()
    cosn[:, 0] = nyq
    c["dft"] = np.concatenate([cos, sinn, sin, cosn[:, :P]], 1).astype(f32)
    w = np.full(SEQ, 2.0)
    w[0] = 1.0
    icos = (w[:, None] * np.cos(2 * np.pi * f.T * tt.T / n)) / n
    isin = (-w[:, None] * np.sin(2 * np.pi * f.T * tt.T / n)) / n
    isin[0] = nyq / n
    c["idft"] = np.concatenate([icos, isin], 0).astype(f32)
    return c


class Chunk:

    def __init__(self, number, group=0):
        self.c = group * RING + number
        self.slot = number % RING
        self.turn = group + number // RING
        self.first = number < RING and isinstance(group, int)
        self.more = not (isinstance(group, int) and number + RING * group + RING >= TOTAL)

    def ahead(self):
        new = Chunk.__new__(Chunk)
        new.c, new.slot, new.turn, new.first, new.more = self.c + RING, self.slot, self.turn + 1, False, True
        return new


def chunks(eng, name):
    c0, n = FIRST[name]
    j = 0
    if c0 == 0:
        for j in range(RING):
            yield j, Chunk(j)
        j = RING
    groups = min(n - j, TOTAL - RING - c0 - j) // RING
    if groups > 1:
        with eng.Fori(0, groups) as g:
            for r in range(RING):
                yield g * RING + (j + r), Chunk(c0 + j + r, g)
        j += groups * RING
    for r in range(j, n):
        yield r, Chunk(c0 + r)


def mlp_rounds(eng, name):
    c0, n = FIRST[name]
    rounds = n // 3 - 1
    peel = 1 if c0 + n == TOTAL else 0
    with eng.Fori(0, rounds - peel) as g:
        yield g, c0 + 2, g
    for i in range(rounds - peel, rounds):
        yield i, c0 + 2 + 3 * i, 0


class Chain:

    def __init__(self, eng, sem):
        self.eng, self.sem, self.count, self.extra = eng, sem, 0, 0

    def link(self, ins):
        self.count += 1
        ins.then_inc(self.sem, 1)
        self.eng.wait_ge(self.sem, self.extra + self.count)

    def begin(self, i, per_round):
        self.start, self.per_round = self.count, per_round
        self.extra = i * per_round

    def end(self, rounds):
        assert self.count - self.start == self.per_round, (self.count - self.start, self.per_round)
        self.count = self.start + rounds * self.per_round
        self.extra = 0


def flat(ap, n):
    dims = " ".join(f"d{i}" for i in range(len(ap.shape)))
    return ap.rearrange(f"{dims} -> ({dims})").rearrange("(r n) -> r n", n=n)


def build(nc, A, out):
    f32, f32r, i32, u32 = mybir.dt.float32, mybir.dt.float32r, mybir.dt.int32, mybir.dt.uint32
    ALU, ACT, AX = mybir.AluOpType, mybir.ActivationFunctionType, mybir.AxisListType
    SUB, ADD, MUL = ALU.subtract, ALU.add, ALU.mult
    ds = bass.ds
    ctx = ExitStack()
    with ctx:
        def sb(name, shape, dt=f32):
            return ctx.enter_context(nc.sbuf_tensor(name, shape, dt))

        def sem(name):
            return ctx.enter_context(nc.semaphore(name))

        raw = [sb(f"raw{i}", [P, CHUNK]) for i in range(RING)]
        w_hi = [sb(f"w_hi{i}", [P, CHUNK], f32r) for i in range(RING)]
        w_lo = [sb(f"w_lo{i}", [P, CHUNK], f32r) for i in range(RING)]
        x = sb("x_res", [P, TT, D])
        h_hi = sb("h_hi", [P, KT, SEQ], f32r)
        h_lo = sb("h_lo", [P, KT, SEQ], f32r)
        ident = sb("ident_sb", [P, P])
        ones = sb("ones", [P, P])
        params = sb("params", [P, PARAM_TILES * P])
        ssq = sb("ssq", [P, TT])
        ms = sb("ms", [P, TT])
        inv = sb("inv", [P, TT])
        neg_half = sb("neg_half", [P, TT])
        eps_col = sb("eps_col", [P, 1])

        work0 = -(-nc.sbuf_base // 32) * 32
        limit = nc.sbuf_usable_end - work0

        def at(name, shape, offset, dt=f32):
            size = int(np.prod(shape[1:])) * 4
            assert offset + size <= limit, (name, offset + size, limit)
            return nc.alloc_sbuf_tensor_at(name, shape, dt, offset=work0 + offset)

        KB = 1024
        x_scaled = at("x_scaled", [P, TT, D], 0)
        param_rows = at("param_rows", [P, PARAM_TILES, P], 8 * KB)
        Z0, XBC0, Q0, GS0, GA0 = 0, 8, 18, 34, 42
        pj = at("pj", [P, 50, SEQ], 0)
        v_t = at("v_t", [P, TT, D], 50 * KB)
        conv = at("conv", [P, 10, SEQ], 58 * KB)
        xs_t = at("xs_t", [P, TT, D], 8 * KB)
        cb = at("cb", [P, SSD_GROUPS, TRI], 68 * KB)
        cum_diag = at("cum_diag", [HEADS, HEADS, SEQ], 71 * KB)
        decay = at("decay_w", [P, 2, TRI], 87 * KB)
        xdt = at("xdt", [P, TT, 2 * HD], 90 * KB)
        tri = at("tri_sb", [P, TT, SEQ], 91 * KB)
        S1 = 93 * KB
        diag16 = at("diag16_sb", [HEADS, HEADS], S1)
        dt_bias = at("dt_bias_sb", [P, HEADS], S1 + 64)
        a_rate = at("a_rate", [P, HEADS], S1 + 128)
        w_dt = at("w_dt", [P, KT, HEADS], S1 + 192)
        dt_x = at("dt_x", [P, TT, HEADS], S1 + 704)
        dt_n = at("dt_n", [P, TT, HEADS], S1 + 832)
        dt_u = at("dt_u", [P, TT, HEADS], S1 + 960)
        dt_w = at("dt_w", [P, TT, HEADS], S1 + 1088)
        dt_l = at("dt_l", [P, TT, HEADS], S1 + 1216)
        dt_r = at("dt_r", [P, TT, HEADS], S1 + 1344)
        dt_t = at("dt_t", [P, TT, HEADS], S1 + 1472)
        dA = at("dA", [P, TT, HEADS], S1 + 1600)
        cum_t = at("cum_t", [P, TT, HEADS], S1 + 1728)
        d_col = at("d_col", [P, PAIRS], S1 + 1856)
        inv_freq = at("inv_freq_sb", [P, 1], S1 + 1888)
        a_log_b = at("a_log_b", [P, HEADS], S1 + 1952)
        cum_f = at("cum_f", [HEADS, SEQ], 95 * KB + 256)
        rot = at("rot_sb", [P, P], 96 * KB + 512)
        causal = at("causal_sb", [P, TRI], 97 * KB)
        cos_f = at("cos_f", [P, SEQ], 98 * KB + 512)
        sin_f = at("sin_f", [P, SEQ], 99 * KB + 512)
        ang = at("ang", [P, SEQ], 100 * KB + 512)
        ang_k = at("ang_k", [P, SEQ], 101 * KB + 512)
        pos_i = at("pos_i", [P, SEQ], 102 * KB + 512, i32)
        y_sum = at("y_sum", [P, SEQ], 103 * KB + 512)
        sq_buf = at("sq_buf", [P, 4, SEQ], 71 * KB)
        ynorm = at("ynorm", [P, 4, SEQ], 75 * KB)
        rstd = at("rstd", [P, SEQ], 79 * KB)
        rope_t = at("rope_t", [P, 2, SEQ], 58 * KB)
        rope_u = at("rope_u", [P, 2, SEQ], 60 * KB)
        qk_st = at("qk_st", [P, 2, SEQ], 62 * KB)
        v_st = at("v_st", [P, TT, 2 * HD], 64 * KB)
        probs = at("probs", [P, 2, TT * SEQ], 65 * KB)
        probs_t = at("probs_t", [P, 2, TT * SEQ], 69 * KB)
        at_max = at("at_max", [P, 2, TT], 73 * KB)
        at_sum = at("at_sum", [P, 2, TT], 73 * KB + 32)
        at_inv = at("at_inv", [P, 2, TT], 73 * KB + 64)
        merge_t = at("merge_t", [P, 2, SEQ], 74 * KB)
        na_mask = at("na_mask_sb", [P, TT * SEQ], 76 * KB)
        na_bias = [at(f"na_bias{b}", [P, 2, TT * SEQ], (78 + 4 * b) * KB) for b in range(2)]
        headones = at("headones_sb", [P, P], 86 * KB)
        qk_gain = at("qk_gain", [P, 2], 86 * KB + 512)
        flip = at("flip_sb", [P, P], 91 * KB)
        na_sq = at("na_sq", [P, 2, SEQ], 87 * KB)
        na_rs = at("na_rs", [P, 2, SEQ], 89 * KB)
        comb = at("comb", [P, EXPERTS, SEQ], 8 * KB)
        silu_g = at("silu_g", [P, 2 * SEQ], 40 * KB)
        hid = at("hid", [P, 2, SEQ], 42 * KB)
        hid_hi = at("hid_hi", [P, 2, SEQ], 44 * KB, f32r)
        hid_lo = at("hid_lo", [P, 2, SEQ], 46 * KB, f32r)
        R0 = 48 * KB
        NL = N_GROUPS + EXPERTS
        w_route = at("w_route", [P, KT, NL], 105 * KB)
        b_route = at("b_route", [P, NL], 106 * KB + 128)
        logits = at("logits", [P, TT, NL], R0 + 1344)
        g_pad = at("g_pad", [P, TT, 8], R0 + 1664)
        g_top = at("g_top", [P, TT, 8], R0 + 1728)
        g_idx = at("g_idx", [P, TT, 8], R0 + 1792, u32)
        g_idxf = at("g_idxf", [P, TT], R0 + 1856)
        g_hot = at("g_hot", [P, TT, N_GROUPS], R0 + 1920)
        g_neg = at("g_neg", [P, TT], R0 + 1952)
        g_exp = at("g_exp", [P, TT, N_GROUPS], R0 + 1984)
        g_sum = at("g_sum", [P, TT], R0 + 2016)
        g_w = at("g_w", [P, TT], R0 + 2048)
        e_prod = at("e_prod", [P, TT, EXPERTS], R0 + 2080)
        e_sel = at("e_sel", [P, TT, GROUP_EXPERTS], R0 + 2336)
        e_top = at("e_top", [P, TT, 8], R0 + 2400)
        e_idx = at("e_idx", [P, TT, 8], R0 + 2464, u32)
        e_idxf = at("e_idxf", [P, TT, 2], R0 + 2528)
        e_hot = at("e_hot", [P, TT, 2, 8], R0 + 2592)
        e_gap = at("e_gap", [P, TT], R0 + 2720)
        e_exp = at("e_exp", [P, TT], R0 + 2752)
        e_den = at("e_den", [P, TT], R0 + 2784)
        e_w = at("e_w", [P, TT, 2], R0 + 2816)
        e_wt = at("e_wt", [P, TT, 8], R0 + 2880)
        comb_t = at("comb_t", [P, TT, N_GROUPS, GROUP_EXPERTS], R0 + 3008)
        comb_f = at("comb_f", [EXPERTS, SEQ], R0 + 3264)
        iota8 = at("iota8_sb", [P, 8], 106 * KB + 288)
        p_t = at("p_t", [P, TT, SEQ], R0 + 5 * KB)
        gate_s = at("gate_s", [P, TT, COLS], R0 + 7 * KB)
        gate_m = at("gate_m", [P, TT, COLS], R0 + 9 * KB)
        final_w = at("final_w", [P, D], R0 + 11 * KB)
        cu = at("cu", [P, KT, SEQ], 24 * KB)
        acv = at("acv", [P, KT, SEQ], 32 * KB)
        hc = at("hc", [P, 3 * KT, SEQ], 24 * KB)
        f_w3 = at("f_w3", [HIDDEN, ORDER * 2 * D], 48 * KB)
        dft = at("dft_sb", [P, TT, 3 * SEQ + P], 64 * KB)
        idft = at("idft_sb", [P, 2 * TT, SEQ], 71 * KB)
        f_decay = at("f_decay", [P, TT, D], 75 * KB)
        embed = at("embed_sb", [EMB, SEQ], 83 * KB)
        f_hid = at("f_hid", [HIDDEN, SEQ], 84 * KB)
        f_k = at("f_k", [HIDDEN, SEQ], 85 * KB)
        f_w1 = at("f_w1", [EMB, HIDDEN], 86 * KB)
        f_w2 = at("f_w2", [HIDDEN, HIDDEN], 86 * KB + 256)
        f_b1 = at("f_b1", [HIDDEN, 1], 86 * KB + 512)
        f_b2 = at("f_b2", [HIDDEN, 1], 86 * KB + 544)
        f_freq = at("f_freq", [HIDDEN, 1], 86 * KB + 576)
        f_rev = at("f_rev", [P, TT, HALF], 0)
        f_even = at("f_even", [P, TT, HALF], 4 * KB)
        f_odd = at("f_odd", [P, TT, HALF], 8 * KB)
        hs_re = at("hs_re", [P, TT, HALF], 12 * KB)
        hs_im = at("hs_im", [P, TT, HALF], 16 * KB)
        u_t = at("u_t", [P, TT, HALF], 20 * KB)
        hs_re2 = at("hs_re2", [P, HALF], 88 * KB)
        f_inv = at("f_inv", [P, HALF], 90 * KB)
        u_st = at("u_st", [P, KT // 2, SEQ], 92 * KB)
        ys = at("ys", [P, 2 * TT, HALF], 96 * KB)
        ys_t = at("ys_t", [P, TT, HALF], 104 * KB)
        f_abs = at("f_abs", [P, 2, TT, HALF], 96 * KB)

        proj = ctx.enter_context(nc.psum_tensor("proj", [P, RING, HALF], f32))
        acc = ctx.enter_context(nc.psum_tensor("acc", [P, TT * 2, HALF], f32))
        misc = ctx.enter_context(nc.psum_tensor("misc", [P, HALF], f32))

        def pair(b):
            return proj[:, b, :].rearrange("p (a n) -> p a n", a=2)

        raw_loaded = [sem(f"raw_loaded{i}") for i in range(RING)]
        hi_ready = sem("hi_ready")
        lo_pool, lo_dve = sem("lo_pool"), sem("lo_dve")
        chunk_used = sem("chunk_used")
        drained = sem("drained")
        x_loaded, x_ready = sem("x_loaded"), sem("x_ready")
        ssq_ready, inv_ready, scaled_ready = sem("ssq_ready"), sem("inv_ready"), sem("scaled_ready")
        turned, turned_read, fhi_ready, h_ready = sem("turned"), sem("turned_read"), sem("fhi_ready"), sem("h_ready")
        small = sem("small")
        ident_loaded, params_loaded = sem("ident_loaded"), sem("params_loaded")
        rows_cleared, params_turned, params_ready = sem("rows_cleared"), sem("params_turned"), sem("params_ready")
        act_chain, dve_chain, pool_chain = sem("act_chain"), sem("dve_chain"), sem("pool_chain")
        silu_ready, banks_read, hid_ready = sem("silu_ready"), sem("banks_read"), sem("hid_ready")
        out_stored = sem("out_stored")
        mixer_tables = sem("mixer_tables")
        z_ready, taps_done, conv_first, conv_done, conv_ready = (
            sem("z_ready"), sem("taps_done"), sem("conv_first"), sem("conv_done"), sem("conv_ready"))
        gates_ready, dt_summed, dt_step, dt_exped = sem("gates_ready"), sem("dt_summed"), sem("dt_step"), sem("dt_exped")
        angles, sines, rates, dA_ready, cum_summed, cum_ready = (
            sem("angles"), sem("sines"), sem("rates"), sem("dA_ready"), sem("cum_summed"), sem("cum_ready"))
        xs_turned, xs_read, cb_summed, cb_ready = sem("xs_turned"), sem("xs_read"), sem("cb_summed"), sem("cb_ready")
        cum_spread, gaps_ready, decay_ready, scores_ready = (
            sem("cum_spread"), sem("gaps_ready"), sem("decay_ready"), sem("scores_ready"))
        y_ready, y_read, y_squared, y_ssq, y_root, y_normed = (
            sem("y_ready"), sem("y_read"), sem("y_squared"), sem("y_ssq"), sem("y_root"), sem("y_normed"))
        rotated, roped, qk_scored, masked, max_ready, exped, normed = (
            sem("rotated"), sem("roped"), sem("qk_scored"), sem("masked"), sem("max_ready"), sem("exped"), sem("normed"))
        v_staged, p_turned, pt_act, pt_dve, o_ready, o_hi, o_read = (
            sem("v_staged"), sem("p_turned"), sem("pt_act"), sem("pt_dve"), sem("o_ready"), sem("o_hi"), sem("o_read"))

        router_tables, late_tables = sem("router_tables"), sem("late_tables")
        routed, comb_made, comb_turned, comb_f_ready, comb_spread, comb_act, comb_dve = (
            sem("routed"), sem("comb_made"), sem("comb_turned"), sem("comb_f_ready"), sem("comb_spread"),
            sem("comb_act"), sem("comb_dve"))
        p_low = sem("p_low")
        gaps_e, exp_e = sem("gaps_e"), sem("exp_e")
        p_turned_ple, p_split, gate_sig = sem("p_turned_ple"), sem("p_split"), sem("gate_sig")
        cu_ready, a_first, a_taps = sem("cu_ready"), sem("a_first"), sem("a_taps")
        qk_squared, qk_summed, qk_root, qk_normed = sem("qk_squared"), sem("qk_summed"), sem("qk_root"), sem("qk_normed")
        bias_loaded = [sem(f"bias_loaded{b}") for b in range(2)]
        q_staged = sem("q_staged")
        xdt_ready, y_gated = sem("xdt_ready"), sem("y_gated")
        hyena_tables = sem("hyena_tables")
        f_summed, f_angle, f_sine = sem("f_summed"), sem("f_angle"), sem("f_sine")
        hc_first, hc_taps = sem("hc_first"), sem("hc_taps")
        filt_summed, rev_copied, parity_ready, abs_ready, mag_ready, norm_summed, h_summed, h_scaled = (
            sem("filt_summed"), sem("rev_copied"), sem("parity_ready"), sem("abs_ready"), sem("mag_ready"),
            sem("norm_summed"), sem("h_summed"), sem("h_scaled"))
        u_staged, u_turned, ut_ready, u_summed, ys_ready, y_summed, z_made = (
            sem("u_staged"), sem("u_turned"), sem("ut_ready"), sem("u_summed"), sem("ys_ready"), sem("y_summed"), sem("z_made"))

        block = ctx.enter_context(nc.Block())

        SCORE_COLS = {True: ((0, P), (P, SEQ)), False: ((0, SEQ), (SEQ, SEQ))}

        @block.sync
        def _(sp):
            def load(s, src, k):
                if not s.first:
                    if s.slot == POOL_SLOT:
                        sp.wait_ge(lo_pool, s.turn)
                    else:
                        sp.wait_ge(lo_dve, s.turn * (RING - 1) + (s.slot - (RING - 1)))
                dst = raw[s.slot][:, :].rearrange("p (k n) -> p k n", k=k)
                sp.dma_start(dst, src).then_inc(raw_loaded[s.slot], 16)

            def load_cols(name, w, first_col):
                view = w.rearrange("(k p) n -> p k n", p=P)
                for j, s in chunks(sp, name):
                    load(s, view[:, :, ds(j * COLS + first_col, COLS)], KT)

            def load_late_tables():
                sp.wait_ge(drained, DRAINED["mix_out"] + FIRST["mix_out"][1])
                for dst, src in ((p_t[:, :, :], A["p"][0, 0].rearrange("(t p) n -> p t n", p=P)),
                                 (final_w[:, :], A["final_norm_w"].partition_broadcast(P)),
                                 (na_mask[:, :], A["na_mask"]), (headones[:, :], A["headones"]), (flip[:, :], A["flip"]),
                                 (qk_gain[0:HD, 0:1], flat(A["b_q_norm_g_2"], 1)), (qk_gain[HD:P, 0:1], flat(A["b_q_norm_g_2"], 1)),
                                 (qk_gain[0:HD, 1:2], flat(A["b_k_norm_g_2"], 1)), (qk_gain[HD:P, 1:2], flat(A["b_k_norm_g_2"], 1))):
                    sp.dma_start(dst, src, allow_slow_non_contiguous=True).then_inc(late_tables, 16)

            def load_mlp(name, gate, up, down, between=None):
                c0, n = FIRST[name]
                load(Chunk(c0), gate(0), KT)
                load(Chunk(c0 + 1), up(0), KT)
                if between:
                    between()
                for i, c, g in mlp_rounds(sp, name):
                    load(Chunk(c, g), gate(i + 1), KT)
                    load(Chunk(c + 1, g), up(i + 1), KT)
                    load(Chunk(c + 2, g), down(i), 2)
                load(Chunk(c0 + n - 1), down(n // 3 - 1), 2)

            def load_hyena_tables():
                sp.wait_ge(drained, DRAINED["na_out"] + FIRST["na_out"][1])
                for dst, src in ((f_w3[:, :], A["c_f_w3_2"][0]), (f_w1[:, :], A["c_f_w1_2"][0]), (f_w2[:, :], A["c_f_w2_2"][0]),
                                 (f_b1[:, :], flat(A["c_f_b1_2"], 1)), (f_b2[:, :], flat(A["c_f_b2_2"], 1)),
                                 (f_freq[:, :], flat(A["c_f_freq_2"], 1)), (embed[:, :], A["embed"]),
                                 (dft[:, :, :], A["dft"].rearrange("(t p) n -> p t n", p=P)),
                                 (idft[:, :, :], A["idft"].rearrange("(t p) n -> p t n", p=P)),
                                 (f_decay[:, :, :], A["decay"].rearrange("(t p) n -> p t n", p=P))):
                    sp.dma_start(dst, src, allow_slow_non_contiguous=True).then_inc(hyena_tables, 16)

            def load_ffn(layer, between=None):
                w13 = A["f_w13_2"][layer].rearrange("(k p) n -> p k n", p=P)
                w2 = A["f_w2_2"][layer].rearrange("(k p) n -> p k n", p=P)
                load_mlp(f"ffn{layer}", lambda i: w13[:, :, ds(i * COLS, COLS)],
                         lambda i: w13[:, :, ds(i * COLS + FFN, COLS)],
                         lambda i: w2[:, ds(i * 2, 2), :], between)

            sp.dma_start(x[:, :, :], A["x"][0].rearrange("(t p) n -> p t n", p=P)).then_inc(x_loaded, 16)
            sp.dma_start(ident[:, :], A["ident"]).then_inc(ident_loaded, 16)
            sp.wait_ge(rows_cleared, 1)
            for name, rows in PARAMS:
                src, done = flat(A[name], P), 0
                while done < rows:
                    tile, row = divmod(ROW[name] + done, P)
                    n = min(rows - done, P - row)
                    sp.dma_start(param_rows[row:row + n, tile, :], src[done:done + n, :]).then_inc(params_loaded, 16)
                    done += n
            load_cols("in_zx", A["w_in"][0], 0)
            for dst, src in ((tri[:, :, :], A["tri"].rearrange("p (t n) -> p t n", t=TT)), (diag16[:, :], A["diag16"]),
                             (dt_bias[:, :], A["dt_bias"][0].partition_broadcast(P)),
                             (a_log_b[:, :], A["a_log"][0].partition_broadcast(P)),
                             (w_dt[:, :, :], A["w_in"][0].rearrange("(k p) n -> p k n", p=P)[:, :, DT_COL:DT_COL + HEADS]),
                             (d_col[0:HD, :], A["d_skip"][0].rearrange("(i a) -> a i", a=2)[0].partition_broadcast(HD)),
                             (d_col[HD:P, :], A["d_skip"][0].rearrange("(i a) -> a i", a=2)[1].partition_broadcast(HD)),
                             (inv_freq[:, :], A["inv_freq"]), (rot[:, :], A["rot"]), (causal[:, :], A["causal"]),
                             (pos_i[:, :], A["positions"][0].partition_broadcast(P))):
                sp.dma_start(dst, src, allow_slow_non_contiguous=True).then_inc(mixer_tables, 16)
            for dst, src in ((w_route[:, :, 0:N_GROUPS], A["w_router_group"][0].rearrange("(k p) n -> p k n", p=P)),
                             (w_route[:, :, N_GROUPS:], A["w_router_expert"][0].rearrange("(k p) n -> p k n", p=P)),
                             (b_route[:, 0:N_GROUPS], A["b_router_group"][0].partition_broadcast(P)),
                             (b_route[:, N_GROUPS:], A["b_router_expert"][0].partition_broadcast(P)),
                             (iota8[:, :], A["iota8"])):
                sp.dma_start(dst, src).then_inc(router_tables, 16)
            inner = SSD_INNER + SSD_CHANNELS + HEADS
            load_cols("in_qk", A["w_in"][0], inner)
            load_cols("in_v", A["w_in"][0], inner + 2 * D)
            load_cols("in_g", A["w_in"][0], inner + 3 * D)
            load_cols("ssd_out", A["w_ssd_out"][0], 0)
            load_cols("attn_out", A["w_attn_out"][0], 0)
            load_cols("mix_out", A["w_out"][0], 0)
            by_expert = {n: A[n][0].rearrange("g e (k p) f -> p (g e) k f", p=P)
                         for n in ("w_exp_gate", "w_exp_up", "w_exp_down")}
            load_mlp("experts", *[lambda i, v=v: v[:, ds(i, 1), :, :].rearrange("p e k f -> p (e k) f")
                                  for v in by_expert.values()], between=load_late_tables)
            load(Chunk(FIRST["ple"][0]), A["w_ple"][0].rearrange("(k p) n -> p k n", p=P), 2)
            load_cols("ple_gate", A["w_ple_gate"][0], 0)
            load_cols("a_in0", A["a_w_in_2"][0], 0)
            load_cols("a_out0", A["a_w_out_2"][0], 0)
            load_ffn(0)
            load_cols("b_qk", A["b_w_qkv_2"][0], 0)
            load_cols("b_v", A["b_w_qkv_2"][0], 2 * D)
            load_cols("na_out", A["b_w_out_2"][0], 0)
            rpb = A["b_rpb_2"]
            head, row = (2 * NA_ROWS - 1) * (2 * NA_COLS - 1), 2 * NA_COLS - 1
            with sp.Fori(0, PAIRS // 2) as ii:
                for b in range(2):
                    i = ii * 2 + b
                    sp.wait_ge(qk_scored, i + (PAIRS - 1))
                    for h in range(2):
                        for r in range(SEQ // GRID_W):
                            t, half = divmod(r, 2)
                            src = bass.AP(rpb.tensor, i * (2 * head) + (h * head + (NA_ROWS - 1 - r) * row + NA_COLS - GRID_W),
                                          [[1, GRID_W], [row, SEQ // GRID_W], [1, GRID_W]])
                            dst = na_bias[b][half * GRID_W:(half + 1) * GRID_W, h, t * SEQ:(t + 1) * SEQ]
                            sp.dma_start(dst.rearrange("p (a b) -> p a b", b=GRID_W), src).then_inc(bias_loaded[b], 16)
            load_ffn(1, load_hyena_tables)
            load_cols("hy_in", A["c_w_in_2"][0], 0)
            load_cols("hy_out", A["c_w_out_2"][0], 0)
            load_ffn(2)
            load_cols("a_in1", A["a_w_in_2"][1], 0)
            load_cols("a_out1", A["a_w_out_2"][1], 0)
            load_ffn(3)
            sp.wait_ge(x_ready, len(X_STATES) - 1)
            sp.dma_start(out[0].rearrange("(t p) n -> p t n", p=P), x[:, :, :]).then_inc(out_stored, 16)
            sp.wait_ge(out_stored, 16)

        PARAM_DMAS = sum(len({(ROW[n] + r) // P for r in range(k)}) for n, k in PARAMS)

        @block.tensor
        def _(pe):
            def wait_parts(s):
                if s.slot == POOL_SLOT:
                    pe.wait_ge(lo_pool, s.turn + 1)
                else:
                    pe.wait_ge(lo_dve, s.turn * (RING - 1) + s.slot)

            def product_f(s):
                hi = w_hi[s.slot][:, :].rearrange("p (k n) -> p k n", k=KT)
                lo = w_lo[s.slot][:, :].rearrange("p (k n) -> p k n", k=KT)
                for a in range(2):
                    for k in range(KT):
                        for w, h in ((hi, h_hi), (hi, h_lo), (lo, h_hi)):
                            last = pe.matmul(pair(s.slot)[:, a, :], w[:, k, a * P:(a + 1) * P], h[:, k, :],
                                             start=(k == 0 and w is hi and h is h_hi),
                                             stop=(k == KT - 1 and w is lo))
                last.then_inc(chunk_used, 1)

            def product_t(s):
                hi = w_hi[s.slot][:, :].rearrange("p (k n) -> p k n", k=KT)
                lo = w_lo[s.slot][:, :].rearrange("p (k n) -> p k n", k=KT)
                for t in range(TT):
                    for k in range(KT):
                        for h, w in ((h_hi, hi), (h_hi, lo), (h_lo, hi)):
                            last = pe.matmul(pair(s.slot)[:, t, :], h[:, k, t * P:(t + 1) * P], w[:, k, :],
                                             start=(k == 0 and w is hi and h is h_hi),
                                             stop=(k == KT - 1 and h is h_lo))
                last.then_inc(chunk_used, 1)

            def project(name, product, operand):
                pe.wait_ge(h_ready, OPERANDS.index(operand) + 1)
                for j, s in chunks(pe, name):
                    wait_parts(s)
                    if isinstance(j, int) and DRAINED[name] + j < RING:
                        pass
                    else:
                        pe.wait_ge(drained, j + (DRAINED[name] - RING + 1))
                    product(s)

            def norm_turn(operand):
                n = NORM_OF[operand]
                pe.wait_ge(scaled_ready, TT * (SQUARED.index(operand) + 1))
                for kk in range(KT // 2):
                    if kk >= RING:
                        pe.wait_ge(turned_read, n * (KT // 2) + kk - RING + 1)
                    for a in range(2):
                        for t in range(TT):
                            k = 2 * kk + a
                            last = pe.transpose(pair(kk % RING)[:, a, t * P:(t + 1) * P],
                                                x_scaled[:, t, k * P:(k + 1) * P], ident[:, :])
                    last.then_inc(turned, 1)

            def ssd():
                pe.wait_ge(dA_ready, 1)
                for t in range(TT):
                    for s in range(t + 1):
                        pe.matmul(misc[:, 64 + t * HEADS:64 + (t + 1) * HEADS], tri[:, s, t * P:(t + 1) * P],
                                  dA[:, s, :], start=(s == 0), stop=(s == t))
                for s in range(TT):
                    last = pe.matmul(misc[0:HEADS, SEQ:2 * SEQ], dA[:, s, :], tri[:, s, :],
                                     start=(s == 0), stop=(s == TT - 1))
                last.then_inc(cum_summed, 1)
                pe.wait_ge(conv_ready, 1)
                for kk in range(KT // 2):
                    if kk >= RING:
                        pe.wait_ge(xs_read, kk - RING + 1)
                    for t in range(TT):
                        for a in range(2):
                            last = pe.transpose(pair(kk % RING)[:, t, a * P:(a + 1) * P],
                                                conv[:, 2 * kk + a, t * P:(t + 1) * P], ident[:, :])
                    last.then_inc(xs_turned, 1)
                for g in range(SSD_GROUPS):
                    r = slice(g * SSD_STATE, (g + 1) * SSD_STATE)
                    pe.matmul(acc[:, g, 0:SEQ], conv[r, 8, 0:P], conv[r, 9, :], start=True, stop=True)
                    last = pe.matmul(acc[:, g, SEQ:TRI], conv[r, 8, P:SEQ], conv[r, 9, P:SEQ], start=True, stop=True)
                last.then_inc(cb_summed, 1)
                pe.wait_ge(cum_ready, 1)
                for g in range(SSD_GROUPS):
                    with pe.Fori(0, PAIRS // SSD_GROUPS) as ii:
                        i = ii + g * (PAIRS // SSD_GROUPS)
                        pe.wait_ge(gaps_ready, i)
                        for h in range(2):
                            last = pe.matmul(acc[:, 2, h * SEQ:(h + 1) * SEQ], ones[0:HEADS, :],
                                             cum_diag[:, 2 * i + h, :], start=True, stop=True)
                        last.then_inc(cum_spread, 1)
                        pe.wait_ge(scores_ready, i + 1)
                        pe.wait_ge(y_read, i)
                        for h in range(2):
                            o = acc[h * HD:(h + 1) * HD, 3, :]
                            pe.matmul(o[:, 0:SEQ], xdt[:, 0, h * HD:(h + 1) * HD], decay[:, h, 0:SEQ],
                                      start=True, stop=False)
                            last = pe.matmul(o[:, P:SEQ], xdt[:, 1, h * HD:(h + 1) * HD], decay[:, h, SEQ:TRI],
                                             start=False, stop=True)
                        last.then_inc(y_ready, 1)
                for g in range(SSD_GROUPS):
                    pe.wait_ge(y_squared, g + 1)
                    for a in range(4):
                        last = pe.matmul(acc[:, g, 0:SEQ], ones[:, :], sq_buf[:, a, :], start=(a == 0), stop=(a == 3))
                    last.then_inc(y_ssq, 1)

            def attention():
                with pe.Fori(0, PAIRS) as i:
                    pe.wait_ge(roped, i)
                    for a in range(2):
                        last = pe.matmul(acc[:, 0, a * SEQ:(a + 1) * SEQ], rot[:, :], pj[:, i + (Q0 + a * KT), :],
                                         start=True, stop=True)
                    last.then_inc(rotated, 1)
                    pe.wait_ge(roped, i + 1)
                    pe.wait_ge(masked, i)
                    for h in range(2):
                        r = slice(h * HD, (h + 1) * HD)
                        for t, (c, n) in enumerate(SCORE_COLS[True]):
                            last = pe.matmul(acc[:, 1 + h, c:c + n], qk_st[r, 0, t * P:(t + 1) * P],
                                             qk_st[r, 1, 0:n], start=True, stop=True)
                    last.then_inc(qk_scored, 1)
                    attention_out(i, 0, True)

            def attention_out(i, base, causal_):
                pe.wait_ge(normed, i + (base + 1))
                pe.wait_ge(pt_act, i + base)
                pe.wait_ge(pt_dve, i + base)
                for h, bank in ((0, acc[:, 3, :]), (1, misc[:, :])):
                    for t, (c, n) in enumerate(SCORE_COLS[causal_]):
                        for kt in range(n // P):
                            to = t * P if kt == 0 else SEQ + (t * P if not causal_ else 0)
                            last = pe.transpose(bank[:, to:to + P], probs[:, h, c + kt * P:c + (kt + 1) * P],
                                                ident[:, :])
                last.then_inc(p_turned, 1)
                pe.wait_ge(pt_act, i + (base + 1))
                pe.wait_ge(pt_dve, i + (base + 1))
                pe.wait_ge(v_staged, i + (base + 1))
                pe.wait_ge(o_read, i + base)
                for h in range(2):
                    o = proj[h * HD:(h + 1) * HD, 0, :]
                    pe.matmul(o[:, 0:SEQ], v_st[:, 0, h * HD:(h + 1) * HD], probs_t[:, h, 0:SEQ], start=True, stop=False)
                    q0 = P if causal_ else 0
                    last = pe.matmul(o[:, q0:SEQ], v_st[:, 1, h * HD:(h + 1) * HD],
                                     probs_t[:, h, SEQ:2 * SEQ - q0], start=False, stop=True)
                last.then_inc(o_ready, 1)

            def down(s, start, stop):
                hi = w_hi[s.slot][:, :].rearrange("p (k n) -> p k n", k=2)
                lo = w_lo[s.slot][:, :].rearrange("p (k n) -> p k n", k=2)
                for k in range(2):
                    for t in range(TT):
                        for h, w in ((hid_hi, hi), (hid_hi, lo), (hid_lo, hi)):
                            for m in range(2):
                                last = pe.matmul(acc[:, 2 * t + m, :], h[:, k, t * P:(t + 1) * P],
                                                 w[:, k, m * HALF:(m + 1) * HALF],
                                                 start=(start and k == 0 and h is hid_hi and w is hi),
                                                 stop=(stop and k == 1 and h is hid_lo), skip_group_check=True)
                last.then_inc(chunk_used, 1)

            def mlp(name, operand, before=None):
                c0, n = FIRST[name]
                base = ROUNDS[name]
                pe.wait_ge(h_ready, OPERANDS.index(operand) + 1)
                if before:
                    before()
                for t in range(TT):
                    for m in range(2):
                        pe.matmul(acc[:, 2 * t + m, :], ident[:, :], x[:, t, m * HALF:(m + 1) * HALF],
                                  start=True, stop=False, skip_group_check=True)
                for r in range(2):
                    wait_parts(Chunk(c0 + r))
                    product_f(Chunk(c0 + r))
                for i, c, g in mlp_rounds(pe, name):
                    wait_parts(Chunk(c, g))
                    pe.wait_ge(banks_read, i + (base + 1))
                    product_f(Chunk(c, g))
                    wait_parts(Chunk(c + 1, g))
                    product_f(Chunk(c + 1, g))
                    wait_parts(Chunk(c + 2, g))
                    pe.wait_ge(hid_ready, i + (base + 1))
                    down(Chunk(c + 2, g), False, False)
                wait_parts(Chunk(c0 + n - 1))
                pe.wait_ge(hid_ready, base + n // 3)
                down(Chunk(c0 + n - 1), False, True)

            def route():
                pe.wait_ge(router_tables, 16 * ROUTER_DMAS)
                for t in range(TT):
                    for k in range(KT):
                        for h in (h_hi, h_lo):
                            last = pe.matmul(misc[:, t * NL:(t + 1) * NL], h[:, k, t * P:(t + 1) * P].bitcast(f32),
                                             w_route[:, k, :], start=(k == 0 and h is h_hi),
                                             stop=(k == KT - 1 and h is h_lo))
                last.then_inc(routed, 1)
                pe.wait_ge(comb_made, 1)
                for t in range(TT):
                    last = pe.transpose(misc[0:EXPERTS, SEQ + t * P:SEQ + (t + 1) * P],
                                        comb_t[:, t, :, :].rearrange("p g e -> p (g e)"), ident[:, :])
                last.then_inc(comb_turned, 1)
                pe.wait_ge(comb_f_ready, 1)
                for k in range(EXPERTS // 2):
                    if k >= RING:
                        pe.wait_ge(comb_dve if (k - RING) % 2 else comb_act, (k - RING) // 2 + 1)
                    for a in range(2):
                        e = 2 * k + a
                        last = pe.matmul(pair(k % RING)[:, a, :], ident[0:EXPERTS, e:e + 1].to_broadcast([EXPERTS, P]),
                                         comb_f[:, :], start=True, stop=True)
                    last.then_inc(comb_spread, 1)
                pe.wait_ge(comb_act, EXPERTS // 4)
                pe.wait_ge(comb_dve, EXPERTS // 4)

            def na_attention():
                with pe.Fori(0, PAIRS) as i:
                    pe.wait_ge(qk_squared, i + 1)
                    pe.wait_ge(qk_root, i)
                    for a in range(2):
                        last = pe.matmul(acc[:, 0, a * SEQ:(a + 1) * SEQ], headones[:, :], na_sq[:, a, :],
                                         start=True, stop=True)
                    last.then_inc(qk_summed, 1)
                pe.wait_ge(late_tables, 16 * LATE_DMAS)
                with pe.Fori(0, PAIRS // 2) as ii:
                    for b in range(2):
                        i = ii * 2 + b
                        pe.wait_ge(q_staged, i + 1)
                        pe.wait_ge(masked, i + PAIRS)
                        pe.wait_ge(bias_loaded[b], ii * (8 * 16) + 8 * 16)
                        for h in range(2):
                            r = slice(h * HD, (h + 1) * HD)
                            for t in range(TT):
                                o = acc[:, 1 + h, t * SEQ:(t + 1) * SEQ]
                                pe.matmul(o, qk_st[r, 0, t * P:(t + 1) * P], qk_st[r, 1, :], start=True, stop=False)
                                last = pe.matmul(o, flip[:, :], na_bias[b][:, h, t * SEQ:(t + 1) * SEQ],
                                                 start=False, stop=True)
                        last.then_inc(qk_scored, 1)
                        attention_out(i, PAIRS, False)

            def hyena():
                pe.wait_ge(hyena_tables, 16 * HYENA_DMAS)
                pe.matmul(misc[0:HIDDEN, 0:SEQ], f_w1[:, :], embed[:, :], start=True, stop=True).then_inc(f_summed, 1)
                pe.wait_ge(f_sine, 1)
                pe.matmul(misc[0:HIDDEN, SEQ:2 * SEQ], f_w2[:, :], f_hid[:, :], start=True, stop=True).then_inc(f_summed, 1)
                pe.wait_ge(f_sine, 2)
                pe.wait_ge(drained, DRAINED["hy_out"])
                with pe.Fori(0, D // HALF) as half:
                    for n in range(ORDER):
                        b = half * ORDER + n
                        pe.wait_ge(ys_ready, b)
                        for way in range(2):
                            for t in range(TT):
                                last = pe.matmul(acc[:, 2 * way + t, :], f_hid[:, t * P:(t + 1) * P],
                                                 f_w3[:, ds(half * HALF + (2 * n + way) * D, HALF)], start=True, stop=True)
                        last.then_inc(filt_summed, 1)
                        pe.wait_ge(u_staged, half + 1)
                        pe.wait_ge(z_made, b)
                        for t in range(TT):
                            for m in range(KT // 2):
                                last = pe.transpose(proj[:, 1 + t, m * P:(m + 1) * P], u_st[:, m, t * P:(t + 1) * P], ident[:, :])
                        last.then_inc(u_turned, 1)
                        pe.wait_ge(parity_ready, b + 1)
                        for bank, part_, first in [(acc[:, f, :], f_even, f * P) for f in range(TT)] + \
                                [(acc[:, 2 + f, :], f_odd, 2 * SEQ + f * P) for f in range(TT)] + [(proj[:, 0, :], f_even, 3 * SEQ)]:
                            for t in range(TT):
                                last = pe.matmul(bank, dft[:, t, first:first + P], part_[:, t, :], start=(t == 0), stop=(t == 1))
                        last.then_inc(h_summed, 1)
                        pe.wait_ge(mag_ready, b + 1)
                        for t in range(TT):
                            last = pe.matmul(misc[:, :], ones[:, :], f_abs[:, 0, t, :], start=(t == 0), stop=(t == 1))
                        last.then_inc(norm_summed, 1)
                        pe.wait_ge(ut_ready, b + 1)
                        pe.wait_ge(h_scaled, b + 1)
                        for f in range(2 * TT):
                            for t in range(TT):
                                last = pe.matmul(acc[:, f, :], dft[:, t, f * P:(f + 1) * P], u_t[:, t, :],
                                                 start=(t == 0), stop=(t == 1))
                        last.then_inc(u_summed, 1)
                        pe.wait_ge(ys_ready, b + 1)
                        for m in range(KT // 2):
                            for f in range(2 * TT):
                                last = pe.matmul(pair(1 + m // 2)[:, m % 2, :], ys[:, f, m * P:(m + 1) * P], idft[:, f, :],
                                                 start=(f == 0), stop=(f == 2 * TT - 1))
                        last.then_inc(y_summed, 1)
                pe.wait_ge(z_made, 2 * ORDER)

            pe.wait_ge(params_loaded, 16 * PARAM_DMAS)
            pe.wait_ge(ident_loaded, 16)
            for i in range(PARAM_TILES):
                last = pe.transpose(misc[:, i * P:(i + 1) * P], param_rows[:, i, :], ident[:, :])
            last.then_inc(params_turned, 1)
            norm_turn("attn")
            project("in_zx", product_f, "attn")
            project("in_qk", product_f, "attn")
            project("in_v", product_t, "attn")
            project("in_g", product_f, "attn")
            pe.wait_ge(mixer_tables, MIXER_DMAS * 16)
            pe.wait_ge(params_ready, 1)
            for t in range(TT):
                for k in range(KT):
                    for h in (h_hi, h_lo):
                        last = pe.matmul(misc[:, t * HEADS:(t + 1) * HEADS],
                                         h[:, k, t * P:(t + 1) * P].bitcast(f32), w_dt[:, k, :],
                                         start=(k == 0 and h is h_hi), stop=(k == KT - 1 and h is h_lo))
            last.then_inc(dt_summed, 1)
            ssd()
            project("ssd_out", product_f, "ssd")
            attention()
            project("attn_out", product_f, "attention")
            project("mix_out", product_t, "merged")
            norm_turn("moe")
            mlp("experts", "moe", route)
            norm_turn("ple")
            pe.wait_ge(late_tables, 16 * LATE_DMAS)
            for a in range(2):
                for t in range(TT):
                    last = pe.transpose(misc[:, a * SEQ + t * P:a * SEQ + (t + 1) * P],
                                        p_t[:, t, a * P:(a + 1) * P], ident[:, :])
            last.then_inc(p_turned_ple, 1)
            s = Chunk(FIRST["ple"][0])
            wait_parts(s)
            pe.wait_ge(p_low, 1)
            down(s, True, True)
            project("ple_gate", product_t, "ple")
            norm_turn("mix0")
            project("a_in0", product_f, "mix0")
            project("a_out0", product_t, "conv0")
            norm_turn("ffn0")
            mlp("ffn0", "ffn0")
            norm_turn("mix1")
            project("b_qk", product_f, "mix1")
            project("b_v", product_t, "mix1")
            na_attention()
            project("na_out", product_t, "na")
            norm_turn("ffn1")
            mlp("ffn1", "ffn1")
            norm_turn("mix2")
            project("hy_in", product_f, "mix2")
            hyena()
            project("hy_out", product_t, "hyena")
            norm_turn("ffn2")
            mlp("ffn2", "ffn2")
            norm_turn("mix3")
            project("a_in1", product_f, "mix3")
            project("a_out1", product_t, "conv1")
            norm_turn("ffn3")
            mlp("ffn3", "ffn3")

        @block.gpsimd
        def _(pool):
            chain = Chain(pool, pool_chain)

            def part(s):
                if s.more and s.slot == POOL_SLOT:
                    low(s.ahead())

            def low(n):
                pool.wait_ge(hi_ready, n.c + 1)
                pool.tensor_tensor(w_lo[n.slot][:, :], raw[n.slot][:, :], w_hi[n.slot][:, :].bitcast(f32), SUB)\
                    .then_inc(lo_pool, 1)

            def parts(name):
                for j, s in chunks(pool, name):
                    part(s)

            def parts_mlp(name):
                c0, n = FIRST[name]
                part(Chunk(c0))
                part(Chunk(c0 + 1))
                for i, c, g in mlp_rounds(pool, name):
                    for r in range(3):
                        part(Chunk(c + r, g))
                part(Chunk(c0 + n - 1))

            def norm_root(operand):
                n = SQUARED.index(operand)
                pool.wait_ge(ssq_ready, TT * (n + 1))
                if n:
                    pool.wait_ge(scaled_ready, TT * n)
                chain.link(pool.tensor_scalar(ms[:, :], ssq[:, :], 1.0 / D, EPS, MUL, ADD))
                pool.tensor_tensor(inv[:, :], ms[:, :], neg_half[:, :], ALU.pow).then_inc(inv_ready, 1)

            pool.memset(param_rows[:, :, :], 0.0).then_inc(rows_cleared, 1)
            pool.memset(neg_half[:, :], -0.5).then_inc(small, 1)
            pool.memset(ones[:, :], 1.0).then_inc(small, 1)
            pool.memset(eps_col[:, :], EPS).then_inc(small, 1)
            pool.wait_ge(small, 3)
            low(Chunk(POOL_SLOT))
            norm_root("attn")
            parts("in_zx")
            parts("in_qk")
            parts("in_v")
            parts("in_g")
            parts("ssd_out")
            parts("attn_out")
            parts("mix_out")
            norm_root("moe")
            parts_mlp("experts")
            norm_root("ple")
            parts("ple")
            parts("ple_gate")
            norm_root("final")
            norm_root("mix0")
            parts("a_in0")
            parts("a_out0")
            norm_root("ffn0")
            parts_mlp("ffn0")
            norm_root("mix1")
            parts("b_qk")
            parts("b_v")
            parts("na_out")
            norm_root("ffn1")
            parts_mlp("ffn1")
            norm_root("mix2")
            parts("hy_in")
            parts("hy_out")
            norm_root("ffn2")
            parts_mlp("ffn2")
            norm_root("mix3")
            parts("a_in1")
            parts("a_out1")
            norm_root("ffn3")
            parts_mlp("ffn3")

        @block.scalar
        def _(act):
            def part(s):
                if s.more:
                    act.wait_ge(chunk_used, s.c + 1)
                    high(s.ahead())

            def high(n):
                act.wait_ge(raw_loaded[n.slot], (n.turn + 1) * 16)
                act.activation(w_hi[n.slot][:, :], raw[n.slot][:, :], ACT.Copy).then_inc(hi_ready, 1)

            def parts(name):
                for j, s in chunks(act, name):
                    part(s)

            def norm(operand):
                n = NORM_OF[operand]
                state, gain, row = X_STATES.index(NORMS[n][1]), NORMS[n][2], NORMS[n][3]
                squares(SQUARED.index(operand), state)
                for kk in range(KT // 2):
                    act.wait_ge(turned, n * (KT // 2) + kk + 1)
                    for a in range(2):
                        col = ROW[gain] + row + 2 * kk + a
                        act.activation(h_hi[:, 2 * kk + a, :], pair(kk % RING)[:, a, :], ACT.Copy,
                                       scale=params[:, col:col + 1]).then_inc(fhi_ready, 1)

            def squares(n, state):
                if state == 0:
                    act.wait_ge(x_loaded, 16)
                else:
                    act.wait_ge(x_ready, state)
                if n:
                    act.wait_ge(inv_ready, n)
                for t in range(TT):
                    if t or n:
                        act.wait_ge(ssq_ready, TT * n + t)
                    act.activation(x_scaled[:, t, :], x[:, t, :], ACT.Square, accum_out=ssq[:, t:t + 1])\
                        .then_inc(ssq_ready, 1)

            def softmax_exp(i, base, causal_):
                act.wait_ge(max_ready, i + (base + 1))
                for h in range(2):
                    for t, (c, n) in enumerate(SCORE_COLS[causal_]):
                        act.activation(probs[:, h, c:c + n], probs[:, h, c:c + n], ACT.Exp,
                                       bias=at_max[:, h, t:t + 1], accum_out=at_sum[:, h, t:t + 1]).then_inc(exped, 1)
                n = TRI if causal_ else 2 * SEQ
                act.wait_ge(p_turned, i + (base + 1))
                act.activation(probs_t[:, 0, 0:n], acc[:, 3, 0:n], ACT.Copy).then_inc(pt_act, 1)
                act.wait_ge(o_ready, i + (base + 1))
                act.activation(h_hi[:, i, :], proj[:, 0, 0:SEQ], ACT.Copy).then_inc(o_hi, 1)

            def silu_gate(base, i, c):
                act.wait_ge(chunk_used, c.c + 1)
                if not (isinstance(i, int) and base + i == 0):
                    act.wait_ge(banks_read, i + base)
                act.activation(silu_g[:, :], proj[:, c.slot, :], ACT.Silu).then_inc(silu_ready, 1)

            def parts_mlp(name):
                c0, n = FIRST[name]
                base = ROUNDS[name]
                silu_gate(base, 0, Chunk(c0))
                part(Chunk(c0))
                part(Chunk(c0 + 1))
                for i, c, g in mlp_rounds(act, name):
                    silu_gate(base, i + 1, Chunk(c, g))
                    for r in range(3):
                        part(Chunk(c + r, g))
                part(Chunk(c0 + n - 1))

            def short_conv(layer):
                act.wait_ge(cu_ready, layer + 1)
                for m in range(KT):
                    col = ROW["a_conv_w_2"] + (layer * 3 + 1) * KT + m
                    act.activation(acv[:, m, :], cu[:, m, :], ACT.Copy, scale=params[:, col:col + 1]).then_inc(a_first, 1)

            def hyena_scalar():
                act.wait_ge(drained, DRAINED["hy_out"])
                w, b0 = ROW["c_short_w_2"] + 3 * KT, ROW["c_short_b_2"]
                with act.Fori(0, 3 * KT) as m:
                    act.activation(hc[:, ds(m, 1), :].rearrange("p o n -> p (o n)"),
                                   pj[:, ds(m, 1), :].rearrange("p o n -> p (o n)"), ACT.Identity,
                                   bias=params[:, ds(m + b0, 1)], scale=params[:, ds(m + w, 1)]).then_inc(hc_first, 1)
                for layer in range(2):
                    act.wait_ge(f_angle, layer + 1)
                    act.activation(f_hid[:, :], f_hid[:, :], ACT.Sin).then_inc(f_sine, 1)
                act.wait_ge(hc_taps, 6 * KT)
                with act.Fori(0, D // HALF) as half:
                    for n in range(ORDER):
                        b = half * ORDER + n
                        if n == 0:
                            act.wait_ge(z_made, b)
                            act.activation(u_st[:, :, :], hc[:, ds(half * (KT // 2), KT // 2), :], ACT.Copy).then_inc(u_staged, 1)
                        act.wait_ge(filt_summed, b + 1)
                        act.wait_ge(parity_ready, b)
                        act.activation(f_rev[:, :, :], acc[:, 2:4, :], ACT.Copy).then_inc(rev_copied, 1)
                        act.wait_ge(u_turned, b + 1)
                        act.wait_ge(u_summed, b)
                        act.activation(u_t[:, :, :], proj[:, 1:3, :], ACT.Copy).then_inc(ut_ready, 1)
                        act.wait_ge(parity_ready, b + 1)
                        act.wait_ge(y_summed, b)
                        act.activation(f_abs[:, 0, :, :], f_even[:, :, :], ACT.Abs).then_inc(abs_ready, 1)
                        act.activation(f_abs[:, 1, :, :], f_odd[:, :, :], ACT.Abs).then_inc(abs_ready, 1)

            for c in range(RING):
                high(Chunk(c))
            act.wait_ge(params_ready, 1)
            norm("attn")
            parts("in_zx")
            parts("in_qk")
            parts("in_v")
            parts("in_g")
            act.wait_ge(drained, DRAINED["in_g"] + FIRST["in_g"][1])
            act.activation(pj[:, GS0:GS0 + 2 * KT, :], pj[:, GS0:GS0 + 2 * KT, :], ACT.Sigmoid).then_inc(gates_ready, 1)
            act.activation(pj[:, Z0:Z0 + KT, :], pj[:, Z0:Z0 + KT, :], ACT.Silu).then_inc(z_ready, 1)
            w0, b0 = ROW["conv_w"] + 3 * XBC_TILES, ROW["conv_b"]
            for m in range(XBC_TILES):
                act.activation(conv[:, m, :], pj[:, XBC0 + m, :], ACT.Identity, bias=params[:, b0 + m:b0 + m + 1],
                               scale=params[:, w0 + m:w0 + m + 1]).then_inc(conv_first, 1)
            act.wait_ge(dt_step, 2)
            act.activation(dt_u[:, :, :], dt_n[:, :, :], ACT.Exp, scale=-1.0).then_inc(dt_exped, 1)
            act.activation(a_rate[:, :], a_log_b[:, :], ACT.Exp).then_inc(dt_exped, 1)
            act.wait_ge(dt_step, 3)
            act.activation(dt_l[:, :, :], dt_w[:, :, :], ACT.Ln).then_inc(dt_exped, 1)
            act.wait_ge(taps_done, 3 * XBC_TILES)
            act.activation(conv[:, :, :], conv[:, :, :], ACT.Silu).then_inc(conv_ready, 1)
            with act.Fori(0, PAIRS) as i:
                act.wait_ge(gaps_ready, i + 1)
                act.activation(decay[:, :, :], decay[:, :, :], ACT.Exp).then_inc(decay_ready, 1)
            for g in range(SSD_GROUPS):
                if g:
                    act.wait_ge(y_ssq, g)
                else:
                    act.wait_ge(y_gated, PAIRS)
                act.activation(sq_buf[:, :, :], pj[:, Z0 + 4 * g:Z0 + 4 * g + 4, :], ACT.Square).then_inc(y_squared, 1)
                act.wait_ge(y_ssq, g + 1)
                if g:
                    act.wait_ge(y_normed, g)
                act.activation(rstd[:, :], acc[:, g, 0:SEQ], ACT.Sqrt, bias=eps_col[:, 0:1],
                               scale=1.0 / (SSD_INNER // SSD_GROUPS)).then_inc(y_root, 1)
            parts("ssd_out")
            for k, (dst, scale) in enumerate(((sin_f, 1.0), (cos_f, 0.5))):
                act.wait_ge(angles, 1)
                act.activation(dst[:, :], ang[:, :], ACT.Sin, scale=scale).then_inc(sines, 1)
            with act.Fori(0, PAIRS) as i:
                act.wait_ge(o_ready, i)
                act.activation(v_st[:, :, :], v_t[:, :, ds(i * P, P)], ACT.Copy).then_inc(v_staged, 1)
                softmax_exp(i, 0, True)
            parts("attn_out")
            parts("mix_out")
            norm("moe")
            for t in range(TT):
                act.wait_ge(gaps_e, 1)
                act.activation(g_exp[:, t, :], logits[:, t, 0:N_GROUPS], ACT.Exp, bias=g_neg[:, t:t + 1],
                               accum_out=g_sum[:, t:t + 1]).then_inc(exp_e, 1)
            act.wait_ge(gaps_e, 2)
            act.activation(e_exp[:, :], e_gap[:, :], ACT.Exp).then_inc(exp_e, 1)
            for k in range(0, EXPERTS // 2, 2):
                act.wait_ge(comb_spread, k + 1)
                act.activation(comb[:, 2 * k:2 * k + 2, :], pair(k % RING), ACT.Copy).then_inc(comb_act, 1)
            parts_mlp("experts")
            norm("ple")
            act.wait_ge(p_turned_ple, 1)
            act.activation(hid_hi[:, :, :], misc[:, :].rearrange("p (a n) -> p a n", a=2), ACT.Copy).then_inc(p_split, 1)
            parts("ple")
            for j, s in chunks(act, "ple_gate"):
                act.wait_ge(chunk_used, s.c + 1)
                act.wait_ge(drained, j + DRAINED["ple_gate"])
                act.activation(gate_s[:, :, :], pair(s.slot), ACT.Sigmoid).then_inc(gate_sig, 1)
                part(s)
            squares(SQUARED.index("final"), X_STATES.index("ple"))
            norm("mix0")
            parts("a_in0")
            short_conv(0)
            parts("a_out0")
            norm("ffn0")
            parts_mlp("ffn0")
            norm("mix1")
            parts("b_qk")
            parts("b_v")
            act.wait_ge(drained, DRAINED["na_out"])
            act.wait_ge(late_tables, 16 * LATE_DMAS)
            with act.Fori(0, PAIRS) as i:
                qk = pj[:, 0:2 * KT, :].rearrange("p (a e) n -> p a e n", a=2)[:, :, i, :]
                act.wait_ge(qk_summed, i)
                act.activation(na_sq[:, :, :], qk, ACT.Square).then_inc(qk_squared, 1)
                act.wait_ge(qk_summed, i + 1)
                act.wait_ge(qk_normed, i)
                act.activation(na_rs[:, :, :], acc[:, 0, :].rearrange("p (a n) -> p a n", a=2), ACT.Sqrt,
                               bias=eps_col[:, 0:1], scale=1.0 / HD).then_inc(qk_root, 1)
            with act.Fori(0, PAIRS) as i:
                act.wait_ge(qk_normed, PAIRS)
                act.wait_ge(qk_scored, i + PAIRS)
                act.activation(qk_st[:, :, :], pj[:, 0:2 * KT, :].rearrange("p (a e) n -> p a e n", a=2)[:, :, i, :],
                               ACT.Copy).then_inc(q_staged, 1)
                act.wait_ge(o_ready, i + PAIRS)
                act.activation(v_st[:, :, :], v_t[:, :, ds(i * P, P)], ACT.Copy).then_inc(v_staged, 1)
                softmax_exp(i, PAIRS, False)
            parts("na_out")
            norm("ffn1")
            parts_mlp("ffn1")
            norm("mix2")
            parts("hy_in")
            hyena_scalar()
            parts("hy_out")
            norm("ffn2")
            parts_mlp("ffn2")
            norm("mix3")
            parts("a_in1")
            short_conv(1)
            parts("a_out1")
            norm("ffn3")
            parts_mlp("ffn3")

        @block.vector
        def _(dve):
            chain = Chain(dve, dve_chain)
            link = chain.link

            def part(s):
                if s.more and s.slot != POOL_SLOT:
                    low(s.ahead())

            def low(n):
                dve.wait_ge(hi_ready, n.c + 1)
                dve.tensor_tensor(w_lo[n.slot][:, :], raw[n.slot][:, :], w_hi[n.slot][:, :].bitcast(f32), SUB)\
                    .then_inc(lo_dve, 1)

            def drain(name, read):
                for j, s in chunks(dve, name):
                    dve.wait_ge(chunk_used, s.c + 1)
                    read(j, pair(s.slot), s).then_inc(drained, 1)
                    part(s)

            def drain_to(name, tile):
                drain(name, lambda j, bank, s: dve.tensor_copy(pj[:, ds(j * 2 + tile, 2), :], bank))

            def drain_x(name):
                def read(j, bank, s):
                    xs = x[:, :, ds(j * COLS, COLS)]
                    return dve.tensor_tensor(xs, xs, bank, ADD)
                drain(name, read)
                dve.wait_ge(drained, DRAINED[name] + FIRST[name][1])
                signal(x_ready)

            def signal(s):
                dve.engine_nop().then_inc(s, 1)

            def scale_x(operand):
                n = SQUARED.index(operand)
                dve.wait_ge(inv_ready, n + 1)
                for t in range(TT):
                    dve.tensor_scalar(x_scaled[:, t, :], x[:, t, :], inv[:, t:t + 1], None, MUL).then_inc(scaled_ready, 1)

            def norm(operand):
                n = NORM_OF[operand]
                gain, row = NORMS[n][2], NORMS[n][3]
                scale_x(operand)
                for kk in range(KT // 2):
                    for a in range(2):
                        k = 2 * kk + a
                        col = ROW[gain] + row + k
                        dve.wait_ge(fhi_ready, n * KT + 2 * kk + 2)
                        last = dve.scalar_tensor_tensor(out=h_lo[:, k, :], in0=pair(kk % RING)[:, a, :],
                                                        scalar=params[:, col:col + 1], in1=h_hi[:, k, :].bitcast(f32),
                                                        op0=MUL, op1=SUB)
                        if a:
                            last.then_inc(turned_read, 1)
                dve.wait_ge(turned_read, (n + 1) * (KT // 2))
                signal(h_ready)

            def split_h(src, tiles=KT):
                link(dve.tensor_copy(h_hi[:, 0:tiles, :], src))
                link(dve.tensor_tensor(h_lo[:, 0:tiles, :], src, h_hi[:, 0:tiles, :].bitcast(f32), SUB))
                signal(h_ready)

            for c in range(RING):
                if c != POOL_SLOT:
                    low(Chunk(c))
            dve.wait_ge(params_turned, 1)
            dve.tensor_copy(params[:, :], misc[:, 0:PARAM_TILES * P]).then_inc(params_ready, 1)
            dve.wait_ge(params_ready, 1)
            norm("attn")
            drain_to("in_zx", 0)
            drain_to("in_qk", Q0)
            drain("in_v", lambda j, bank, s: dve.tensor_copy(v_t[:, :, ds(j * COLS, COLS)], bank))
            drain_to("in_g", GS0)
            dve.wait_ge(mixer_tables, MIXER_DMAS * 16)
            dve.wait_ge(dt_summed, 1)
            dve.tensor_tensor(dt_x[:, :, :], misc[:, 0:TT * HEADS].rearrange("p (t h) -> p t h", t=TT),
                              dt_bias[:, :].unsqueeze(1).to_broadcast([P, TT, HEADS]), ADD).then_inc(dt_step, 1)
            dve.wait_ge(dt_step, 1)
            dve.scalar_tensor_tensor(out=dt_n[:, :, :], in0=dt_x[:, :, :], scalar=-1.0, in1=dt_x[:, :, :],
                                     op0=MUL, op1=ALU.max).then_inc(dt_step, 1)
            dve.wait_ge(dt_exped, 2)
            dve.tensor_scalar(dt_w[:, :, :], dt_u[:, :, :], 1.0, None, ADD).then_inc(dt_step, 1)
            dve.wait_ge(dt_step, 3)
            link(dve.tensor_scalar(dt_r[:, :, :], dt_w[:, :, :], -1.0, 1e-30, ADD, ADD))
            link(dve.reciprocal(dt_r[:, :, :], dt_r[:, :, :]))
            link(dve.tensor_tensor(dt_r[:, :, :], dt_r[:, :, :], dt_u[:, :, :], MUL))
            dve.wait_ge(dt_exped, 3)
            link(dve.tensor_scalar(dt_n[:, :, :], dt_l[:, :, :], 1e-30, None, ADD))
            link(dve.tensor_tensor(dt_r[:, :, :], dt_r[:, :, :], dt_n[:, :, :], MUL))
            link(dve.scalar_tensor_tensor(out=dt_t[:, :, :], in0=dt_x[:, :, :], scalar=0.0, in1=dt_r[:, :, :],
                                          op0=ALU.max, op1=ADD))
            dve.scalar_tensor_tensor(out=dA[:, :, :], in0=dt_t[:, :, :], scalar=-1.0,
                                     in1=a_rate[:, :].unsqueeze(1).to_broadcast([P, TT, HEADS]),
                                     op0=MUL, op1=MUL).then_inc(dA_ready, 1)
            for shift in range(1, SSD_TAPS):
                w = ROW["conv_w"] + (SSD_TAPS - 1 - shift) * XBC_TILES
                for m in range(XBC_TILES):
                    dve.wait_ge(conv_first, m + 1)
                    if shift > 1:
                        dve.wait_ge(taps_done, (shift - 2) * XBC_TILES + m + 1)
                    dve.scalar_tensor_tensor(out=conv[:, m, shift:], in0=pj[:, XBC0 + m, 0:SEQ - shift],
                                             scalar=params[:, w + m:w + m + 1], in1=conv[:, m, shift:],
                                             op0=MUL, op1=ADD).then_inc(taps_done, 1)
            dve.wait_ge(cum_summed, 1)
            link(dve.tensor_copy(cum_t[:, :, :], misc[:, 64:64 + TT * HEADS].rearrange("p (t h) -> p t h", t=TT)))
            link(dve.tensor_copy(cum_f[:, :], misc[0:HEADS, SEQ:2 * SEQ]))
            dve.tensor_tensor(cum_diag[:, :, :], cum_f[:, :].unsqueeze(1).to_broadcast([HEADS, HEADS, SEQ]),
                              diag16[:, :].unsqueeze(2).to_broadcast([HEADS, HEADS, SEQ]), MUL).then_inc(cum_ready, 1)
            for kk in range(KT // 2):
                dve.wait_ge(xs_turned, kk + 1)
                dve.tensor_copy(xs_t[:, :, kk * COLS:(kk + 1) * COLS], pair(kk % RING)).then_inc(xs_read, 1)
            dve.wait_ge(cb_summed, 1)
            for g in range(SSD_GROUPS):
                link(dve.tensor_tensor(cb[:, g, 0:SEQ], acc[:, g, 0:SEQ], tri[:, 0, :], MUL))
                link(dve.tensor_tensor(cb[:, g, SEQ:TRI], acc[:, g, SEQ:TRI], tri[:, 1, P:SEQ], MUL))
            dve.wait_ge(xs_read, KT // 2)
            dve.wait_ge(gates_ready, 1)
            dve.wait_ge(z_ready, 1)
            for g in range(SSD_GROUPS):
                n = PAIRS // SSD_GROUPS
                with dve.Fori(0, n) as ii:
                    i = ii + g * n
                    dve.wait_ge(y_ready, i)
                    dve.tensor_tensor(xdt[:, :, :].rearrange("p t (h c) -> p t h c", h=2),
                                      xs_t[:, :, ds(i * P, P)].rearrange("p t (h c) -> p t h c", h=2),
                                      dt_t[:, :, ds(i * 2, 2)].unsqueeze(3).to_broadcast([P, TT, 2, HD]), MUL)\
                        .then_inc(xdt_ready, 1)
                    dve.wait_ge(cum_spread, i + 1)
                    for h in range(2):
                        for t, (a, b, q0) in enumerate(((0, SEQ, 0), (SEQ, TRI, P))):
                            last = dve.tensor_scalar(decay[:, h, a:b], acc[:, 2, h * SEQ + q0:(h + 1) * SEQ],
                                                     cum_t[:, t, ds(i * 2 + h, 1)], 0.0, SUB, ALU.min)
                    last.then_inc(gaps_ready, 1)
                    dve.wait_ge(decay_ready, i + 1)
                    dve.wait_ge(xdt_ready, i + 1)
                    dve.tensor_tensor(decay[:, :, :], decay[:, :, :],
                                      cb[:, g, :].unsqueeze(1).to_broadcast([P, 2, TRI]), MUL).then_inc(scores_ready, 1)
                    dve.wait_ge(y_ready, i + 1)
                    dve.scalar_tensor_tensor(out=y_sum[:, :], in0=conv[:, i, :], scalar=d_col[:, ds(i, 1)],
                                             in1=acc[:, 3, 0:SEQ], op0=MUL, op1=ADD).then_inc(y_read, 1)
                    dve.wait_ge(y_read, i + 1)
                    dve.tensor_tensor(pj[:, i, :], pj[:, i, :], y_sum[:, :], MUL).then_inc(y_gated, 1)
            for g in range(SSD_GROUPS):
                dve.wait_ge(y_gated, PAIRS)
                dve.wait_ge(y_root, g + 1)
                link(dve.reciprocal(rstd[:, :], rstd[:, :]))
                for a in range(4):
                    col = ROW["ssd_norm_w"] + 4 * g + a
                    last = dve.scalar_tensor_tensor(out=ynorm[:, a, :], in0=pj[:, 4 * g + a, :],
                                                    scalar=params[:, col:col + 1], in1=rstd[:, :],
                                                    op0=MUL, op1=MUL)
                last.then_inc(y_normed, 1)
                dve.wait_ge(y_normed, g + 1)
                link(dve.tensor_copy(h_hi[:, 4 * g:4 * g + 4, :], ynorm[:, :, :]))
                link(dve.tensor_tensor(h_lo[:, 4 * g:4 * g + 4, :], ynorm[:, :, :],
                                       h_hi[:, 4 * g:4 * g + 4, :].bitcast(f32), SUB))
            signal(h_ready)
            drain("ssd_out", lambda j, bank, s: dve.tensor_tensor(
                pj[:, ds(j * 2, 2), :], bank, pj[:, ds(j * 2 + GS0, 2), :], MUL))

            def softmax_rows(i, base, causal_):
                cols = SCORE_COLS[causal_]
                dve.wait_ge(masked, i + (base + 1))
                if causal_:
                    for t, (c, n) in enumerate(cols):
                        last = dve.tensor_reduce(at_max[:, :, t:t + 1].rearrange("p h o -> p (h o)"), probs[:, :, c:c + n],
                                                 AX.X, ALU.max, negate=True)
                else:
                    last = dve.tensor_reduce(at_max[:, :, :], probs[:, :, :].rearrange("p h (t k) -> p h t k", t=TT),
                                             AX.X, ALU.max, negate=True)
                last.then_inc(max_ready, 1)
                dve.wait_ge(exped, i * 4 + (base * 4 + 4))
                link(dve.reciprocal(at_inv[:, :, :], at_sum[:, :, :]))
                for h in range(2):
                    for t, (c, n) in enumerate(cols):
                        last = dve.tensor_scalar(probs[:, h, c:c + n], probs[:, h, c:c + n],
                                                 at_inv[:, h, t:t + 1], None, MUL)
                last.then_inc(normed, 1)
                dve.wait_ge(p_turned, i + (base + 1))
                n = TRI if causal_ else 2 * SEQ
                dve.tensor_copy(probs_t[:, 1, 0:n], misc[:, 0:n]).then_inc(pt_dve, 1)
                dve.wait_ge(o_hi, i + (base + 1))
                dve.tensor_tensor(h_lo[:, i, :], proj[:, 0, 0:SEQ], h_hi[:, i, :].bitcast(f32), SUB).then_inc(o_read, 1)

            dve.tensor_copy(ang_k[:, :], pos_i[:, :]).then_inc(dve_chain, 1)
            chain.count += 1
            dve.wait_ge(dve_chain, chain.count)
            link(dve.tensor_scalar(ang[:, :], ang_k[:, :], inv_freq[:, 0:1], None, MUL))
            reduce_angle(dve, link, ang[:, :], ang_k[:, :])
            signal(angles)
            dve.wait_ge(sines, 2)
            link(dve.tensor_tensor(cos_f[:, :], cos_f[:, :], cos_f[:, :], MUL))
            link(dve.tensor_scalar(cos_f[:, :], cos_f[:, :], -2.0, 1.0, MUL, ADD))
            with dve.Fori(0, PAIRS) as i:
                chain.begin(i, 3)
                qk = pj[:, Q0:Q0 + 2 * KT, :].rearrange("p (a e) n -> p a e n", a=2)[:, :, i, :]
                link(dve.tensor_tensor(rope_t[:, :, :], qk, cos_f[:, :].unsqueeze(1).to_broadcast([P, 2, SEQ]), MUL))
                dve.wait_ge(rotated, i + 1)
                link(dve.tensor_tensor(rope_u[:, :, :], acc[:, 0, :].rearrange("p (a n) -> p a n", a=2),
                                       sin_f[:, :].unsqueeze(1).to_broadcast([P, 2, SEQ]), MUL))
                dve.wait_ge(qk_scored, i)
                dve.tensor_tensor(qk_st[:, :, :], rope_t[:, :, :], rope_u[:, :, :], ADD).then_inc(roped, 1)
                dve.wait_ge(qk_scored, i + 1)
                dve.wait_ge(p_turned, i)
                dve.scalar_tensor_tensor(out=probs[:, :, 0:TRI], in0=acc[:, 1:3, 0:TRI], scalar=HD ** -0.5,
                                         in1=causal[:, :].unsqueeze(1).to_broadcast([P, 2, TRI]),
                                         op0=MUL, op1=ADD).then_inc(masked, 1)
                softmax_rows(i, 0, True)
            chain.end(PAIRS)
            dve.wait_ge(o_read, PAIRS)
            signal(h_ready)
            def merge(j, bank, s):
                dve.wait_ge(drained, j + DRAINED["attn_out"])
                link(dve.tensor_tensor(merge_t[:, :, :], bank, pj[:, ds(j * 2 + GA0, 2), :], MUL))
                return dve.tensor_tensor(pj[:, ds(j * 2, 2), :], pj[:, ds(j * 2, 2), :], merge_t[:, :, :], ADD)
            drain("attn_out", merge)
            dve.wait_ge(drained, DRAINED["attn_out"] + 4)
            split_h(pj[:, 0:KT, :])
            drain_x("mix_out")
            def gated(name, weighted=False):
                c0, n = FIRST[name]
                base = ROUNDS[name]

                def product(i, c):
                    dve.wait_ge(silu_ready, i + (base + 1))
                    dve.wait_ge(hid_ready, i + base)
                    dve.wait_ge(chunk_used, c.c + 1)
                    dve.tensor_tensor(hid[:, :, :], silu_g[:, :].rearrange("p (a n) -> p a n", a=2), pair(c.slot), MUL)\
                        .then_inc(banks_read, 1)
                    dve.wait_ge(banks_read, i + (base + 1))
                    if weighted:
                        link(dve.tensor_tensor(hid[:, :, :], hid[:, :, :], comb[:, ds(i, 1), :].to_broadcast([P, 2, SEQ]), MUL))

                def split(i):
                    link(dve.tensor_copy(hid_hi[:, :, :], hid[:, :, :]))
                    dve.tensor_tensor(hid_lo[:, :, :], hid[:, :, :], hid_hi[:, :, :].bitcast(f32), SUB).then_inc(hid_ready, 1)

                dve.wait_ge(chunk_used, c0 + 1)
                part(Chunk(c0))
                product(0, Chunk(c0 + 1))
                part(Chunk(c0 + 1))
                split(0)
                rounds = n // 3 - 1
                looped = rounds - (1 if c0 + n == TOTAL else 0)
                for i, c, g in mlp_rounds(dve, name):
                    if g is i:
                        chain.begin(i, 2 if weighted else 1)
                    dve.wait_ge(chunk_used, Chunk(c, g).c + 1)
                    part(Chunk(c, g))
                    product(i + 1, Chunk(c + 1, g))
                    part(Chunk(c + 1, g))
                    dve.wait_ge(chunk_used, Chunk(c + 2, g).c + 1)
                    split(i + 1)
                    part(Chunk(c + 2, g))
                    if g is i:
                        chain.end(looped)
                dve.wait_ge(chunk_used, c0 + n)
                part(Chunk(c0 + n - 1))
                dve.tensor_copy(x[:, :, :], acc[:, :, :].rearrange("p (t m) n -> p t (m n)", t=TT)).then_inc(x_ready, 1)

            def short_conv(layer):
                cols = ROW["a_conv_w_2"] + layer * 3 * KT
                dve.wait_ge(drained, DRAINED[f"a_out{layer}"])
                dve.tensor_tensor(cu[:, :, :], pj[:, KT:2 * KT, :], pj[:, 2 * KT:3 * KT, :], MUL).then_inc(cu_ready, 1)
                for m in range(KT):
                    dve.wait_ge(a_first, layer * KT + m + 1)
                    dve.scalar_tensor_tensor(out=acv[:, m, 1:], in0=cu[:, m, 0:SEQ - 1], scalar=params[:, cols + m:cols + m + 1],
                                             in1=acv[:, m, 1:], op0=MUL, op1=ADD).then_inc(a_taps, 1)
                for m in range(KT):
                    dve.wait_ge(a_taps, 2 * KT * layer + m + 1)
                    w = cols + 2 * KT + m
                    dve.scalar_tensor_tensor(out=acv[:, m, 0:SEQ - 1], in0=cu[:, m, 1:], scalar=params[:, w:w + 1],
                                             in1=acv[:, m, 0:SEQ - 1], op0=MUL, op1=ADD).then_inc(a_taps, 1)
                dve.wait_ge(a_taps, 2 * KT * (layer + 1))
                link(dve.tensor_tensor(acv[:, :, :], acv[:, :, :], pj[:, 0:KT, :], MUL))
                split_h(acv[:, :, :])

            def hyena_vector():
                dve.wait_ge(hyena_tables, 16 * HYENA_DMAS)
                for layer, bias in enumerate((f_b1, f_b2)):
                    dve.wait_ge(f_summed, layer + 1)
                    link(dve.tensor_scalar(f_hid[:, :], misc[0:HIDDEN, layer * SEQ:(layer + 1) * SEQ], bias[:, 0:1],
                                           f_freq[:, 0:1], ADD, MUL))
                    reduce_angle(dve, link, f_hid[:, :], f_k[:, :])
                    signal(f_angle)
                w = ROW["c_short_w_2"]
                with dve.Fori(0, 3 * KT) as m:
                    dve.wait_ge(hc_first, m + 1)
                    tile, src = [a[:, ds(m, 1), :].rearrange("p o n -> p (o n)") for a in (hc, pj)]
                    dve.scalar_tensor_tensor(out=tile[:, 1:], in0=src[:, 0:SEQ - 1], scalar=params[:, ds(m + w, 1)],
                                             in1=tile[:, 1:], op0=MUL, op1=ADD).then_inc(hc_taps, 1)
                    dve.wait_ge(hc_taps, m * 2 + 1)
                    dve.scalar_tensor_tensor(out=tile[:, 0:SEQ - 1], in0=src[:, 1:], scalar=params[:, ds(m + (w + 6 * KT), 1)],
                                             in1=tile[:, 0:SEQ - 1], op0=MUL, op1=ADD).then_inc(hc_taps, 1)
                dve.wait_ge(hc_taps, 6 * KT)
                with dve.Fori(0, D // HALF) as half:
                    chain.begin(half, ORDER * 17)
                    for n in range(ORDER):
                        b = half * ORDER + n
                        decay_half = f_decay[:, :, ds(half * HALF, HALF)]
                        dve.wait_ge(rev_copied, b + 1)
                        dve.wait_ge(h_summed, b)
                        dve.wait_ge(abs_ready, 2 * b)
                        link(dve.tensor_tensor(f_even[:, :, :], acc[:, 0:2, :], f_rev[:, :, :], ADD))
                        link(dve.tensor_tensor(f_odd[:, :, :], acc[:, 0:2, :], f_rev[:, :, :], SUB))
                        link(dve.tensor_tensor(f_even[:, :, :], f_even[:, :, :], decay_half, MUL))
                        link(dve.tensor_tensor(f_odd[:, :, :], f_odd[:, :, :], decay_half, MUL))
                        dve.memset(f_odd[0:1, 0, :], 0.0).then_inc(parity_ready, 1)
                        dve.wait_ge(abs_ready, 2 * b + 2)
                        dve.tensor_tensor(f_abs[:, 0, :, :], f_abs[:, 0, :, :], f_abs[:, 1, :, :], ALU.max).then_inc(mag_ready, 1)
                        dve.wait_ge(norm_summed, b + 1)
                        link(dve.reciprocal(f_inv[:, :], misc[:, :]))
                        dve.wait_ge(h_summed, b + 1)
                        norm_b = f_inv[:, :].unsqueeze(1).to_broadcast([P, TT, HALF])
                        link(dve.tensor_tensor(hs_re[:, :, :], acc[:, 0:2, :], norm_b, MUL))
                        link(dve.tensor_tensor(hs_im[:, :, :], acc[:, 2:4, :], norm_b, MUL))
                        dve.tensor_tensor(hs_re2[:, :], proj[:, 0, :], f_inv[:, :], MUL).then_inc(h_scaled, 1)
                        dve.wait_ge(u_summed, b + 1)
                        dve.wait_ge(h_scaled, b + 1)
                        link(dve.tensor_tensor(ys[:, 0:2, :], acc[:, 0:2, :], hs_re[:, :, :], MUL))
                        link(dve.tensor_tensor(ys_t[:, :, :], acc[:, 2:4, :], hs_im[:, :, :], MUL))
                        link(dve.tensor_tensor(ys[:, 0:2, :], ys[:, 0:2, :], ys_t[:, :, :], SUB))
                        link(dve.tensor_tensor(ys[:, 2:4, :], acc[:, 0:2, :], hs_im[:, :, :], MUL))
                        link(dve.tensor_tensor(ys_t[:, 0, :], acc[:, 2, :], hs_re2[:, :], MUL))
                        link(dve.tensor_tensor(ys_t[:, 1, :], acc[:, 3, :], hs_re[:, 1, :], MUL))
                        dve.tensor_tensor(ys[:, 2:4, :], ys[:, 2:4, :], ys_t[:, :, :], ADD).then_inc(ys_ready, 1)
                        dve.wait_ge(y_summed, b + 1)
                        dve.wait_ge(ys_ready, b + 1)
                        z = ys_t[:, :, :].rearrange("p t n -> p (t n)").rearrange("p (m n) -> p m n", n=SEQ)
                        for m in range(KT // 2):
                            skip = params[:, ds(half * (KT // 2) + (ROW["c_f_skip_2"] + n * KT + m), 1)]
                            link(dve.scalar_tensor_tensor(out=z[:, m, :], in0=u_st[:, m, :], scalar=skip,
                                                          in1=pair(1 + m // 2)[:, m % 2, :], op0=MUL, op1=ADD))
                        gate = hc[:, ds(half * (KT // 2) + (n + 1) * KT, KT // 2), :]
                        dest = hc[:, ds(half * (KT // 2), KT // 2), :] if n == ORDER - 1 else u_st[:, :, :]
                        dve.tensor_tensor(dest, z[:, :, :], gate, MUL).then_inc(z_made, 1)
                        dve.wait_ge(z_made, b + 1)
                chain.end(D // HALF)
                split_h(hc[:, 0:KT, :])

            norm("moe")
            dve.wait_ge(router_tables, 16 * ROUTER_DMAS)
            link(dve.memset(g_pad[:, :, :], -3e38))
            dve.wait_ge(routed, 1)
            link(dve.tensor_tensor(logits[:, :, :], misc[:, 0:TT * NL].rearrange("p (t n) -> p t n", t=TT),
                                   b_route[:, :].unsqueeze(1).to_broadcast([P, TT, NL]), ADD))
            link(dve.tensor_copy(g_pad[:, :, 0:N_GROUPS], logits[:, :, 0:N_GROUPS]))
            for t in range(TT):
                link(dve.max(g_top[:, t, :], g_pad[:, t, :]))
            dve.tensor_scalar(g_neg[:, :], g_top[:, :, 0], -1.0, None, MUL).then_inc(gaps_e, 1)
            for t in range(TT):
                link(dve.max_index(out=g_idx[:, t, :], in_max=g_top[:, t, :], in_values=g_pad[:, t, :]))
            link(dve.tensor_copy(g_idxf[:, :], g_idx[:, :, 0]))
            for t in range(TT):
                link(dve.tensor_scalar(g_hot[:, t, :], iota8[:, 0:N_GROUPS], g_idxf[:, t:t + 1], None, ALU.is_equal))
            for t in range(TT):
                link(dve.tensor_tensor(e_prod[:, t, :].rearrange("p (g e) -> p g e", g=N_GROUPS),
                                       logits[:, t, N_GROUPS:].rearrange("p (g e) -> p g e", g=N_GROUPS),
                                       g_hot[:, t, :].unsqueeze(2).to_broadcast([P, N_GROUPS, GROUP_EXPERTS]), MUL))
            for t in range(TT):
                link(dve.tensor_reduce(e_sel[:, t, :], e_prod[:, t, :].rearrange("p (g e) -> p e g", g=N_GROUPS), AX.X, ADD))
            for t in range(TT):
                link(dve.max(e_top[:, t, :], e_sel[:, t, :]))
            dve.tensor_tensor(e_gap[:, :], e_top[:, :, 1], e_top[:, :, 0], SUB).then_inc(gaps_e, 1)
            for t in range(TT):
                link(dve.max_index(out=e_idx[:, t, :], in_max=e_top[:, t, :], in_values=e_sel[:, t, :]))
            link(dve.tensor_copy(e_idxf[:, :, :], e_idx[:, :, 0:2]))
            for t in range(TT):
                for k in range(2):
                    link(dve.tensor_scalar(e_hot[:, t, k, :], iota8[:, :], e_idxf[:, t, k:k + 1], None, ALU.is_equal))
            dve.wait_ge(exp_e, 3)
            link(dve.reciprocal(g_w[:, :], g_sum[:, :]))
            link(dve.tensor_scalar(e_den[:, :], e_exp[:, :], 1.0, None, ADD))
            link(dve.reciprocal(e_den[:, :], e_den[:, :]))
            link(dve.tensor_tensor(e_w[:, :, 0], e_den[:, :], g_w[:, :], MUL))
            link(dve.tensor_tensor(e_w[:, :, 1], e_w[:, :, 0], e_exp[:, :], MUL))
            for t in range(TT):
                link(dve.tensor_scalar(e_wt[:, t, :], e_hot[:, t, 0, :], e_w[:, t, 0:1], None, MUL))
                link(dve.scalar_tensor_tensor(out=e_wt[:, t, :], in0=e_hot[:, t, 1, :], scalar=e_w[:, t, 1:2],
                                              in1=e_wt[:, t, :], op0=MUL, op1=ADD))
            for t in range(TT):
                link(dve.tensor_tensor(comb_t[:, t, :, :], g_hot[:, t, :].unsqueeze(2).to_broadcast([P, N_GROUPS, GROUP_EXPERTS]),
                                       e_wt[:, t, :].unsqueeze(1).to_broadcast([P, N_GROUPS, GROUP_EXPERTS]), MUL))
            signal(comb_made)
            dve.wait_ge(comb_turned, 1)
            dve.tensor_copy(comb_f[:, :], misc[0:EXPERTS, SEQ:2 * SEQ]).then_inc(comb_f_ready, 1)
            for k in range(1, EXPERTS // 2, 2):
                dve.wait_ge(comb_spread, k + 1)
                dve.tensor_copy(comb[:, 2 * k:2 * k + 2, :], pair(k % RING)).then_inc(comb_dve, 1)
            dve.wait_ge(comb_act, EXPERTS // 4)
            dve.wait_ge(comb_dve, EXPERTS // 4)
            gated("experts", True)
            norm("ple")
            dve.wait_ge(p_split, 1)
            dve.tensor_tensor(hid_lo[:, :, :], misc[:, :].rearrange("p (a n) -> p a n", a=2),
                              hid_hi[:, :, :].bitcast(f32), SUB).then_inc(p_low, 1)
            c = Chunk(FIRST["ple"][0])
            dve.wait_ge(chunk_used, c.c + 1)
            part(c)

            def add_ple(j, bank, s):
                dve.wait_ge(gate_sig, j + 1)
                dve.wait_ge(drained, j + DRAINED["ple_gate"])
                xs = x[:, :, ds(j * COLS, COLS)]
                link(dve.tensor_tensor(gate_m[:, :, :], gate_s[:, :, :],
                                       acc[:, :, :].rearrange("p (t m) n -> p t (m n)", t=TT)[:, :, ds(j * COLS, COLS)], MUL))
                return dve.tensor_tensor(xs, xs, gate_m[:, :, :], ADD)
            drain("ple_gate", add_ple)
            dve.wait_ge(drained, DRAINED["ple_gate"] + FIRST["ple_gate"][1])
            signal(x_ready)
            dve.wait_ge(late_tables, 16 * LATE_DMAS)
            dve.wait_ge(inv_ready, SQUARED.index("final") + 1)
            for t in range(TT):
                dve.scalar_tensor_tensor(out=x[:, t, :], in0=x[:, t, :], scalar=inv[:, t:t + 1], in1=final_w[:, :],
                                         op0=MUL, op1=MUL).then_inc(scaled_ready, 1)
            dve.wait_ge(scaled_ready, TT * (SQUARED.index("final") + 1))
            signal(x_ready)
            norm("mix0")
            drain_to("a_in0", 0)
            short_conv(0)
            drain_x("a_out0")
            norm("ffn0")
            gated("ffn0")
            norm("mix1")
            drain_to("b_qk", 0)
            drain("b_v", lambda j, bank, s: dve.tensor_copy(v_t[:, :, ds(j * COLS, COLS)], bank))
            link(dve.tensor_scalar(qk_gain[:, 0:1], qk_gain[:, 0:1], HD ** -0.5, None, MUL))
            with dve.Fori(0, PAIRS) as i:
                chain.begin(i, 1)
                dve.wait_ge(qk_root, i + 1)
                link(dve.reciprocal(na_rs[:, :, :], na_rs[:, :, :]))
                for a in range(2):
                    last = dve.scalar_tensor_tensor(out=pj[:, i + a * KT, :], in0=pj[:, i + a * KT, :],
                                                    scalar=qk_gain[:, a:a + 1], in1=na_rs[:, a, :], op0=MUL, op1=MUL)
                last.then_inc(qk_normed, 1)
            chain.end(PAIRS)
            with dve.Fori(0, PAIRS) as i:
                chain.begin(i, 1)
                dve.wait_ge(qk_scored, i + (PAIRS + 1))
                dve.wait_ge(p_turned, i + PAIRS)
                dve.tensor_tensor(probs[:, :, :], acc[:, 1:3, :],
                                  na_mask[:, :].unsqueeze(1).to_broadcast([P, 2, TT * SEQ]), ADD).then_inc(masked, 1)
                softmax_rows(i, PAIRS, False)
            chain.end(PAIRS)
            dve.wait_ge(o_read, 2 * PAIRS)
            signal(h_ready)
            drain_x("na_out")
            norm("ffn1")
            gated("ffn1")
            norm("mix2")
            drain_to("hy_in", 0)
            hyena_vector()
            drain_x("hy_out")
            norm("ffn2")
            gated("ffn2")
            norm("mix3")
            drain_to("a_in1", 0)
            short_conv(1)
            drain_x("a_out1")
            norm("ffn3")
            gated("ffn3")

    return nc


def reduce_angle(dve, link, angle, k):
    ALU = mybir.AluOpType
    link(dve.tensor_scalar(k, angle, 1.0 / (2 * math.pi), ROUND, ALU.mult, ALU.add))
    link(dve.tensor_scalar(k, k, -ROUND, None, ALU.add))
    for part in (TWO_PI_1, TWO_PI_2, TWO_PI_3):
        link(dve.scalar_tensor_tensor(out=angle, in0=k, scalar=-part, in1=angle, op0=ALU.mult, op1=ALU.add))


INPUTS = ["x", "p", "positions", "attn_norm_w", "w_in", "conv_w", "conv_b", "dt_bias", "a_log", "d_skip", "ssd_norm_w",
          "w_ssd_out", "w_attn_out", "w_out", "moe_norm_w", "w_router_group", "b_router_group", "w_router_expert",
          "b_router_expert", "w_exp_gate", "w_exp_up", "w_exp_down", "ple_norm_w", "w_ple", "w_ple_gate",
          "final_norm_w", "norm_mix_g_2", "norm_ffn_g_2", "a_w_in_2", "a_conv_w_2", "a_w_out_2", "b_w_qkv_2",
          "b_q_norm_g_2", "b_k_norm_g_2", "b_rpb_2", "b_w_out_2", "c_w_in_2", "c_short_w_2", "c_short_b_2",
          "c_f_w1_2", "c_f_b1_2", "c_f_w2_2", "c_f_b2_2", "c_f_w3_2", "c_f_freq_2", "c_f_skip_2", "c_w_out_2",
          "f_w13_2", "f_w2_2"]


def kernel(**inputs):
    import numpy as _np
    import concourse.bacc as _bacc
    from concourse import mybir as _mybir
    from concourse.bass_utils import run_bass_kernel_spmd as _run

    nc = _bacc.Bacc("TRN2", target_bir_lowering=False, num_devices=1)
    arrays, views = {}, {}
    for name, a in [(n, _np.asarray(inputs[n])) for n in INPUTS] + list(constants().items()):
        a = _np.ascontiguousarray(a)
        arrays[f"in_{name}_dram"] = a
        views[name] = nc.dram_tensor(f"in_{name}_dram", a.shape, _mybir.dt.from_np(a.dtype), kind="ExternalInput").ap()
    out = nc.dram_tensor("out_0_dram", (1, SEQ, D), _mybir.dt.float32, kind="ExternalOutput").ap()
    build(nc, views, out)
    r = _run(nc, [arrays], core_ids=[0])
    return r.results[0]["out_0_dram"]
```

```python
import math
from contextlib import ExitStack

import numpy as np
import concourse.bass as bass
from concourse import mybir

P = 128
SEQ, D = 256, 1024
TT = SEQ // P
KT = D // P
COLS = 256
RING = 3
POOL_SLOT = 0
CHUNK = KT * COLS
HEADS, HD = 16, 64
PAIRS = HEADS // 2
SSD_GROUPS, SSD_STATE, SSD_TAPS = 2, 64, 4
SSD_INNER = HEADS * HD
SSD_CHANNELS = SSD_INNER + 2 * SSD_GROUPS * SSD_STATE
XBC_TILES = SSD_CHANNELS // P
DT_COL = SSD_INNER + SSD_CHANNELS
MIXER_DMAS = 11
N_GROUPS, GROUP_EXPERTS = 4, 8
EXPERTS = N_GROUPS * GROUP_EXPERTS
D_EXPERT = 256
FFN = ((8 * D + 3 * 256 - 1) // (3 * 256)) * 256
LAYERS = 4
HALF = 512
GRID_W, NA_ROWS, NA_COLS = 64, 8, 16
ORDER, BANDS, EMB, HIDDEN = 2, 16, 33, 64
EPS = 1e-6
NEG = -1e30
CREDIT = 1
TRI = P + SEQ

MLP_CHUNKS = 3 * (FFN // COLS)
STREAM = [("in_zx", 9), ("in_qk", 8), ("in_v", 4), ("in_g", 8), ("ssd_out", 4), ("attn_out", 4), ("mix_out", 4), ("experts", 3 * EXPERTS),
          ("ple", 1), ("ple_gate", 4),
          ("a_in0", 12), ("a_out0", 4), ("ffn0", MLP_CHUNKS),
          ("b_qk", 8), ("b_v", 4), ("na_out", 4), ("ffn1", MLP_CHUNKS),
          ("hy_v", 4), ("hy_x1", 4), ("hy_x2", 4), ("hy_out", 4), ("ffn2", MLP_CHUNKS),
          ("a_in1", 12), ("a_out1", 4), ("ffn3", MLP_CHUNKS)]
FIRST = {}
_c = 0
for _name, _n in STREAM:
    FIRST[_name] = (_c, _n)
    _c += _n
TOTAL = _c
BANKED = [n for n, _ in STREAM if n not in ("experts", "ple") and not n.startswith("ffn")]
DRAINED = {}
_c = 0
for _name in BANKED:
    DRAINED[_name] = _c
    _c += dict(STREAM)[_name]
LATE_DMAS, ROUTER_DMAS, HYENA_DMAS = 9, 5, 10
X_STATES = ["input", "mix_out", "experts", "ple", "final", "a_out0", "ffn0", "na_out", "ffn1", "hy_out",
            "ffn2", "a_out1", "ffn3"]
OPERANDS = ["attn", "ssd", "attention", "merged", "moe", "ple", "mix0", "conv0", "ffn0", "mix1", "na",
            "ffn1", "mix2", "hyena", "ffn2", "mix3", "conv1", "ffn3"]
NORMS = [("attn", "input", "attn_norm_w", 0), ("moe", "mix_out", "moe_norm_w", 0),
         ("ple", "experts", "ple_norm_w", 0)]
for _i, _a, _b in ((0, "final", "a_out0"), (1, "ffn0", "na_out"), (2, "ffn1", "hy_out"), (3, "ffn2", "a_out1")):
    NORMS += [(f"mix{_i}", _a, "norm_mix_g_2", 8 * _i), (f"ffn{_i}", _b, "norm_ffn_g_2", 8 * _i)]
NORM_OF = {_o: _k for _k, (_o, *_r) in enumerate(NORMS)}
SQUARED = [_o for _o, *_r in NORMS]
SQUARED.insert(3, "final")
ROUNDS = {"experts": 0}
for _i in range(LAYERS):
    ROUNDS[f"ffn{_i}"] = EXPERTS + _i * (FFN // COLS)

PARAMS = [("attn_norm_w", 8), ("moe_norm_w", 8), ("ple_norm_w", 8), ("ssd_norm_w", 8),
          ("conv_w", 40), ("conv_b", 10), ("norm_mix_g_2", 32), ("norm_ffn_g_2", 32),
          ("a_conv_w_2", 48), ("c_short_w_2", 72), ("c_short_b_2", 24), ("c_f_skip_2", 16)]
ROW = {}
_c = 0
for _name, _n in PARAMS:
    ROW[_name] = _c
    _c += _n
PARAM_ROWS = _c
PARAM_TILES = -(-PARAM_ROWS // P)


TWO_PI_1 = 6.28125
TWO_PI_2 = float(np.float32(np.round((2 * math.pi - TWO_PI_1) * 2 ** 20) / 2 ** 20))
TWO_PI_3 = float(np.float32(2 * math.pi - TWO_PI_1 - TWO_PI_2))
ROUND = 1.5 * 2 ** 23


def constants():
    f32 = np.float32
    c = {}
    c["ident"] = np.eye(P, dtype=f32)
    tri = np.zeros((P, TT, SEQ), f32)
    for t in range(TT):
        tri[:, t] = (np.arange(P)[:, None] + P * t) <= np.arange(SEQ)[None]
    c["tri"] = tri.reshape(P, TT * SEQ)
    q = np.arange(P)[:, None]
    c["causal"] = np.concatenate([np.where(np.arange(P)[None] <= q, 0, NEG),
                                  np.where(np.arange(SEQ)[None] <= q + P, 0, NEG)], 1).astype(f32)
    half = HD // 2
    rot = np.zeros((P, P), f32)
    for m in range(P):
        if m % HD < half:
            rot[m + half, m] = -1
        else:
            rot[m - half, m] = 1
    c["rot"] = rot
    inv = f32(10000.0) ** (-np.arange(half, dtype=f32) / f32(half))
    c["inv_freq"] = np.tile(inv, P // half).reshape(P, 1).astype(f32)
    c["diag16"] = np.eye(HEADS, dtype=f32)
    c["iota8"] = np.tile(np.arange(8, dtype=f32), (P, 1))
    c["headones"] = np.kron(np.eye(2, dtype=f32), np.ones((HD, HD), f32))
    c["flip"] = np.kron(np.eye(2, dtype=f32), np.eye(GRID_W, dtype=f32)[::-1])
    col = np.arange(SEQ) % GRID_W
    start = np.clip(col - NA_COLS // 2, 0, GRID_W - NA_COLS)
    ok = (col[None] >= start[:, None]) & (col[None] < start[:, None] + NA_COLS)
    c["na_mask"] = np.where(ok, 0, NEG).astype(f32).reshape(TT, P, SEQ).transpose(1, 0, 2).reshape(P, -1)
    t = np.linspace(0.0, 1.0, SEQ, dtype=f32)[:, None]
    bands = np.linspace(1e-4, BANDS - 1, BANDS, dtype=f32)
    ang = (f32(2.0 * math.pi) * np.arange(SEQ, dtype=f32)[:, None] / f32(SEQ) * bands).astype(f32)
    z = np.concatenate([t, np.cos(ang), -np.sin(ang)], -1).astype(f32)
    c["embed"] = np.ascontiguousarray(z.T)
    lt = math.log(1e-2)
    deltas = np.abs(np.linspace(lt / 1.5, lt / 0.3, D, dtype=f32))
    c["decay"] = np.exp(-t * deltas).astype(f32)
    n = 2 * SEQ
    tt = np.arange(SEQ)[:, None]
    f = np.arange(SEQ)[None]
    cos, sin = np.cos(2 * np.pi * tt * f / n), -np.sin(2 * np.pi * tt * f / n)
    nyq = np.cos(np.pi * np.arange(SEQ))
    sinn = sin.copy()
    sinn[:, 0] = nyq
    cosn = cos.copy()
    cosn[:, 0] = nyq
    c["dft"] = np.concatenate([cos, sinn, sin, cosn[:, :P]], 1).astype(f32)
    w = np.full(SEQ, 2.0)
    w[0] = 1.0
    icos = (w[:, None] * np.cos(2 * np.pi * f.T * tt.T / n)) / n
    isin = (-w[:, None] * np.sin(2 * np.pi * f.T * tt.T / n)) / n
    isin[0] = nyq / n
    c["idft"] = np.concatenate([icos, isin], 0).astype(f32)
    return c


class Chunk:

    def __init__(self, number, group=0):
        self.c = group * RING + number
        self.slot = number % RING
        self.turn = group + number // RING
        self.first = number < RING and isinstance(group, int)
        self.more = not (isinstance(group, int) and number + RING * group + RING >= TOTAL)

    def ahead(self):
        new = Chunk.__new__(Chunk)
        new.c, new.slot, new.turn, new.first, new.more = self.c + RING, self.slot, self.turn + 1, False, True
        return new


def chunks(eng, name):
    c0, n = FIRST[name]
    j = 0
    if c0 == 0:
        for j in range(RING):
            yield j, Chunk(j)
        j = RING
    groups = min(n - j, TOTAL - RING - c0 - j) // RING
    if groups > 1:
        with eng.Fori(0, groups) as g:
            for r in range(RING):
                yield g * RING + (j + r), Chunk(c0 + j + r, g)
        j += groups * RING
    for r in range(j, n):
        yield r, Chunk(c0 + r)


def mlp_rounds(eng, name):
    c0, n = FIRST[name]
    rounds = n // 3 - 1
    peel = 1 if c0 + n == TOTAL else 0
    with eng.Fori(0, rounds - peel) as g:
        yield g, c0 + 2, g
    for i in range(rounds - peel, rounds):
        yield i, c0 + 2 + 3 * i, 0


class Chain:

    def __init__(self, eng, sem):
        self.eng, self.sem, self.count, self.extra = eng, sem, 0, 0

    def link(self, ins):
        self.count += 1
        ins.then_inc(self.sem, 1)
        self.eng.wait_ge(self.sem, self.extra + self.count)

    def begin(self, i, per_round):
        self.start, self.per_round = self.count, per_round
        self.extra = i * per_round

    def end(self, rounds):
        assert self.count - self.start == self.per_round, (self.count - self.start, self.per_round)
        self.count = self.start + rounds * self.per_round
        self.extra = 0


def flat(ap, n):
    dims = " ".join(f"d{i}" for i in range(len(ap.shape)))
    return ap.rearrange(f"{dims} -> ({dims})").rearrange("(r n) -> r n", n=n)


def build(nc, A, out):
    f32, f32r, i32, u32 = mybir.dt.float32, mybir.dt.float32r, mybir.dt.int32, mybir.dt.uint32
    ALU, ACT, AX = mybir.AluOpType, mybir.ActivationFunctionType, mybir.AxisListType
    SUB, ADD, MUL = ALU.subtract, ALU.add, ALU.mult
    ds = bass.ds
    ctx = ExitStack()
    with ctx:
        def sb(name, shape, dt=f32):
            return ctx.enter_context(nc.sbuf_tensor(name, shape, dt))

        def sem(name):
            return ctx.enter_context(nc.semaphore(name))

        raw = [sb(f"raw{i}", [P, CHUNK]) for i in range(RING)]
        w_hi = [sb(f"w_hi{i}", [P, CHUNK], f32r) for i in range(RING)]
        w_lo = [sb(f"w_lo{i}", [P, CHUNK], f32r) for i in range(RING)]
        x = sb("x_res", [P, TT, D])
        h_hi = sb("h_hi", [P, KT, SEQ], f32r)
        h_lo = sb("h_lo", [P, KT, SEQ], f32r)
        ident = sb("ident_sb", [P, P])
        ones = sb("ones", [P, P])
        params = sb("params", [P, PARAM_TILES * P])
        ssq = sb("ssq", [P, TT])
        ms = sb("ms", [P, TT])
        inv = sb("inv", [P, TT])
        neg_half = sb("neg_half", [P, TT])
        eps_col = sb("eps_col", [P, 1])

        work0 = -(-nc.sbuf_base // 32) * 32
        limit = nc.sbuf_usable_end - work0

        def at(name, shape, offset, dt=f32):
            size = int(np.prod(shape[1:])) * 4
            assert offset + size <= limit, (name, offset + size, limit)
            return nc.alloc_sbuf_tensor_at(name, shape, dt, offset=work0 + offset)

        KB = 1024
        x_scaled = at("x_scaled", [P, TT, D], 0)
        param_rows = at("param_rows", [P, PARAM_TILES, P], 8 * KB)
        Z0, XBC0, Q0, GS0, GA0 = 0, 8, 18, 34, 42
        pj = at("pj", [P, 50, SEQ], 0)
        v_t = at("v_t", [P, TT, D], 50 * KB)
        conv = at("conv", [P, 10, SEQ], 58 * KB)
        xs_t = at("xs_t", [P, TT, D], 8 * KB)
        cb = at("cb", [P, SSD_GROUPS, TRI], 68 * KB)
        cum_diag = at("cum_diag", [HEADS, HEADS, SEQ], 71 * KB)
        decay = at("decay_w", [P, 2, TRI], 87 * KB)
        xdt = at("xdt", [P, TT, 2 * HD], 90 * KB)
        tri = at("tri_sb", [P, TT, SEQ], 91 * KB)
        S1 = 93 * KB
        diag16 = at("diag16_sb", [HEADS, HEADS], S1)
        dt_bias = at("dt_bias_sb", [P, HEADS], S1 + 64)
        a_rate = at("a_rate", [P, HEADS], S1 + 128)
        w_dt = at("w_dt", [P, KT, HEADS], S1 + 192)
        dt_x = at("dt_x", [P, TT, HEADS], S1 + 704)
        dt_n = at("dt_n", [P, TT, HEADS], S1 + 832)
        dt_u = at("dt_u", [P, TT, HEADS], S1 + 960)
        dt_w = at("dt_w", [P, TT, HEADS], S1 + 1088)
        dt_l = at("dt_l", [P, TT, HEADS], S1 + 1216)
        dt_r = at("dt_r", [P, TT, HEADS], S1 + 1344)
        dt_t = at("dt_t", [P, TT, HEADS], S1 + 1472)
        dA = at("dA", [P, TT, HEADS], S1 + 1600)
        cum_t = at("cum_t", [P, TT, HEADS], S1 + 1728)
        d_col = at("d_col", [P, PAIRS], S1 + 1856)
        inv_freq = at("inv_freq_sb", [P, 1], S1 + 1888)
        a_log_b = at("a_log_b", [P, HEADS], S1 + 1952)
        cum_f = at("cum_f", [HEADS, SEQ], 95 * KB + 256)
        rot = at("rot_sb", [P, P], 96 * KB + 512)
        causal = at("causal_sb", [P, TRI], 97 * KB)
        cos_f = at("cos_f", [P, SEQ], 98 * KB + 512)
        sin_f = at("sin_f", [P, SEQ], 99 * KB + 512)
        ang = at("ang", [P, SEQ], 100 * KB + 512)
        ang_k = at("ang_k", [P, SEQ], 101 * KB + 512)
        pos_i = at("pos_i", [P, SEQ], 102 * KB + 512, i32)
        y_sum = at("y_sum", [P, SEQ], 103 * KB + 512)
        sq_buf = at("sq_buf", [P, 4, SEQ], 71 * KB)
        ynorm = at("ynorm", [P, 4, SEQ], 75 * KB)
        rstd = at("rstd", [P, SEQ], 79 * KB)
        rope_t = at("rope_t", [P, 2, SEQ], 58 * KB)
        rope_u = at("rope_u", [P, 2, SEQ], 60 * KB)
        qk_st = [at(f"qk_st{u}", [P, 2, SEQ], (62, 87)[u] * KB) for u in range(2)]
        v_st = [at(f"v_st{u}", [P, TT, 2 * HD], (64, 89)[u] * KB) for u in range(2)]
        probs = [at(f"probs{u}", [P, 2, TT * SEQ], (65, 78)[u] * KB) for u in range(2)]
        probs_t = [at(f"probs_t{u}", [P, 2, TT * SEQ], (69, 82)[u] * KB) for u in range(2)]
        at_max = [at(f"at_max{u}", [P, 2, TT], 73 * KB + 96 * u) for u in range(2)]
        at_sum = [at(f"at_sum{u}", [P, 2, TT], 73 * KB + 96 * u + 32) for u in range(2)]
        at_inv = [at(f"at_inv{u}", [P, 2, TT], 73 * KB + 96 * u + 64) for u in range(2)]
        merge_t = at("merge_t", [P, 2, SEQ], 74 * KB)
        na_mask = at("na_mask_sb", [P, TT * SEQ], 76 * KB)
        na_bias = [at(f"na_bias{b}", [P, 2, TT * SEQ], (24 + 4 * b) * KB) for b in range(2)]
        headones = at("headones_sb", [P, P], 86 * KB)
        qk_gain = at("qk_gain", [P, 2], 86 * KB + 512)
        flip = at("flip_sb", [P, P], 91 * KB)
        na_sq = at("na_sq", [P, KT, SEQ], 32 * KB)
        na_rs = [at(f"na_rs{a}", [P, KT, SEQ], (40, 16)[a] * KB) for a in range(2)]
        comb = at("comb", [P, EXPERTS, SEQ], 8 * KB)
        silu_g = at("silu_g", [P, 2 * SEQ], 40 * KB)
        hid = at("hid", [P, 2, SEQ], 42 * KB)
        hid_hi = at("hid_hi", [P, 2, SEQ], 44 * KB, f32r)
        hid_lo = at("hid_lo", [P, 2, SEQ], 46 * KB, f32r)
        R0 = 48 * KB
        NL = N_GROUPS + EXPERTS
        w_route = at("w_route", [P, KT, NL], 105 * KB)
        b_route = at("b_route", [P, NL], 106 * KB + 128)
        logits = at("logits", [P, TT, NL], R0 + 1344)
        g_pad = at("g_pad", [P, TT, 8], R0 + 1664)
        g_top = at("g_top", [P, TT, 8], R0 + 1728)
        g_idx = at("g_idx", [P, TT, 8], R0 + 1792, u32)
        g_idxf = at("g_idxf", [P, TT], R0 + 1856)
        g_hot = at("g_hot", [P, TT, N_GROUPS], R0 + 1920)
        g_neg = at("g_neg", [P, TT], R0 + 1952)
        g_exp = at("g_exp", [P, TT, N_GROUPS], R0 + 1984)
        g_sum = at("g_sum", [P, TT], R0 + 2016)
        g_w = at("g_w", [P, TT], R0 + 2048)
        e_prod = at("e_prod", [P, TT, EXPERTS], R0 + 2080)
        e_sel = at("e_sel", [P, TT, GROUP_EXPERTS], R0 + 2336)
        e_top = at("e_top", [P, TT, 8], R0 + 2400)
        e_idx = at("e_idx", [P, TT, 8], R0 + 2464, u32)
        e_idxf = at("e_idxf", [P, TT, 2], R0 + 2528)
        e_hot = at("e_hot", [P, TT, 2, 8], R0 + 2592)
        e_gap = at("e_gap", [P, TT], R0 + 2720)
        e_exp = at("e_exp", [P, TT], R0 + 2752)
        e_den = at("e_den", [P, TT], R0 + 2784)
        e_w = at("e_w", [P, TT, 2], R0 + 2816)
        e_wt = at("e_wt", [P, TT, 8], R0 + 2880)
        comb_t = at("comb_t", [P, TT, N_GROUPS, GROUP_EXPERTS], R0 + 3008)
        comb_f = at("comb_f", [EXPERTS, SEQ], R0 + 3264)
        iota8 = at("iota8_sb", [P, 8], 106 * KB + 288)
        p_t = at("p_t", [P, TT, SEQ], R0 + 5 * KB)
        gate_s = at("gate_s", [P, TT, COLS], R0 + 7 * KB)
        gate_m = at("gate_m", [P, TT, COLS], R0 + 9 * KB)
        final_w = at("final_w", [P, D], R0 + 11 * KB)
        cu = at("cu", [P, KT, SEQ], 24 * KB)
        acv = at("acv", [P, KT, SEQ], 32 * KB)
        hc = at("hc", [P, 3 * KT, SEQ], 24 * KB)
        f_w3 = at("f_w3", [HIDDEN, ORDER * 2 * D], 48 * KB)
        dft = at("dft_sb", [P, TT, 3 * SEQ + P], 64 * KB)
        idft = at("idft_sb", [P, 2 * TT, SEQ], 71 * KB)
        f_decay = at("f_decay", [P, TT, D], 75 * KB)
        embed = at("embed_sb", [EMB, SEQ], 83 * KB)
        f_hid = at("f_hid", [HIDDEN, SEQ], 84 * KB)
        f_k = at("f_k", [HIDDEN, SEQ], 85 * KB)
        f_w1 = at("f_w1", [EMB, HIDDEN], 86 * KB)
        f_w2 = at("f_w2", [HIDDEN, HIDDEN], 86 * KB + 256)
        f_b1 = at("f_b1", [HIDDEN, 1], 86 * KB + 512)
        f_b2 = at("f_b2", [HIDDEN, 1], 86 * KB + 544)
        f_freq = at("f_freq", [HIDDEN, 1], 86 * KB + 576)
        f_rev = at("f_rev", [P, TT, HALF], 0)
        f_even = at("f_even", [P, TT, HALF], 4 * KB)
        f_odd = at("f_odd", [P, TT, HALF], 8 * KB)
        hs_re = at("hs_re", [P, TT, HALF], 12 * KB)
        hs_im = at("hs_im", [P, TT, HALF], 16 * KB)
        u_t = at("u_t", [P, TT, HALF], 20 * KB)
        hs_re2 = at("hs_re2", [P, HALF], 88 * KB)
        f_inv = at("f_inv", [P, HALF], 90 * KB)
        u_st = at("u_st", [P, KT // 2, SEQ], 92 * KB)
        ys = at("ys", [P, 2 * TT, HALF], 96 * KB)
        ys_t = at("ys_t", [P, TT, HALF], 104 * KB)
        f_abs = at("f_abs", [P, 2, TT, HALF], 96 * KB)

        proj = ctx.enter_context(nc.psum_tensor("proj", [P, RING, HALF], f32))
        acc = ctx.enter_context(nc.psum_tensor("acc", [P, TT * 2, HALF], f32))
        misc = ctx.enter_context(nc.psum_tensor("misc", [P, HALF], f32))

        scores = [acc[:, 0:2, :], acc[:, 2:4, :]]
        turned_p = [[proj[:, 0, :], proj[:, 1, :]], [proj[:, 2, :], misc[:, :]]]

        def pair(b):
            return pair_of(proj[:, b, :])

        def pair_of(bank):
            return bank.rearrange("p (a n) -> p a n", a=2)

        side = [pair(0), pair_of(misc[:, :])]

        raw_loaded = [sem(f"raw_loaded{i}") for i in range(RING)]
        hi_ready = sem("hi_ready")
        lo_pool, lo_dve = sem("lo_pool"), sem("lo_dve")
        chunk_used = sem("chunk_used")
        drained = sem("drained")
        x_loaded, x_ready = sem("x_loaded"), sem("x_ready")
        ssq_ready, inv_ready, scaled_ready = sem("ssq_ready"), sem("inv_ready"), sem("scaled_ready")
        turned, turned_read, fhi_ready, h_ready = sem("turned"), sem("turned_read"), sem("fhi_ready"), sem("h_ready")
        small = sem("small")
        ident_loaded, params_loaded = sem("ident_loaded"), sem("params_loaded")
        rows_cleared, params_turned, params_ready = sem("rows_cleared"), sem("params_turned"), sem("params_ready")
        act_chain, dve_chain, pool_chain = sem("act_chain"), sem("dve_chain"), sem("pool_chain")
        silu_ready, banks_read, hid_ready = sem("silu_ready"), sem("banks_read"), sem("hid_ready")
        out_stored = sem("out_stored")
        mixer_tables = sem("mixer_tables")
        z_ready, taps_done, conv_first, conv_done, conv_ready = (
            sem("z_ready"), sem("taps_done"), sem("conv_first"), sem("conv_done"), sem("conv_ready"))
        gates_ready, dt_summed, dt_step, dt_exped = sem("gates_ready"), sem("dt_summed"), sem("dt_step"), sem("dt_exped")
        angles, sines, rates, dA_ready, cum_summed, cum_ready = (
            sem("angles"), sem("sines"), sem("rates"), sem("dA_ready"), sem("cum_summed"), sem("cum_ready"))
        xs_turned, xs_read, cb_summed, cb_ready = sem("xs_turned"), sem("xs_read"), sem("cb_summed"), sem("cb_ready")
        cum_spread, gaps_ready, decay_ready, scores_ready = (
            sem("cum_spread"), sem("gaps_ready"), sem("decay_ready"), sem("scores_ready"))
        y_ready, y_read, y_squared, y_ssq, y_root, y_normed = (
            sem("y_ready"), sem("y_read"), sem("y_squared"), sem("y_ssq"), sem("y_root"), sem("y_normed"))
        rotated, roped, qk_scored, masked, max_ready, exped, normed = (
            sem("rotated"), sem("roped"), sem("qk_scored"), sem("masked"), sem("max_ready"), sem("exped"), sem("normed"))
        v_staged, p_turned, pt_act, pt_dve, o_ready, o_hi, o_read = (
            sem("v_staged"), sem("p_turned"), sem("pt_act"), sem("pt_dve"), sem("o_ready"), sem("o_hi"), sem("o_read"))

        router_tables, late_tables = sem("router_tables"), sem("late_tables")
        routed, comb_made, comb_turned, comb_f_ready, comb_spread, comb_act, comb_dve = (
            sem("routed"), sem("comb_made"), sem("comb_turned"), sem("comb_f_ready"), sem("comb_spread"),
            sem("comb_act"), sem("comb_dve"))
        p_low = sem("p_low")
        gaps_e, exp_e = sem("gaps_e"), sem("exp_e")
        p_turned_ple, p_split, gate_sig = sem("p_turned_ple"), sem("p_split"), sem("gate_sig")
        cu_ready, a_first, a_taps = sem("cu_ready"), sem("a_first"), sem("a_taps")
        qk_squared, qk_summed, qk_root, qk_normed = sem("qk_squared"), sem("qk_summed"), sem("qk_root"), sem("qk_normed")
        bias_loaded = [sem(f"bias_loaded{b}") for b in range(2)]
        q_staged = sem("q_staged")
        xdt_ready, y_gated = sem("xdt_ready"), sem("y_gated")
        hyena_tables = sem("hyena_tables")
        f_summed, f_angle, f_sine = sem("f_summed"), sem("f_angle"), sem("f_sine")
        hc_first, hc_taps = sem("hc_first"), sem("hc_taps")
        filt_summed, rev_copied, parity_ready, abs_ready, mag_ready, norm_summed, h_summed, h_scaled = (
            sem("filt_summed"), sem("rev_copied"), sem("parity_ready"), sem("abs_ready"), sem("mag_ready"),
            sem("norm_summed"), sem("h_summed"), sem("h_scaled"))
        u_staged, u_turned, ut_ready, u_summed, ys_ready, y_summed, z_made = (
            sem("u_staged"), sem("u_turned"), sem("ut_ready"), sem("u_summed"), sem("ys_ready"), sem("y_summed"), sem("z_made"))

        credited = [gaps_ready, y_read, roped, pt_act, pt_dve, o_read, qk_root, ys_ready, z_made, o_ready,
                    qk_summed, qk_normed, parity_ready, u_summed, y_summed, y_ready, qk_scored, p_turned, h_summed, abs_ready]

        block = ctx.enter_context(nc.Block())

        SCORE_COLS = {True: ((0, P), (P, SEQ)), False: ((0, SEQ), (SEQ, SEQ))}

        @block.sync
        def _(sp):
            def load(s, src, k):
                if not s.first:
                    if s.slot == POOL_SLOT:
                        sp.wait_ge(lo_pool, s.turn)
                    else:
                        sp.wait_ge(lo_dve, s.turn * (RING - 1) + (s.slot - (RING - 1)))
                dst = raw[s.slot][:, :].rearrange("p (k n) -> p k n", k=k)
                sp.dma_start(dst, src).then_inc(raw_loaded[s.slot], 16)

            def load_cols(name, w, first_col):
                view = w.rearrange("(k p) n -> p k n", p=P)
                for j, s in chunks(sp, name):
                    load(s, view[:, :, ds(j * COLS + first_col, COLS)], KT)

            def load_late_tables():
                sp.wait_ge(drained, DRAINED["mix_out"] + FIRST["mix_out"][1])
                for dst, src in ((p_t[:, :, :], A["p"][0, 0].rearrange("(t p) n -> p t n", p=P)),
                                 (final_w[:, :], A["final_norm_w"].partition_broadcast(P)),
                                 (na_mask[:, :], A["na_mask"]), (headones[:, :], A["headones"]), (flip[:, :], A["flip"]),
                                 (qk_gain[0:HD, 0:1], flat(A["b_q_norm_g_2"], 1)), (qk_gain[HD:P, 0:1], flat(A["b_q_norm_g_2"], 1)),
                                 (qk_gain[0:HD, 1:2], flat(A["b_k_norm_g_2"], 1)), (qk_gain[HD:P, 1:2], flat(A["b_k_norm_g_2"], 1))):
                    sp.dma_start(dst, src, allow_slow_non_contiguous=True).then_inc(late_tables, 16)

            def load_mlp(name, gate, up, down):
                c0, n = FIRST[name]
                load(Chunk(c0), gate(0), KT)
                load(Chunk(c0 + 1), up(0), KT)
                for i, c, g in mlp_rounds(sp, name):
                    load(Chunk(c, g), gate(i + 1), KT)
                    load(Chunk(c + 1, g), up(i + 1), KT)
                    load(Chunk(c + 2, g), down(i), 2)
                load(Chunk(c0 + n - 1), down(n // 3 - 1), 2)

            def load_hyena_tables():
                sp.wait_ge(drained, DRAINED["na_out"] + FIRST["na_out"][1])
                for dst, src in ((f_w3[:, :], A["c_f_w3_2"][0]), (f_w1[:, :], A["c_f_w1_2"][0]), (f_w2[:, :], A["c_f_w2_2"][0]),
                                 (f_b1[:, :], flat(A["c_f_b1_2"], 1)), (f_b2[:, :], flat(A["c_f_b2_2"], 1)),
                                 (f_freq[:, :], flat(A["c_f_freq_2"], 1)), (embed[:, :], A["embed"]),
                                 (dft[:, :, :], A["dft"].rearrange("(t p) n -> p t n", p=P)),
                                 (idft[:, :, :], A["idft"].rearrange("(t p) n -> p t n", p=P)),
                                 (f_decay[:, :, :], A["decay"].rearrange("(t p) n -> p t n", p=P))):
                    sp.dma_start(dst, src, allow_slow_non_contiguous=True).then_inc(hyena_tables, 16)

            def load_ffn(layer):
                w13 = A["f_w13_2"][layer].rearrange("(k p) n -> p k n", p=P)
                w2 = A["f_w2_2"][layer].rearrange("(k p) n -> p k n", p=P)
                load_mlp(f"ffn{layer}", lambda i: w13[:, :, ds(i * COLS, COLS)],
                         lambda i: w13[:, :, ds(i * COLS + FFN, COLS)],
                         lambda i: w2[:, ds(i * 2, 2), :])

            sp.dma_start(x[:, :, :], A["x"][0].rearrange("(t p) n -> p t n", p=P)).then_inc(x_loaded, 16)
            sp.dma_start(ident[:, :], A["ident"]).then_inc(ident_loaded, 16)
            sp.wait_ge(rows_cleared, 1)
            for name, rows in PARAMS:
                src, done = flat(A[name], P), 0
                while done < rows:
                    tile, row = divmod(ROW[name] + done, P)
                    n = min(rows - done, P - row)
                    sp.dma_start(param_rows[row:row + n, tile, :], src[done:done + n, :]).then_inc(params_loaded, 16)
                    done += n
            load_cols("in_zx", A["w_in"][0], 0)
            for dst, src in ((tri[:, :, :], A["tri"].rearrange("p (t n) -> p t n", t=TT)), (diag16[:, :], A["diag16"]),
                             (dt_bias[:, :], A["dt_bias"][0].partition_broadcast(P)),
                             (a_log_b[:, :], A["a_log"][0].partition_broadcast(P)),
                             (w_dt[:, :, :], A["w_in"][0].rearrange("(k p) n -> p k n", p=P)[:, :, DT_COL:DT_COL + HEADS]),
                             (d_col[0:HD, :], A["d_skip"][0].rearrange("(i a) -> a i", a=2)[0].partition_broadcast(HD)),
                             (d_col[HD:P, :], A["d_skip"][0].rearrange("(i a) -> a i", a=2)[1].partition_broadcast(HD)),
                             (inv_freq[:, :], A["inv_freq"]), (rot[:, :], A["rot"]), (causal[:, :], A["causal"]),
                             (pos_i[:, :], A["positions"][0].partition_broadcast(P))):
                sp.dma_start(dst, src, allow_slow_non_contiguous=True).then_inc(mixer_tables, 16)
            for dst, src in ((w_route[:, :, 0:N_GROUPS], A["w_router_group"][0].rearrange("(k p) n -> p k n", p=P)),
                             (w_route[:, :, N_GROUPS:], A["w_router_expert"][0].rearrange("(k p) n -> p k n", p=P)),
                             (b_route[:, 0:N_GROUPS], A["b_router_group"][0].partition_broadcast(P)),
                             (b_route[:, N_GROUPS:], A["b_router_expert"][0].partition_broadcast(P)),
                             (iota8[:, :], A["iota8"])):
                sp.dma_start(dst, src).then_inc(router_tables, 16)
            inner = SSD_INNER + SSD_CHANNELS + HEADS
            load_cols("in_qk", A["w_in"][0], inner)
            load_cols("in_v", A["w_in"][0], inner + 2 * D)
            load_cols("in_g", A["w_in"][0], inner + 3 * D)
            load_cols("ssd_out", A["w_ssd_out"][0], 0)
            load_cols("attn_out", A["w_attn_out"][0], 0)
            load_cols("mix_out", A["w_out"][0], 0)
            by_expert = {n: A[n][0].rearrange("g e (k p) f -> p (g e) k f", p=P)
                         for n in ("w_exp_gate", "w_exp_up", "w_exp_down")}
            load_mlp("experts", *[lambda i, v=v: v[:, ds(i, 1), :, :].rearrange("p e k f -> p (e k) f")
                                  for v in by_expert.values()])
            load_late_tables()
            load(Chunk(FIRST["ple"][0]), A["w_ple"][0].rearrange("(k p) n -> p k n", p=P), 2)
            load_cols("ple_gate", A["w_ple_gate"][0], 0)
            load_cols("a_in0", A["a_w_in_2"][0], 0)
            load_cols("a_out0", A["a_w_out_2"][0], 0)
            load_ffn(0)
            load_cols("b_qk", A["b_w_qkv_2"][0], 0)
            load_cols("b_v", A["b_w_qkv_2"][0], 2 * D)
            load_cols("na_out", A["b_w_out_2"][0], 0)
            rpb = A["b_rpb_2"]
            head, row = (2 * NA_ROWS - 1) * (2 * NA_COLS - 1), 2 * NA_COLS - 1
            with sp.Fori(0, PAIRS // 2) as ii:
                for b in range(2):
                    i = ii * 2 + b
                    sp.wait_ge(qk_scored, i + (PAIRS - 1) + CREDIT)
                    for h in range(2):
                        for r in range(SEQ // GRID_W):
                            t, half = divmod(r, 2)
                            src = bass.AP(rpb.tensor, i * (2 * head) + (h * head + (NA_ROWS - 1 - r) * row + NA_COLS - GRID_W),
                                          [[1, GRID_W], [row, SEQ // GRID_W], [1, GRID_W]])
                            dst = na_bias[b][half * GRID_W:(half + 1) * GRID_W, h, t * SEQ:(t + 1) * SEQ]
                            sp.dma_start(dst.rearrange("p (a b) -> p a b", b=GRID_W), src).then_inc(bias_loaded[b], 16)
            load_ffn(1)
            load_cols("hy_v", A["c_w_in_2"][0], 0)
            load_cols("hy_x1", A["c_w_in_2"][0], D)
            load_hyena_tables()
            load_cols("hy_x2", A["c_w_in_2"][0], 2 * D)
            load_cols("hy_out", A["c_w_out_2"][0], 0)
            load_ffn(2)
            load_cols("a_in1", A["a_w_in_2"][1], 0)
            load_cols("a_out1", A["a_w_out_2"][1], 0)
            load_ffn(3)
            sp.wait_ge(x_ready, len(X_STATES) - 1)
            sp.dma_start(out[0].rearrange("(t p) n -> p t n", p=P), x[:, :, :]).then_inc(out_stored, 16)
            sp.wait_ge(out_stored, 16)

        PARAM_DMAS = sum(len({(ROW[n] + r) // P for r in range(k)}) for n, k in PARAMS)

        @block.tensor
        def _(pe):
            def wait_parts(s):
                if s.slot == POOL_SLOT:
                    pe.wait_ge(lo_pool, s.turn + 1)
                else:
                    pe.wait_ge(lo_dve, s.turn * (RING - 1) + s.slot)

            def product_f(s):
                hi = w_hi[s.slot][:, :].rearrange("p (k n) -> p k n", k=KT)
                lo = w_lo[s.slot][:, :].rearrange("p (k n) -> p k n", k=KT)
                for a in range(2):
                    for k in range(KT):
                        for w, h in ((hi, h_hi), (hi, h_lo), (lo, h_hi)):
                            last = pe.matmul(pair(s.slot)[:, a, :], w[:, k, a * P:(a + 1) * P], h[:, k, :],
                                             start=(k == 0 and w is hi and h is h_hi),
                                             stop=(k == KT - 1 and w is lo))
                last.then_inc(chunk_used, 1)

            def product_t(s):
                hi = w_hi[s.slot][:, :].rearrange("p (k n) -> p k n", k=KT)
                lo = w_lo[s.slot][:, :].rearrange("p (k n) -> p k n", k=KT)
                for t in range(TT):
                    for k in range(KT):
                        for h, w in ((h_hi, hi), (h_hi, lo), (h_lo, hi)):
                            last = pe.matmul(pair(s.slot)[:, t, :], h[:, k, t * P:(t + 1) * P], w[:, k, :],
                                             start=(k == 0 and w is hi and h is h_hi),
                                             stop=(k == KT - 1 and h is h_lo))
                last.then_inc(chunk_used, 1)

            def project(name, product, operand, after=()):
                pe.wait_ge(h_ready, OPERANDS.index(operand) + 1)
                for j, s in chunks(pe, name):
                    wait_parts(s)
                    if isinstance(j, int) and DRAINED[name] + j < RING:
                        pass
                    else:
                        pe.wait_ge(drained, j + (DRAINED[name] - RING + 1))
                    product(s)
                    if j in after:
                        after[j]()

            def norm_turn(operand):
                n = NORM_OF[operand]
                pe.wait_ge(scaled_ready, TT * (SQUARED.index(operand) + 1))
                for kk in range(KT // 2):
                    if kk >= RING:
                        pe.wait_ge(turned_read, n * (KT // 2) + kk - RING + 1)
                    for a in range(2):
                        for t in range(TT):
                            k = 2 * kk + a
                            last = pe.transpose(pair(kk % RING)[:, a, t * P:(t + 1) * P],
                                                x_scaled[:, t, k * P:(k + 1) * P], ident[:, :])
                    last.then_inc(turned, 1)

            def sum_decays():
                pe.wait_ge(dA_ready, 1)
                for t in range(TT):
                    for s in range(t + 1):
                        pe.matmul(misc[:, 64 + t * HEADS:64 + (t + 1) * HEADS], tri[:, s, t * P:(t + 1) * P],
                                  dA[:, s, :], start=(s == 0), stop=(s == t))
                for s in range(TT):
                    last = pe.matmul(misc[0:HEADS, SEQ:2 * SEQ], dA[:, s, :], tri[:, s, :],
                                     start=(s == 0), stop=(s == TT - 1))
                last.then_inc(cum_summed, 1)

            def ssd():
                pe.wait_ge(conv_ready, 1)
                pe.wait_ge(drained, DRAINED["ssd_out"])
                for kk in range(KT // 2):
                    if kk >= RING:
                        pe.wait_ge(xs_read, kk - RING + 1)
                    for t in range(TT):
                        for a in range(2):
                            last = pe.transpose(pair(kk % RING)[:, t, a * P:(a + 1) * P],
                                                conv[:, 2 * kk + a, t * P:(t + 1) * P], ident[:, :])
                    last.then_inc(xs_turned, 1)
                for g in range(SSD_GROUPS):
                    r = slice(g * SSD_STATE, (g + 1) * SSD_STATE)
                    pe.matmul(acc[:, g, 0:SEQ], conv[r, 8, 0:P], conv[r, 9, :], start=True, stop=True)
                    last = pe.matmul(acc[:, g, SEQ:TRI], conv[r, 8, P:SEQ], conv[r, 9, P:SEQ], start=True, stop=True)
                last.then_inc(cb_summed, 1)
                pe.wait_ge(cum_ready, 1)
                for g in range(SSD_GROUPS):
                    with pe.Fori(0, PAIRS // SSD_GROUPS) as ii:
                        i = ii + g * (PAIRS // SSD_GROUPS)
                        pe.wait_ge(gaps_ready, i + CREDIT)
                        for h in range(2):
                            last = pe.matmul(acc[:, 2, h * SEQ:(h + 1) * SEQ], ones[0:HEADS, :],
                                             cum_diag[:, 2 * i + h, :], start=True, stop=True)
                        last.then_inc(cum_spread, 1)
                        pe.wait_ge(scores_ready, i + 1)
                        pe.wait_ge(y_read, i + CREDIT)
                        for h in range(2):
                            o = acc[h * HD:(h + 1) * HD, 3, :]
                            pe.matmul(o[:, 0:SEQ], xdt[:, 0, h * HD:(h + 1) * HD], decay[:, h, 0:SEQ],
                                      start=True, stop=False)
                            last = pe.matmul(o[:, P:SEQ], xdt[:, 1, h * HD:(h + 1) * HD], decay[:, h, SEQ:TRI],
                                             start=False, stop=True)
                        last.then_inc(y_ready, 1)
                for g in range(SSD_GROUPS):
                    pe.wait_ge(y_squared, g + 1)
                    for a in range(4):
                        last = pe.matmul(acc[:, g, 0:SEQ], ones[:, :], sq_buf[:, a, :], start=(a == 0), stop=(a == 3))
                    last.then_inc(y_ssq, 1)

            def attention():
                pe.wait_ge(drained, DRAINED["attn_out"])
                with pe.Fori(0, PAIRS // 2) as ii:
                    for u in range(2):
                        i = ii * 2 + u
                        pe.wait_ge(pt_act, ii * 2 + CREDIT)
                        for a in range(2):
                            last = pe.matmul(turned_p[u][0][:, a * SEQ:(a + 1) * SEQ], rot[:, :],
                                             pj[:, i + (Q0 + a * KT), :], start=True, stop=True)
                        last.then_inc(rotated, 1)
                    for u in range(2):
                        i = ii * 2 + u
                        pe.wait_ge(roped, i + 1 + CREDIT)
                        pe.wait_ge(o_read, ii * 2 + CREDIT)
                        for h in range(2):
                            r = slice(h * HD, (h + 1) * HD)
                            for t, (c, n) in enumerate(SCORE_COLS[True]):
                                last = pe.matmul(scores[u][:, h, c:c + n], qk_st[u][r, 0, t * P:(t + 1) * P],
                                                 qk_st[u][r, 1, 0:n], start=True, stop=True)
                        last.then_inc(qk_scored, 1)
                    attention_out(ii, 0, True)

            def attention_out(ii, base, causal_):
                for u in range(2):
                    i = ii * 2 + u
                    pe.wait_ge(normed, i + (base + 1))
                    if not causal_:
                        pe.wait_ge(pt_act, ii * 2 + base + CREDIT)
                        pe.wait_ge(pt_dve, ii * 2 + base + CREDIT)
                    elif u == 0:
                        pe.wait_ge(pt_dve, ii * 2 + base + CREDIT)
                    for h in range(2):
                        for t, (c, n) in enumerate(SCORE_COLS[causal_]):
                            for kt in range(n // P):
                                to = t * P if kt == 0 else SEQ + (t * P if not causal_ else 0)
                                last = pe.transpose(turned_p[u][h][:, to:to + P],
                                                    probs[u][:, h, c + kt * P:c + (kt + 1) * P], ident[:, :])
                    last.then_inc(p_turned, 1)
                for u in range(2):
                    i = ii * 2 + u
                    pe.wait_ge(pt_act, i + (base + 1) + CREDIT)
                    pe.wait_ge(pt_dve, i + (base + 1) + CREDIT)
                    pe.wait_ge(v_staged, i + (base + 1))
                    for h in range(2):
                        o = scores[u][h * HD:(h + 1) * HD, 0, :]
                        pe.matmul(o[:, 0:SEQ], v_st[u][:, 0, h * HD:(h + 1) * HD], probs_t[u][:, h, 0:SEQ],
                                  start=True, stop=False)
                        q0 = P if causal_ else 0
                        last = pe.matmul(o[:, q0:SEQ], v_st[u][:, 1, h * HD:(h + 1) * HD],
                                         probs_t[u][:, h, SEQ:2 * SEQ - q0], start=False, stop=True)
                    last.then_inc(o_ready, 1)

            def down(s, start, stop):
                hi = w_hi[s.slot][:, :].rearrange("p (k n) -> p k n", k=2)
                lo = w_lo[s.slot][:, :].rearrange("p (k n) -> p k n", k=2)
                for k in range(2):
                    for t in range(TT):
                        for h, w in ((hid_hi, hi), (hid_hi, lo), (hid_lo, hi)):
                            for m in range(2):
                                last = pe.matmul(acc[:, 2 * t + m, :], h[:, k, t * P:(t + 1) * P],
                                                 w[:, k, m * HALF:(m + 1) * HALF],
                                                 start=(start and k == 0 and h is hid_hi and w is hi),
                                                 stop=(stop and k == 1 and h is hid_lo), skip_group_check=True)
                last.then_inc(chunk_used, 1)

            def mlp(name, operand, before=None):
                c0, n = FIRST[name]
                base = ROUNDS[name]
                pe.wait_ge(h_ready, OPERANDS.index(operand) + 1)
                if before:
                    before()
                for t in range(TT):
                    for m in range(2):
                        pe.matmul(acc[:, 2 * t + m, :], ident[:, :], x[:, t, m * HALF:(m + 1) * HALF],
                                  start=True, stop=False, skip_group_check=True)
                for r in range(2):
                    wait_parts(Chunk(c0 + r))
                    product_f(Chunk(c0 + r))
                for i, c, g in mlp_rounds(pe, name):
                    wait_parts(Chunk(c, g))
                    pe.wait_ge(banks_read, i + (base + 1))
                    product_f(Chunk(c, g))
                    wait_parts(Chunk(c + 1, g))
                    product_f(Chunk(c + 1, g))
                    wait_parts(Chunk(c + 2, g))
                    pe.wait_ge(hid_ready, i + (base + 1))
                    down(Chunk(c + 2, g), False, False)
                wait_parts(Chunk(c0 + n - 1))
                pe.wait_ge(hid_ready, base + n // 3)
                down(Chunk(c0 + n - 1), False, True)

            def route():
                pe.wait_ge(router_tables, 16 * ROUTER_DMAS)
                for t in range(TT):
                    for k in range(KT):
                        for h in (h_hi, h_lo):
                            last = pe.matmul(misc[:, t * NL:(t + 1) * NL], h[:, k, t * P:(t + 1) * P].bitcast(f32),
                                             w_route[:, k, :], start=(k == 0 and h is h_hi),
                                             stop=(k == KT - 1 and h is h_lo))
                last.then_inc(routed, 1)
                pe.wait_ge(comb_made, 1)
                for t in range(TT):
                    last = pe.transpose(misc[0:EXPERTS, SEQ + t * P:SEQ + (t + 1) * P],
                                        comb_t[:, t, :, :].rearrange("p g e -> p (g e)"), ident[:, :])
                last.then_inc(comb_turned, 1)
                pe.wait_ge(comb_f_ready, 1)
                for k in range(EXPERTS // 2):
                    if k >= RING:
                        pe.wait_ge(comb_dve if (k - RING) % 2 else comb_act, (k - RING) // 2 + 1)
                    for a in range(2):
                        e = 2 * k + a
                        last = pe.matmul(pair(k % RING)[:, a, :], ident[0:EXPERTS, e:e + 1].to_broadcast([EXPERTS, P]),
                                         comb_f[:, :], start=True, stop=True)
                    last.then_inc(comb_spread, 1)
                pe.wait_ge(comb_act, EXPERTS // 4)
                pe.wait_ge(comb_dve, EXPERTS // 4)

            def sum_squares(a):
                pe.wait_ge(late_tables, 16 * LATE_DMAS)
                pe.wait_ge(qk_squared, a + 1)
                pe.wait_ge(qk_root, a + CREDIT)
                for m in range(KT // 2):
                    last = pe.matmul(acc[:, m, :], headones[:, :], na_sq[:, 2 * m:2 * m + 2, :], start=True, stop=True)
                last.then_inc(qk_summed, 1)

            def na_attention():
                pe.wait_ge(drained, DRAINED["na_out"])
                pe.wait_ge(qk_root, 2 + CREDIT)
                with pe.Fori(0, PAIRS // 2) as ii:
                    for u in range(2):
                        i = ii * 2 + u
                        pe.wait_ge(q_staged, i + 1)
                        pe.wait_ge(o_read, ii * 2 + PAIRS + CREDIT)
                        pe.wait_ge(bias_loaded[u], ii * (8 * 16) + 8 * 16)
                        for h in range(2):
                            r = slice(h * HD, (h + 1) * HD)
                            for t in range(TT):
                                o = scores[u][:, h, t * SEQ:(t + 1) * SEQ]
                                pe.matmul(o, qk_st[u][r, 0, t * P:(t + 1) * P], qk_st[u][r, 1, :], start=True, stop=False)
                                last = pe.matmul(o, flip[:, :], na_bias[u][:, h, t * SEQ:(t + 1) * SEQ],
                                                 start=False, stop=True)
                        last.then_inc(qk_scored, 1)
                    attention_out(ii, PAIRS, False)

            def filter_layer(layer):
                if layer == 0:
                    pe.wait_ge(hyena_tables, 16 * HYENA_DMAS)
                    pe.matmul(misc[0:HIDDEN, 0:SEQ], f_w1[:, :], embed[:, :], start=True, stop=True).then_inc(f_summed, 1)
                else:
                    pe.wait_ge(f_sine, 1)
                    pe.matmul(misc[0:HIDDEN, SEQ:2 * SEQ], f_w2[:, :], f_hid[:, :], start=True, stop=True).then_inc(f_summed, 1)

            def hyena():
                pe.wait_ge(f_sine, 2)
                pe.wait_ge(drained, DRAINED["hy_out"])
                with pe.Fori(0, D // HALF) as half:
                    for n in range(ORDER):
                        b = half * ORDER + n
                        for v in range(2):
                            pe.wait_ge(ys_ready, b * 2 + CREDIT)
                            for way in range(2):
                                for t in range(TT):
                                    last = pe.matmul(pair_of(acc[:, 2 * v + way, :])[:, t, :], f_hid[:, t * P:(t + 1) * P],
                                                     f_w3[:, ds(half * HALF + (2 * n + way) * D + v * COLS, COLS)],
                                                     start=True, stop=True)
                            last.then_inc(filt_summed, 1)
                        for v in range(2):
                            pe.wait_ge(u_staged, half + 1)
                            pe.wait_ge(z_made, b * 2 + CREDIT)
                            for t in range(TT):
                                for m in range(2):
                                    last = pe.transpose(pair(1 + v)[:, t, m * P:(m + 1) * P],
                                                        u_st[:, 2 * v + m, t * P:(t + 1) * P], ident[:, :])
                            last.then_inc(u_turned, 1)
                        for v in range(2):
                            cols = slice(v * COLS, (v + 1) * COLS)
                            pe.wait_ge(parity_ready, b * 2 + (v + 1) + CREDIT)
                            for bank, part_, first in [(pair_of(acc[:, 2 * v, :])[:, f, :], f_even, f * P) for f in range(TT)] + \
                                    [(pair_of(acc[:, 2 * v + 1, :])[:, f, :], f_odd, 2 * SEQ + f * P) for f in range(TT)] + \
                                    [(side[v][:, 0, :], f_even, 3 * SEQ)]:
                                for t in range(TT):
                                    last = pe.matmul(bank, dft[:, t, first:first + P], part_[:, t, cols], start=(t == 0), stop=(t == 1))
                            last.then_inc(h_summed, 1)
                        for v in range(2):
                            pe.wait_ge(mag_ready, b * 2 + (v + 1))
                            for t in range(TT):
                                last = pe.matmul(side[v][:, 1, :], ones[:, :], f_abs[:, 0, t, v * COLS:(v + 1) * COLS],
                                                 start=(t == 0), stop=(t == 1))
                            last.then_inc(norm_summed, 1)
                        for v in range(2):
                            pe.wait_ge(ut_ready, b * 2 + (v + 1))
                            pe.wait_ge(h_scaled, b * 2 + (v + 1))
                            for f in range(2 * TT):
                                for t in range(TT):
                                    last = pe.matmul(pair_of(acc[:, 2 * v + f // 2, :])[:, f % 2, :], dft[:, t, f * P:(f + 1) * P],
                                                     u_t[:, t, v * COLS:(v + 1) * COLS], start=(t == 0), stop=(t == 1))
                            last.then_inc(u_summed, 1)
                        for v in range(2):
                            pe.wait_ge(ys_ready, b * 2 + (v + 1) + CREDIT)
                            for m in range(2):
                                for f in range(2 * TT):
                                    last = pe.matmul(pair(1 + v)[:, m, :], ys[:, f, (2 * v + m) * P:(2 * v + m + 1) * P],
                                                     idft[:, f, :], start=(f == 0), stop=(f == 2 * TT - 1))
                            last.then_inc(y_summed, 1)
                pe.wait_ge(z_made, 4 * ORDER + CREDIT)

            pe.wait_ge(params_loaded, 16 * PARAM_DMAS)
            pe.wait_ge(ident_loaded, 16)
            for i in range(PARAM_TILES):
                last = pe.transpose(misc[:, i * P:(i + 1) * P], param_rows[:, i, :], ident[:, :])
            last.then_inc(params_turned, 1)
            norm_turn("attn")
            project("in_zx", product_f, "attn")
            project("in_qk", product_f, "attn")
            pe.wait_ge(mixer_tables, MIXER_DMAS * 16)
            pe.wait_ge(params_ready, 1)
            for t in range(TT):
                for k in range(KT):
                    for h in (h_hi, h_lo):
                        last = pe.matmul(misc[:, t * HEADS:(t + 1) * HEADS],
                                         h[:, k, t * P:(t + 1) * P].bitcast(f32), w_dt[:, k, :],
                                         start=(k == 0 and h is h_hi), stop=(k == KT - 1 and h is h_lo))
            last.then_inc(dt_summed, 1)
            project("in_v", product_t, "attn")
            sum_decays()
            project("in_g", product_f, "attn")
            ssd()
            project("ssd_out", product_f, "ssd")
            attention()
            project("attn_out", product_f, "attention")
            project("mix_out", product_t, "merged")
            norm_turn("moe")
            mlp("experts", "moe", route)
            norm_turn("ple")
            pe.wait_ge(late_tables, 16 * LATE_DMAS)
            for a in range(2):
                for t in range(TT):
                    last = pe.transpose(misc[:, a * SEQ + t * P:a * SEQ + (t + 1) * P],
                                        p_t[:, t, a * P:(a + 1) * P], ident[:, :])
            last.then_inc(p_turned_ple, 1)
            s = Chunk(FIRST["ple"][0])
            wait_parts(s)
            pe.wait_ge(p_low, 1)
            down(s, True, True)
            project("ple_gate", product_t, "ple")
            norm_turn("mix0")
            project("a_in0", product_f, "mix0")
            project("a_out0", product_t, "conv0")
            norm_turn("ffn0")
            mlp("ffn0", "ffn0")
            norm_turn("mix1")
            project("b_qk", product_f, "mix1")
            project("b_v", product_t, "mix1", {0: lambda: sum_squares(0), 1: lambda: sum_squares(1)})
            na_attention()
            project("na_out", product_t, "na")
            norm_turn("ffn1")
            mlp("ffn1", "ffn1")
            norm_turn("mix2")
            project("hy_v", product_f, "mix2")
            project("hy_x1", product_f, "mix2")
            project("hy_x2", product_f, "mix2", {0: lambda: filter_layer(0), 2: lambda: filter_layer(1)})
            hyena()
            project("hy_out", product_t, "hyena")
            norm_turn("ffn2")
            mlp("ffn2", "ffn2")
            norm_turn("mix3")
            project("a_in1", product_f, "mix3")
            project("a_out1", product_t, "conv1")
            norm_turn("ffn3")
            mlp("ffn3", "ffn3")

        @block.gpsimd
        def _(pool):
            chain = Chain(pool, pool_chain)

            def part(s):
                if s.more and s.slot == POOL_SLOT:
                    low(s.ahead())

            def low(n):
                pool.wait_ge(hi_ready, n.c + 1)
                pool.tensor_tensor(w_lo[n.slot][:, :], raw[n.slot][:, :], w_hi[n.slot][:, :].bitcast(f32), SUB)\
                    .then_inc(lo_pool, 1)

            def parts(name):
                for j, s in chunks(pool, name):
                    part(s)

            def parts_mlp(name):
                c0, n = FIRST[name]
                part(Chunk(c0))
                part(Chunk(c0 + 1))
                for i, c, g in mlp_rounds(pool, name):
                    for r in range(3):
                        part(Chunk(c + r, g))
                part(Chunk(c0 + n - 1))

            def norm_root(operand):
                n = SQUARED.index(operand)
                pool.wait_ge(ssq_ready, TT * (n + 1))
                if n:
                    pool.wait_ge(scaled_ready, TT * n)
                chain.link(pool.tensor_scalar(ms[:, :], ssq[:, :], 1.0 / D, EPS, MUL, ADD))
                pool.tensor_tensor(inv[:, :], ms[:, :], neg_half[:, :], ALU.pow).then_inc(inv_ready, 1)

            pool.memset(param_rows[:, :, :], 0.0).then_inc(rows_cleared, 1)
            for s in credited:
                pool.sem_inc(s, CREDIT)
            pool.memset(neg_half[:, :], -0.5).then_inc(small, 1)
            pool.memset(ones[:, :], 1.0).then_inc(small, 1)
            pool.memset(eps_col[:, :], EPS).then_inc(small, 1)
            pool.wait_ge(small, 3)
            low(Chunk(POOL_SLOT))
            norm_root("attn")
            parts("in_zx")
            parts("in_qk")
            parts("in_v")
            parts("in_g")
            parts("ssd_out")
            parts("attn_out")
            parts("mix_out")
            norm_root("moe")
            parts_mlp("experts")
            norm_root("ple")
            parts("ple")
            parts("ple_gate")
            norm_root("final")
            norm_root("mix0")
            parts("a_in0")
            parts("a_out0")
            norm_root("ffn0")
            parts_mlp("ffn0")
            norm_root("mix1")
            parts("b_qk")
            parts("b_v")
            parts("na_out")
            norm_root("ffn1")
            parts_mlp("ffn1")
            norm_root("mix2")
            parts("hy_v")
            parts("hy_x1")
            parts("hy_x2")
            parts("hy_out")
            norm_root("ffn2")
            parts_mlp("ffn2")
            norm_root("mix3")
            parts("a_in1")
            parts("a_out1")
            norm_root("ffn3")
            parts_mlp("ffn3")

        @block.scalar
        def _(act):
            def part(s):
                if s.more:
                    act.wait_ge(chunk_used, s.c + 1)
                    high(s.ahead())

            def high(n):
                act.wait_ge(raw_loaded[n.slot], (n.turn + 1) * 16)
                act.activation(w_hi[n.slot][:, :], raw[n.slot][:, :], ACT.Copy).then_inc(hi_ready, 1)

            def parts(name, after=()):
                for j, s in chunks(act, name):
                    part(s)
                    if j in after:
                        after[j]()

            def norm(operand):
                n = NORM_OF[operand]
                state, gain, row = X_STATES.index(NORMS[n][1]), NORMS[n][2], NORMS[n][3]
                squares(SQUARED.index(operand), state)
                for kk in range(KT // 2):
                    act.wait_ge(turned, n * (KT // 2) + kk + 1)
                    for a in range(2):
                        col = ROW[gain] + row + 2 * kk + a
                        act.activation(h_hi[:, 2 * kk + a, :], pair(kk % RING)[:, a, :], ACT.Copy,
                                       scale=params[:, col:col + 1]).then_inc(fhi_ready, 1)

            def squares(n, state):
                if state == 0:
                    act.wait_ge(x_loaded, 16)
                else:
                    act.wait_ge(x_ready, state)
                if n:
                    act.wait_ge(inv_ready, n)
                for t in range(TT):
                    if t or n:
                        act.wait_ge(ssq_ready, TT * n + t)
                    act.activation(x_scaled[:, t, :], x[:, t, :], ACT.Square, accum_out=ssq[:, t:t + 1])\
                        .then_inc(ssq_ready, 1)

            def softmax_exp(ii, base, causal_):
                for u in range(2):
                    act.wait_ge(max_ready, ii * 2 + (base + u + 1))
                    for h in range(2):
                        for t, (c, n) in enumerate(SCORE_COLS[causal_]):
                            act.activation(probs[u][:, h, c:c + n], probs[u][:, h, c:c + n], ACT.Exp,
                                           bias=at_max[u][:, h, t:t + 1], accum_out=at_sum[u][:, h, t:t + 1]).then_inc(exped, 1)
                n = TRI if causal_ else 2 * SEQ
                for u in range(2):
                    act.wait_ge(p_turned, ii * 2 + (base + u + 1) + CREDIT)
                    act.activation(probs_t[u][:, 0, 0:n], turned_p[u][0][:, 0:n], ACT.Copy).then_inc(pt_act, 1)
                for u in range(2):
                    act.wait_ge(o_ready, ii * 2 + (base + u + 1) + CREDIT)
                    act.activation(h_hi[:, ii * 2 + u, :], scores[u][:, 0, 0:SEQ], ACT.Copy).then_inc(o_hi, 1)

            def stage_v(ii, u, base):
                act.wait_ge(o_ready, ii * 2 + base + CREDIT)
                act.activation(v_st[u][:, :, :], v_t[:, :, ds((ii * 2 + u) * P, P)], ACT.Copy).then_inc(v_staged, 1)

            def silu_gate(base, i, c):
                act.wait_ge(chunk_used, c.c + 1)
                if not (isinstance(i, int) and base + i == 0):
                    act.wait_ge(banks_read, i + base)
                act.activation(silu_g[:, :], proj[:, c.slot, :], ACT.Silu).then_inc(silu_ready, 1)

            def parts_mlp(name):
                c0, n = FIRST[name]
                base = ROUNDS[name]
                silu_gate(base, 0, Chunk(c0))
                part(Chunk(c0))
                part(Chunk(c0 + 1))
                for i, c, g in mlp_rounds(act, name):
                    silu_gate(base, i + 1, Chunk(c, g))
                    for r in range(3):
                        part(Chunk(c + r, g))
                part(Chunk(c0 + n - 1))

            def short_conv(layer):
                act.wait_ge(cu_ready, layer + 1)
                for m in range(KT):
                    col = ROW["a_conv_w_2"] + (layer * 3 + 1) * KT + m
                    act.activation(acv[:, m, :], cu[:, m, :], ACT.Copy, scale=params[:, col:col + 1]).then_inc(a_first, 1)

            def hyena_tap(group):
                act.wait_ge(drained, DRAINED[("hy_x1", "hy_x2", "hy_out")[group]])
                w, b0 = ROW["c_short_w_2"] + 3 * KT, ROW["c_short_b_2"]
                with act.Fori(group * KT, (group + 1) * KT) as m:
                    act.activation(hc[:, ds(m, 1), :].rearrange("p o n -> p (o n)"),
                                   pj[:, ds(m, 1), :].rearrange("p o n -> p (o n)"), ACT.Identity,
                                   bias=params[:, ds(m + b0, 1)], scale=params[:, ds(m + w, 1)]).then_inc(hc_first, 1)

            def filter_sine(layer):
                act.wait_ge(f_angle, layer + 1)
                act.activation(f_hid[:, :], f_hid[:, :], ACT.Sin).then_inc(f_sine, 1)

            def hyena_scalar():
                act.wait_ge(hc_taps, 6 * KT)
                with act.Fori(0, D // HALF) as half:
                    for n in range(ORDER):
                        b = half * ORDER + n
                        if n == 0:
                            act.wait_ge(z_made, b * 2 + CREDIT)
                            act.activation(u_st[:, :, :], hc[:, ds(half * (KT // 2), KT // 2), :], ACT.Copy).then_inc(u_staged, 1)
                        for v in range(2):
                            act.wait_ge(filt_summed, b * 2 + (v + 1))
                            act.wait_ge(parity_ready, b * 2 + CREDIT)
                            act.activation(f_rev[:, :, v * COLS:(v + 1) * COLS], pair_of(acc[:, 2 * v + 1, :]), ACT.Copy)\
                                .then_inc(rev_copied, 1)
                        for v in range(2):
                            act.wait_ge(u_turned, b * 2 + (v + 1))
                            act.wait_ge(u_summed, b * 2 + CREDIT)
                            act.activation(u_t[:, :, v * COLS:(v + 1) * COLS], pair(1 + v), ACT.Copy).then_inc(ut_ready, 1)
                        for v in range(2):
                            cols = slice(v * COLS, (v + 1) * COLS)
                            act.wait_ge(parity_ready, b * 2 + (v + 1) + CREDIT)
                            act.wait_ge(y_summed, b * 2 + CREDIT)
                            act.activation(f_abs[:, 0, :, cols], f_even[:, :, cols], ACT.Abs).then_inc(abs_ready, 1)
                            act.activation(f_abs[:, 1, :, cols], f_odd[:, :, cols], ACT.Abs).then_inc(abs_ready, 1)

            for c in range(RING):
                high(Chunk(c))
            act.wait_ge(params_ready, 1)
            norm("attn")
            parts("in_zx")
            parts("in_qk")
            act.wait_ge(mixer_tables, MIXER_DMAS * 16)
            act.activation(a_rate[:, :], a_log_b[:, :], ACT.Exp).then_inc(dt_exped, 1)
            act.wait_ge(dt_step, 2)
            act.activation(dt_u[:, :, :], dt_n[:, :, :], ACT.Exp, scale=-1.0).then_inc(dt_exped, 1)
            act.wait_ge(dt_step, 3)
            act.activation(dt_l[:, :, :], dt_w[:, :, :], ACT.Ln).then_inc(dt_exped, 1)
            act.wait_ge(drained, DRAINED["in_qk"])
            w0, b0 = ROW["conv_w"] + 3 * XBC_TILES, ROW["conv_b"]
            for m in range(XBC_TILES):
                act.activation(conv[:, m, :], pj[:, XBC0 + m, :], ACT.Identity, bias=params[:, b0 + m:b0 + m + 1],
                               scale=params[:, w0 + m:w0 + m + 1]).then_inc(conv_first, 1)
            parts("in_v")
            act.wait_ge(taps_done, 3 * XBC_TILES)
            act.activation(conv[:, :, :], conv[:, :, :], ACT.Silu).then_inc(conv_ready, 1)
            act.activation(pj[:, Z0:Z0 + KT, :], pj[:, Z0:Z0 + KT, :], ACT.Silu).then_inc(z_ready, 1)
            parts("in_g")
            act.wait_ge(drained, DRAINED["ssd_out"])
            act.activation(pj[:, GS0:GS0 + 2 * KT, :], pj[:, GS0:GS0 + 2 * KT, :], ACT.Sigmoid).then_inc(gates_ready, 1)
            with act.Fori(0, PAIRS) as i:
                act.wait_ge(gaps_ready, i + 1 + CREDIT)
                act.activation(decay[:, :, :], decay[:, :, :], ACT.Exp).then_inc(decay_ready, 1)
            for g in range(SSD_GROUPS):
                if g:
                    act.wait_ge(y_ssq, g)
                else:
                    act.wait_ge(y_gated, PAIRS)
                act.activation(sq_buf[:, :, :], pj[:, Z0 + 4 * g:Z0 + 4 * g + 4, :], ACT.Square).then_inc(y_squared, 1)
                act.wait_ge(y_ssq, g + 1)
                if g:
                    act.wait_ge(y_normed, g)
                act.activation(rstd[:, :], acc[:, g, 0:SEQ], ACT.Sqrt, bias=eps_col[:, 0:1],
                               scale=1.0 / (SSD_INNER // SSD_GROUPS)).then_inc(y_root, 1)
            parts("ssd_out")
            for k, (dst, scale) in enumerate(((sin_f, 1.0), (cos_f, 0.5))):
                act.wait_ge(angles, 1)
                act.activation(dst[:, :], ang[:, :], ACT.Sin, scale=scale).then_inc(sines, 1)
            with act.Fori(0, PAIRS // 2) as ii:
                for u in range(2):
                    stage_v(ii, u, 0)
                softmax_exp(ii, 0, True)
            parts("attn_out")
            parts("mix_out")
            norm("moe")
            for t in range(TT):
                act.wait_ge(gaps_e, 1)
                act.activation(g_exp[:, t, :], logits[:, t, 0:N_GROUPS], ACT.Exp, bias=g_neg[:, t:t + 1],
                               accum_out=g_sum[:, t:t + 1]).then_inc(exp_e, 1)
            act.wait_ge(gaps_e, 2)
            act.activation(e_exp[:, :], e_gap[:, :], ACT.Exp).then_inc(exp_e, 1)
            for k in range(0, EXPERTS // 2, 2):
                act.wait_ge(comb_spread, k + 1)
                act.activation(comb[:, 2 * k:2 * k + 2, :], pair(k % RING), ACT.Copy).then_inc(comb_act, 1)
            parts_mlp("experts")
            norm("ple")
            act.wait_ge(p_turned_ple, 1)
            act.activation(hid_hi[:, :, :], misc[:, :].rearrange("p (a n) -> p a n", a=2), ACT.Copy).then_inc(p_split, 1)
            parts("ple")
            for j, s in chunks(act, "ple_gate"):
                act.wait_ge(chunk_used, s.c + 1)
                act.wait_ge(drained, j + DRAINED["ple_gate"])
                act.activation(gate_s[:, :, :], pair(s.slot), ACT.Sigmoid).then_inc(gate_sig, 1)
                part(s)
            squares(SQUARED.index("final"), X_STATES.index("ple"))
            norm("mix0")
            parts("a_in0")
            short_conv(0)
            parts("a_out0")
            norm("ffn0")
            parts_mlp("ffn0")
            norm("mix1")
            parts("b_qk")
            def square(a):
                act.wait_ge(qk_summed, a + CREDIT)
                act.activation(na_sq[:, :, :], pj[:, a * KT:(a + 1) * KT, :], ACT.Square).then_inc(qk_squared, 1)

            def root(a):
                act.wait_ge(qk_summed, a + 1 + CREDIT)
                act.activation(na_rs[a][:, :, :], acc[:, :, :].rearrange("p m (a n) -> p (m a) n", a=2), ACT.Sqrt,
                               bias=eps_col[:, 0:1], scale=1.0 / HD).then_inc(qk_root, 1)
            act.wait_ge(drained, DRAINED["b_v"])
            square(0)
            parts("b_v", {0: lambda: (root(0), square(1)), 1: lambda: root(1)})
            act.wait_ge(drained, DRAINED["na_out"])
            act.wait_ge(late_tables, 16 * LATE_DMAS)
            act.wait_ge(qk_normed, 2 + CREDIT)
            with act.Fori(0, PAIRS // 2) as ii:
                for u in range(2):
                    i = ii * 2 + u
                    act.wait_ge(qk_scored, ii * 2 + PAIRS + CREDIT)
                    act.activation(qk_st[u][:, :, :], pj[:, 0:2 * KT, :].rearrange("p (a e) n -> p a e n", a=2)[:, :, i, :],
                                   ACT.Copy).then_inc(q_staged, 1)
                for u in range(2):
                    stage_v(ii, u, PAIRS)
                softmax_exp(ii, PAIRS, False)
            parts("na_out")
            norm("ffn1")
            parts_mlp("ffn1")
            norm("mix2")
            parts("hy_v")
            hyena_tap(0)
            parts("hy_x1")
            hyena_tap(1)
            parts("hy_x2", {1: lambda: filter_sine(0), 3: lambda: filter_sine(1)})
            hyena_tap(2)
            hyena_scalar()
            parts("hy_out")
            norm("ffn2")
            parts_mlp("ffn2")
            norm("mix3")
            parts("a_in1")
            short_conv(1)
            parts("a_out1")
            norm("ffn3")
            parts_mlp("ffn3")

        @block.vector
        def _(dve):
            chain = Chain(dve, dve_chain)
            link = chain.link

            def part(s):
                if s.more and s.slot != POOL_SLOT:
                    low(s.ahead())

            def low(n):
                dve.wait_ge(hi_ready, n.c + 1)
                dve.tensor_tensor(w_lo[n.slot][:, :], raw[n.slot][:, :], w_hi[n.slot][:, :].bitcast(f32), SUB)\
                    .then_inc(lo_dve, 1)

            def drain(name, read, after=()):
                for j, s in chunks(dve, name):
                    dve.wait_ge(chunk_used, s.c + 1)
                    read(j, pair(s.slot), s).then_inc(drained, 1)
                    part(s)
                    if j in after:
                        after[j]()

            def drain_to(name, tile):
                drain(name, lambda j, bank, s: dve.tensor_copy(pj[:, ds(j * 2 + tile, 2), :], bank))

            def drain_x(name):
                def read(j, bank, s):
                    xs = x[:, :, ds(j * COLS, COLS)]
                    return dve.tensor_tensor(xs, xs, bank, ADD)
                drain(name, read)
                dve.wait_ge(drained, DRAINED[name] + FIRST[name][1])
                signal(x_ready)

            def signal(s):
                dve.engine_nop().then_inc(s, 1)

            def scale_x(operand):
                n = SQUARED.index(operand)
                dve.wait_ge(inv_ready, n + 1)
                for t in range(TT):
                    dve.tensor_scalar(x_scaled[:, t, :], x[:, t, :], inv[:, t:t + 1], None, MUL).then_inc(scaled_ready, 1)

            def norm(operand):
                n = NORM_OF[operand]
                gain, row = NORMS[n][2], NORMS[n][3]
                scale_x(operand)
                for kk in range(KT // 2):
                    for a in range(2):
                        k = 2 * kk + a
                        col = ROW[gain] + row + k
                        dve.wait_ge(fhi_ready, n * KT + 2 * kk + 2)
                        last = dve.scalar_tensor_tensor(out=h_lo[:, k, :], in0=pair(kk % RING)[:, a, :],
                                                        scalar=params[:, col:col + 1], in1=h_hi[:, k, :].bitcast(f32),
                                                        op0=MUL, op1=SUB)
                        if a:
                            last.then_inc(turned_read, 1)
                dve.wait_ge(turned_read, (n + 1) * (KT // 2))
                signal(h_ready)

            def split_h(src, tiles=KT):
                link(dve.tensor_copy(h_hi[:, 0:tiles, :], src))
                link(dve.tensor_tensor(h_lo[:, 0:tiles, :], src, h_hi[:, 0:tiles, :].bitcast(f32), SUB))
                signal(h_ready)

            for c in range(RING):
                if c != POOL_SLOT:
                    low(Chunk(c))
            dve.wait_ge(params_turned, 1)
            dve.tensor_copy(params[:, :], misc[:, 0:PARAM_TILES * P]).then_inc(params_ready, 1)
            dve.wait_ge(params_ready, 1)
            norm("attn")
            drain_to("in_zx", 0)
            drain_to("in_qk", Q0)
            dve.wait_ge(mixer_tables, MIXER_DMAS * 16)
            dve.wait_ge(dt_summed, 1)
            dve.tensor_tensor(dt_x[:, :, :], misc[:, 0:TT * HEADS].rearrange("p (t h) -> p t h", t=TT),
                              dt_bias[:, :].unsqueeze(1).to_broadcast([P, TT, HEADS]), ADD).then_inc(dt_step, 1)
            dve.wait_ge(dt_step, 1)
            dve.scalar_tensor_tensor(out=dt_n[:, :, :], in0=dt_x[:, :, :], scalar=-1.0, in1=dt_x[:, :, :],
                                     op0=MUL, op1=ALU.max).then_inc(dt_step, 1)
            dve.wait_ge(dt_exped, 2)
            dve.tensor_scalar(dt_w[:, :, :], dt_u[:, :, :], 1.0, None, ADD).then_inc(dt_step, 1)
            dve.wait_ge(dt_step, 3)
            link(dve.tensor_scalar(dt_r[:, :, :], dt_w[:, :, :], -1.0, 1e-30, ADD, ADD))
            link(dve.reciprocal(dt_r[:, :, :], dt_r[:, :, :]))
            link(dve.tensor_tensor(dt_r[:, :, :], dt_r[:, :, :], dt_u[:, :, :], MUL))
            dve.wait_ge(dt_exped, 3)
            link(dve.tensor_scalar(dt_n[:, :, :], dt_l[:, :, :], 1e-30, None, ADD))
            link(dve.tensor_tensor(dt_r[:, :, :], dt_r[:, :, :], dt_n[:, :, :], MUL))
            link(dve.scalar_tensor_tensor(out=dt_t[:, :, :], in0=dt_x[:, :, :], scalar=0.0, in1=dt_r[:, :, :],
                                          op0=ALU.max, op1=ADD))
            dve.scalar_tensor_tensor(out=dA[:, :, :], in0=dt_t[:, :, :], scalar=-1.0,
                                     in1=a_rate[:, :].unsqueeze(1).to_broadcast([P, TT, HEADS]),
                                     op0=MUL, op1=MUL).then_inc(dA_ready, 1)
            for shift in range(1, SSD_TAPS):
                w = ROW["conv_w"] + (SSD_TAPS - 1 - shift) * XBC_TILES
                for m in range(XBC_TILES):
                    dve.wait_ge(conv_first, m + 1)
                    if shift > 1:
                        dve.wait_ge(taps_done, (shift - 2) * XBC_TILES + m + 1)
                    dve.scalar_tensor_tensor(out=conv[:, m, shift:], in0=pj[:, XBC0 + m, 0:SEQ - shift],
                                             scalar=params[:, w + m:w + m + 1], in1=conv[:, m, shift:],
                                             op0=MUL, op1=ADD).then_inc(taps_done, 1)
            drain("in_v", lambda j, bank, s: dve.tensor_copy(v_t[:, :, ds(j * COLS, COLS)], bank))
            dve.wait_ge(cum_summed, 1)
            link(dve.tensor_copy(cum_t[:, :, :], misc[:, 64:64 + TT * HEADS].rearrange("p (t h) -> p t h", t=TT)))
            link(dve.tensor_copy(cum_f[:, :], misc[0:HEADS, SEQ:2 * SEQ]))
            dve.tensor_tensor(cum_diag[:, :, :], cum_f[:, :].unsqueeze(1).to_broadcast([HEADS, HEADS, SEQ]),
                              diag16[:, :].unsqueeze(2).to_broadcast([HEADS, HEADS, SEQ]), MUL).then_inc(cum_ready, 1)
            drain_to("in_g", GS0)
            for kk in range(KT // 2):
                dve.wait_ge(xs_turned, kk + 1)
                dve.tensor_copy(xs_t[:, :, kk * COLS:(kk + 1) * COLS], pair(kk % RING)).then_inc(xs_read, 1)
            dve.wait_ge(cb_summed, 1)
            for g in range(SSD_GROUPS):
                link(dve.tensor_tensor(cb[:, g, 0:SEQ], acc[:, g, 0:SEQ], tri[:, 0, :], MUL))
                link(dve.tensor_tensor(cb[:, g, SEQ:TRI], acc[:, g, SEQ:TRI], tri[:, 1, P:SEQ], MUL))
            dve.wait_ge(xs_read, KT // 2)
            dve.wait_ge(z_ready, 1)
            for g in range(SSD_GROUPS):
                n = PAIRS // SSD_GROUPS
                with dve.Fori(0, n) as ii:
                    i = ii + g * n
                    dve.wait_ge(y_ready, i + CREDIT)
                    dve.tensor_tensor(xdt[:, :, :].rearrange("p t (h c) -> p t h c", h=2),
                                      xs_t[:, :, ds(i * P, P)].rearrange("p t (h c) -> p t h c", h=2),
                                      dt_t[:, :, ds(i * 2, 2)].unsqueeze(3).to_broadcast([P, TT, 2, HD]), MUL)\
                        .then_inc(xdt_ready, 1)
                    dve.wait_ge(cum_spread, i + 1)
                    for h in range(2):
                        for t, (a, b, q0) in enumerate(((0, SEQ, 0), (SEQ, TRI, P))):
                            last = dve.tensor_scalar(decay[:, h, a:b], acc[:, 2, h * SEQ + q0:(h + 1) * SEQ],
                                                     cum_t[:, t, ds(i * 2 + h, 1)], 0.0, SUB, ALU.min)
                    last.then_inc(gaps_ready, 1)
                    dve.wait_ge(decay_ready, i + 1)
                    dve.wait_ge(xdt_ready, i + 1)
                    dve.tensor_tensor(decay[:, :, :], decay[:, :, :],
                                      cb[:, g, :].unsqueeze(1).to_broadcast([P, 2, TRI]), MUL).then_inc(scores_ready, 1)
                    dve.wait_ge(y_ready, i + 1 + CREDIT)
                    dve.scalar_tensor_tensor(out=y_sum[:, :], in0=conv[:, i, :], scalar=d_col[:, ds(i, 1)],
                                             in1=acc[:, 3, 0:SEQ], op0=MUL, op1=ADD).then_inc(y_read, 1)
                    dve.wait_ge(y_read, i + 1 + CREDIT)
                    dve.tensor_tensor(pj[:, i, :], pj[:, i, :], y_sum[:, :], MUL).then_inc(y_gated, 1)
            for g in range(SSD_GROUPS):
                dve.wait_ge(y_gated, PAIRS)
                dve.wait_ge(y_root, g + 1)
                link(dve.reciprocal(rstd[:, :], rstd[:, :]))
                for a in range(4):
                    col = ROW["ssd_norm_w"] + 4 * g + a
                    last = dve.scalar_tensor_tensor(out=ynorm[:, a, :], in0=pj[:, 4 * g + a, :],
                                                    scalar=params[:, col:col + 1], in1=rstd[:, :],
                                                    op0=MUL, op1=MUL)
                last.then_inc(y_normed, 1)
                dve.wait_ge(y_normed, g + 1)
                link(dve.tensor_copy(h_hi[:, 4 * g:4 * g + 4, :], ynorm[:, :, :]))
                link(dve.tensor_tensor(h_lo[:, 4 * g:4 * g + 4, :], ynorm[:, :, :],
                                       h_hi[:, 4 * g:4 * g + 4, :].bitcast(f32), SUB))
            signal(h_ready)
            dve.wait_ge(gates_ready, 1)
            drain("ssd_out", lambda j, bank, s: dve.tensor_tensor(
                pj[:, ds(j * 2, 2), :], bank, pj[:, ds(j * 2 + GS0, 2), :], MUL))

            def softmax_rows(ii, base, causal_):
                cols = SCORE_COLS[causal_]
                for u in range(2):
                    i = ii * 2 + u
                    dve.wait_ge(qk_scored, i + (base + 1) + CREDIT)
                    dve.wait_ge(p_turned, ii * 2 + base + CREDIT)
                    if causal_:
                        dve.scalar_tensor_tensor(out=probs[u][:, :, 0:TRI], in0=scores[u][:, :, 0:TRI], scalar=HD ** -0.5,
                                                 in1=causal[:, :].unsqueeze(1).to_broadcast([P, 2, TRI]),
                                                 op0=MUL, op1=ADD).then_inc(masked, 1)
                    else:
                        dve.tensor_tensor(probs[u][:, :, :], scores[u],
                                          na_mask[:, :].unsqueeze(1).to_broadcast([P, 2, TT * SEQ]), ADD).then_inc(masked, 1)
                    dve.wait_ge(masked, i + (base + 1))
                    if causal_:
                        for t, (c, n) in enumerate(cols):
                            last = dve.tensor_reduce(at_max[u][:, :, t:t + 1].rearrange("p h o -> p (h o)"),
                                                     probs[u][:, :, c:c + n], AX.X, ALU.max, negate=True)
                    else:
                        last = dve.tensor_reduce(at_max[u][:, :, :], probs[u][:, :, :].rearrange("p h (t k) -> p h t k", t=TT),
                                                 AX.X, ALU.max, negate=True)
                    last.then_inc(max_ready, 1)
                for u in range(2):
                    dve.wait_ge(exped, ii * 8 + (base * 4 + 4 * u + 4))
                    link(dve.reciprocal(at_inv[u][:, :, :], at_sum[u][:, :, :]))
                    for h in range(2):
                        for t, (c, n) in enumerate(cols):
                            last = dve.tensor_scalar(probs[u][:, h, c:c + n], probs[u][:, h, c:c + n],
                                                     at_inv[u][:, h, t:t + 1], None, MUL)
                    last.then_inc(normed, 1)
                n = TRI if causal_ else 2 * SEQ
                for u in range(2):
                    dve.wait_ge(p_turned, ii * 2 + (base + u + 1) + CREDIT)
                    dve.tensor_copy(probs_t[u][:, 1, 0:n], turned_p[u][1][:, 0:n]).then_inc(pt_dve, 1)
                for u in range(2):
                    i = ii * 2 + u
                    dve.wait_ge(o_hi, i + (base + 1))
                    dve.tensor_tensor(h_lo[:, i, :], scores[u][:, 0, 0:SEQ], h_hi[:, i, :].bitcast(f32), SUB).then_inc(o_read, 1)

            dve.tensor_copy(ang_k[:, :], pos_i[:, :]).then_inc(dve_chain, 1)
            chain.count += 1
            dve.wait_ge(dve_chain, chain.count)
            link(dve.tensor_scalar(ang[:, :], ang_k[:, :], inv_freq[:, 0:1], None, MUL))
            reduce_angle(dve, link, ang[:, :], ang_k[:, :])
            signal(angles)
            dve.wait_ge(sines, 2)
            link(dve.tensor_tensor(cos_f[:, :], cos_f[:, :], cos_f[:, :], MUL))
            link(dve.tensor_scalar(cos_f[:, :], cos_f[:, :], -2.0, 1.0, MUL, ADD))
            with dve.Fori(0, PAIRS // 2) as ii:
                chain.begin(ii, 6)
                for u in range(2):
                    i = ii * 2 + u
                    qk = pj[:, Q0:Q0 + 2 * KT, :].rearrange("p (a e) n -> p a e n", a=2)[:, :, i, :]
                    dve.wait_ge(roped, i + CREDIT)
                    link(dve.tensor_tensor(rope_t[:, :, :], qk, cos_f[:, :].unsqueeze(1).to_broadcast([P, 2, SEQ]), MUL))
                    dve.wait_ge(rotated, i + 1)
                    link(dve.tensor_tensor(rope_u[:, :, :], turned_p[u][0].rearrange("p (a n) -> p a n", a=2),
                                           sin_f[:, :].unsqueeze(1).to_broadcast([P, 2, SEQ]), MUL))
                    dve.wait_ge(qk_scored, ii * 2 + CREDIT)
                    dve.tensor_tensor(qk_st[u][:, :, :], rope_t[:, :, :], rope_u[:, :, :], ADD).then_inc(roped, 1)
                softmax_rows(ii, 0, True)
            chain.end(PAIRS // 2)
            dve.wait_ge(o_read, PAIRS + CREDIT)
            signal(h_ready)
            def merge(j, bank, s):
                dve.wait_ge(drained, j + DRAINED["attn_out"])
                link(dve.tensor_tensor(merge_t[:, :, :], bank, pj[:, ds(j * 2 + GA0, 2), :], MUL))
                return dve.tensor_tensor(pj[:, ds(j * 2, 2), :], pj[:, ds(j * 2, 2), :], merge_t[:, :, :], ADD)
            drain("attn_out", merge)
            dve.wait_ge(drained, DRAINED["attn_out"] + 4)
            split_h(pj[:, 0:KT, :])
            drain_x("mix_out")
            def gated(name, weighted=False):
                c0, n = FIRST[name]
                base = ROUNDS[name]

                def product(i, c):
                    dve.wait_ge(silu_ready, i + (base + 1))
                    dve.wait_ge(hid_ready, i + base)
                    dve.wait_ge(chunk_used, c.c + 1)
                    dve.tensor_tensor(hid[:, :, :], silu_g[:, :].rearrange("p (a n) -> p a n", a=2), pair(c.slot), MUL)\
                        .then_inc(banks_read, 1)
                    dve.wait_ge(banks_read, i + (base + 1))
                    if weighted:
                        link(dve.tensor_tensor(hid[:, :, :], hid[:, :, :], comb[:, ds(i, 1), :].to_broadcast([P, 2, SEQ]), MUL))

                def split(i):
                    link(dve.tensor_copy(hid_hi[:, :, :], hid[:, :, :]))
                    dve.tensor_tensor(hid_lo[:, :, :], hid[:, :, :], hid_hi[:, :, :].bitcast(f32), SUB).then_inc(hid_ready, 1)

                dve.wait_ge(chunk_used, c0 + 1)
                part(Chunk(c0))
                product(0, Chunk(c0 + 1))
                part(Chunk(c0 + 1))
                split(0)
                rounds = n // 3 - 1
                looped = rounds - (1 if c0 + n == TOTAL else 0)
                for i, c, g in mlp_rounds(dve, name):
                    if g is i:
                        chain.begin(i, 2 if weighted else 1)
                    dve.wait_ge(chunk_used, Chunk(c, g).c + 1)
                    part(Chunk(c, g))
                    product(i + 1, Chunk(c + 1, g))
                    part(Chunk(c + 1, g))
                    dve.wait_ge(chunk_used, Chunk(c + 2, g).c + 1)
                    split(i + 1)
                    part(Chunk(c + 2, g))
                    if g is i:
                        chain.end(looped)
                dve.wait_ge(chunk_used, c0 + n)
                part(Chunk(c0 + n - 1))
                dve.tensor_copy(x[:, :, :], acc[:, :, :].rearrange("p (t m) n -> p t (m n)", t=TT)).then_inc(x_ready, 1)

            def short_conv(layer):
                cols = ROW["a_conv_w_2"] + layer * 3 * KT
                dve.wait_ge(drained, DRAINED[f"a_out{layer}"])
                dve.tensor_tensor(cu[:, :, :], pj[:, KT:2 * KT, :], pj[:, 2 * KT:3 * KT, :], MUL).then_inc(cu_ready, 1)
                for m in range(KT):
                    dve.wait_ge(a_first, layer * KT + m + 1)
                    dve.scalar_tensor_tensor(out=acv[:, m, 1:], in0=cu[:, m, 0:SEQ - 1], scalar=params[:, cols + m:cols + m + 1],
                                             in1=acv[:, m, 1:], op0=MUL, op1=ADD).then_inc(a_taps, 1)
                for m in range(KT):
                    dve.wait_ge(a_taps, 2 * KT * layer + m + 1)
                    w = cols + 2 * KT + m
                    dve.scalar_tensor_tensor(out=acv[:, m, 0:SEQ - 1], in0=cu[:, m, 1:], scalar=params[:, w:w + 1],
                                             in1=acv[:, m, 0:SEQ - 1], op0=MUL, op1=ADD).then_inc(a_taps, 1)
                dve.wait_ge(a_taps, 2 * KT * (layer + 1))
                link(dve.tensor_tensor(acv[:, :, :], acv[:, :, :], pj[:, 0:KT, :], MUL))
                split_h(acv[:, :, :])

            def filter_angle(layer):
                dve.wait_ge(hyena_tables, 16 * HYENA_DMAS)
                dve.wait_ge(f_summed, layer + 1)
                link(dve.tensor_scalar(f_hid[:, :], misc[0:HIDDEN, layer * SEQ:(layer + 1) * SEQ], (f_b1, f_b2)[layer][:, 0:1],
                                       f_freq[:, 0:1], ADD, MUL))
                reduce_angle(dve, link, f_hid[:, :], f_k[:, :])
                signal(f_angle)

            def hyena_taps(group):
                w = ROW["c_short_w_2"]
                with dve.Fori(group * KT, (group + 1) * KT) as m:
                    dve.wait_ge(hc_first, m + 1)
                    tile, src = [a[:, ds(m, 1), :].rearrange("p o n -> p (o n)") for a in (hc, pj)]
                    dve.scalar_tensor_tensor(out=tile[:, 1:], in0=src[:, 0:SEQ - 1], scalar=params[:, ds(m + w, 1)],
                                             in1=tile[:, 1:], op0=MUL, op1=ADD).then_inc(hc_taps, 1)
                    dve.wait_ge(hc_taps, m * 2 + 1)
                    dve.scalar_tensor_tensor(out=tile[:, 0:SEQ - 1], in0=src[:, 1:], scalar=params[:, ds(m + (w + 6 * KT), 1)],
                                             in1=tile[:, 0:SEQ - 1], op0=MUL, op1=ADD).then_inc(hc_taps, 1)

            def hyena_vector():
                dve.wait_ge(hc_taps, 6 * KT)
                with dve.Fori(0, D // HALF) as half:
                    chain.begin(half, ORDER * 28)
                    for n in range(ORDER):
                        b = half * ORDER + n
                        for v in range(2):
                            cols = slice(v * COLS, (v + 1) * COLS)
                            even, odd, forward = f_even[:, :, cols], f_odd[:, :, cols], pair_of(acc[:, 2 * v, :])
                            decay_v = f_decay[:, :, ds(half * HALF + v * COLS, COLS)]
                            dve.wait_ge(rev_copied, b * 2 + (v + 1))
                            dve.wait_ge(h_summed, b * 2 + CREDIT)
                            dve.wait_ge(abs_ready, b * 4 + CREDIT)
                            link(dve.tensor_tensor(even, forward, f_rev[:, :, cols], ADD))
                            link(dve.tensor_tensor(odd, forward, f_rev[:, :, cols], SUB))
                            link(dve.tensor_tensor(even, even, decay_v, MUL))
                            link(dve.tensor_tensor(odd, odd, decay_v, MUL))
                            dve.memset(f_odd[0:1, 0, cols], 0.0).then_inc(parity_ready, 1)
                        for v in range(2):
                            cols = slice(v * COLS, (v + 1) * COLS)
                            dve.wait_ge(abs_ready, b * 4 + (2 * v + 2) + CREDIT)
                            dve.tensor_tensor(f_abs[:, 0, :, cols], f_abs[:, 0, :, cols], f_abs[:, 1, :, cols], ALU.max)\
                                .then_inc(mag_ready, 1)
                        for v in range(2):
                            cols = slice(v * COLS, (v + 1) * COLS)
                            dve.wait_ge(norm_summed, b * 2 + (v + 1))
                            link(dve.reciprocal(f_inv[:, cols], side[v][:, 1, :]))
                            dve.wait_ge(h_summed, b * 2 + (v + 1) + CREDIT)
                            norm_v = f_inv[:, cols].unsqueeze(1).to_broadcast([P, TT, COLS])
                            link(dve.tensor_tensor(hs_re[:, :, cols], pair_of(acc[:, 2 * v, :]), norm_v, MUL))
                            link(dve.tensor_tensor(hs_im[:, :, cols], pair_of(acc[:, 2 * v + 1, :]), norm_v, MUL))
                            dve.tensor_tensor(hs_re2[:, cols], side[v][:, 0, :], f_inv[:, cols], MUL).then_inc(h_scaled, 1)
                        for v in range(2):
                            cols = slice(v * COLS, (v + 1) * COLS)
                            re, im, tmp = ys[:, 0:2, cols], ys[:, 2:4, cols], ys_t[:, :, cols]
                            u_re, u_im = pair_of(acc[:, 2 * v, :]), pair_of(acc[:, 2 * v + 1, :])
                            dve.wait_ge(u_summed, b * 2 + (v + 1) + CREDIT)
                            dve.wait_ge(h_scaled, b * 2 + (v + 1))
                            link(dve.tensor_tensor(re, u_re, hs_re[:, :, cols], MUL))
                            link(dve.tensor_tensor(tmp, u_im, hs_im[:, :, cols], MUL))
                            link(dve.tensor_tensor(re, re, tmp, SUB))
                            link(dve.tensor_tensor(im, u_re, hs_im[:, :, cols], MUL))
                            link(dve.tensor_tensor(ys_t[:, 0, cols], u_im[:, 0, :], hs_re2[:, cols], MUL))
                            link(dve.tensor_tensor(ys_t[:, 1, cols], u_im[:, 1, :], hs_re[:, 1, cols], MUL))
                            dve.tensor_tensor(im, im, tmp, ADD).then_inc(ys_ready, 1)
                        for v in range(2):
                            dve.wait_ge(y_summed, b * 2 + (v + 1) + CREDIT)
                            dve.wait_ge(ys_ready, b * 2 + 2 + CREDIT)
                            dve.wait_ge(z_made, b * 2 + v + CREDIT)
                            z = ys_t[:, v, :].rearrange("p (m n) -> p m n", n=SEQ)
                            for m in range(2):
                                skip = params[:, ds(half * (KT // 2) + (ROW["c_f_skip_2"] + n * KT + 2 * v + m), 1)]
                                last = dve.scalar_tensor_tensor(out=z[:, m, :], in0=u_st[:, 2 * v + m, :], scalar=skip,
                                                                in1=pair(1 + v)[:, m, :], op0=MUL, op1=ADD)
                            link(last)
                            gate = hc[:, ds(half * (KT // 2) + ((n + 1) * KT + 2 * v), 2), :]
                            dest = hc[:, ds(half * (KT // 2) + 2 * v, 2), :] if n == ORDER - 1 else u_st[:, 2 * v:2 * v + 2, :]
                            dve.tensor_tensor(dest, z[:, :, :], gate, MUL).then_inc(z_made, 1)
                chain.end(D // HALF)
                dve.wait_ge(z_made, 4 * ORDER + CREDIT)
                split_h(hc[:, 0:KT, :])

            norm("moe")
            dve.wait_ge(router_tables, 16 * ROUTER_DMAS)
            link(dve.memset(g_pad[:, :, :], -3e38))
            dve.wait_ge(routed, 1)
            link(dve.tensor_tensor(logits[:, :, :], misc[:, 0:TT * NL].rearrange("p (t n) -> p t n", t=TT),
                                   b_route[:, :].unsqueeze(1).to_broadcast([P, TT, NL]), ADD))
            link(dve.tensor_copy(g_pad[:, :, 0:N_GROUPS], logits[:, :, 0:N_GROUPS]))
            for t in range(TT):
                link(dve.max(g_top[:, t, :], g_pad[:, t, :]))
            dve.tensor_scalar(g_neg[:, :], g_top[:, :, 0], -1.0, None, MUL).then_inc(gaps_e, 1)
            for t in range(TT):
                link(dve.max_index(out=g_idx[:, t, :], in_max=g_top[:, t, :], in_values=g_pad[:, t, :]))
            link(dve.tensor_copy(g_idxf[:, :], g_idx[:, :, 0]))
            for t in range(TT):
                link(dve.tensor_scalar(g_hot[:, t, :], iota8[:, 0:N_GROUPS], g_idxf[:, t:t + 1], None, ALU.is_equal))
            for t in range(TT):
                link(dve.tensor_tensor(e_prod[:, t, :].rearrange("p (g e) -> p g e", g=N_GROUPS),
                                       logits[:, t, N_GROUPS:].rearrange("p (g e) -> p g e", g=N_GROUPS),
                                       g_hot[:, t, :].unsqueeze(2).to_broadcast([P, N_GROUPS, GROUP_EXPERTS]), MUL))
            for t in range(TT):
                link(dve.tensor_reduce(e_sel[:, t, :], e_prod[:, t, :].rearrange("p (g e) -> p e g", g=N_GROUPS), AX.X, ADD))
            for t in range(TT):
                link(dve.max(e_top[:, t, :], e_sel[:, t, :]))
            dve.tensor_tensor(e_gap[:, :], e_top[:, :, 1], e_top[:, :, 0], SUB).then_inc(gaps_e, 1)
            for t in range(TT):
                link(dve.max_index(out=e_idx[:, t, :], in_max=e_top[:, t, :], in_values=e_sel[:, t, :]))
            link(dve.tensor_copy(e_idxf[:, :, :], e_idx[:, :, 0:2]))
            for t in range(TT):
                for k in range(2):
                    link(dve.tensor_scalar(e_hot[:, t, k, :], iota8[:, :], e_idxf[:, t, k:k + 1], None, ALU.is_equal))
            dve.wait_ge(exp_e, 3)
            link(dve.reciprocal(g_w[:, :], g_sum[:, :]))
            link(dve.tensor_scalar(e_den[:, :], e_exp[:, :], 1.0, None, ADD))
            link(dve.reciprocal(e_den[:, :], e_den[:, :]))
            link(dve.tensor_tensor(e_w[:, :, 0], e_den[:, :], g_w[:, :], MUL))
            link(dve.tensor_tensor(e_w[:, :, 1], e_w[:, :, 0], e_exp[:, :], MUL))
            for t in range(TT):
                link(dve.tensor_scalar(e_wt[:, t, :], e_hot[:, t, 0, :], e_w[:, t, 0:1], None, MUL))
                link(dve.scalar_tensor_tensor(out=e_wt[:, t, :], in0=e_hot[:, t, 1, :], scalar=e_w[:, t, 1:2],
                                              in1=e_wt[:, t, :], op0=MUL, op1=ADD))
            for t in range(TT):
                link(dve.tensor_tensor(comb_t[:, t, :, :], g_hot[:, t, :].unsqueeze(2).to_broadcast([P, N_GROUPS, GROUP_EXPERTS]),
                                       e_wt[:, t, :].unsqueeze(1).to_broadcast([P, N_GROUPS, GROUP_EXPERTS]), MUL))
            signal(comb_made)
            dve.wait_ge(comb_turned, 1)
            dve.tensor_copy(comb_f[:, :], misc[0:EXPERTS, SEQ:2 * SEQ]).then_inc(comb_f_ready, 1)
            for k in range(1, EXPERTS // 2, 2):
                dve.wait_ge(comb_spread, k + 1)
                dve.tensor_copy(comb[:, 2 * k:2 * k + 2, :], pair(k % RING)).then_inc(comb_dve, 1)
            dve.wait_ge(comb_act, EXPERTS // 4)
            dve.wait_ge(comb_dve, EXPERTS // 4)
            gated("experts", True)
            norm("ple")
            dve.wait_ge(p_split, 1)
            dve.tensor_tensor(hid_lo[:, :, :], misc[:, :].rearrange("p (a n) -> p a n", a=2),
                              hid_hi[:, :, :].bitcast(f32), SUB).then_inc(p_low, 1)
            c = Chunk(FIRST["ple"][0])
            dve.wait_ge(chunk_used, c.c + 1)
            part(c)

            def add_ple(j, bank, s):
                dve.wait_ge(gate_sig, j + 1)
                dve.wait_ge(drained, j + DRAINED["ple_gate"])
                xs = x[:, :, ds(j * COLS, COLS)]
                link(dve.tensor_tensor(gate_m[:, :, :], gate_s[:, :, :],
                                       acc[:, :, :].rearrange("p (t m) n -> p t (m n)", t=TT)[:, :, ds(j * COLS, COLS)], MUL))
                return dve.tensor_tensor(xs, xs, gate_m[:, :, :], ADD)
            drain("ple_gate", add_ple)
            dve.wait_ge(drained, DRAINED["ple_gate"] + FIRST["ple_gate"][1])
            signal(x_ready)
            dve.wait_ge(late_tables, 16 * LATE_DMAS)
            dve.wait_ge(inv_ready, SQUARED.index("final") + 1)
            for t in range(TT):
                dve.scalar_tensor_tensor(out=x[:, t, :], in0=x[:, t, :], scalar=inv[:, t:t + 1], in1=final_w[:, :],
                                         op0=MUL, op1=MUL).then_inc(scaled_ready, 1)
            dve.wait_ge(scaled_ready, TT * (SQUARED.index("final") + 1))
            signal(x_ready)
            norm("mix0")
            drain_to("a_in0", 0)
            short_conv(0)
            drain_x("a_out0")
            norm("ffn0")
            gated("ffn0")
            norm("mix1")
            drain_to("b_qk", 0)
            dve.wait_ge(late_tables, 16 * LATE_DMAS)
            link(dve.tensor_scalar(qk_gain[:, 0:1], qk_gain[:, 0:1], HD ** -0.5, None, MUL))

            def normalize(a):
                dve.wait_ge(qk_root, a + 1 + CREDIT)
                link(dve.reciprocal(na_rs[a][:, :, :], na_rs[a][:, :, :]))
                qk = pj[:, a * KT:(a + 1) * KT, :]
                dve.scalar_tensor_tensor(out=qk, in0=qk, scalar=qk_gain[:, a:a + 1], in1=na_rs[a][:, :, :],
                                         op0=MUL, op1=MUL).then_inc(qk_normed, 1)
            drain("b_v", lambda j, bank, s: dve.tensor_copy(v_t[:, :, ds(j * COLS, COLS)], bank),
                  {1: lambda: normalize(0), 2: lambda: normalize(1)})
            with dve.Fori(0, PAIRS // 2) as ii:
                chain.begin(ii, 2)
                softmax_rows(ii, PAIRS, False)
            chain.end(PAIRS // 2)
            dve.wait_ge(o_read, 2 * PAIRS + CREDIT)
            signal(h_ready)
            drain_x("na_out")
            norm("ffn1")
            gated("ffn1")
            norm("mix2")
            drain_to("hy_v", 0)
            hyena_taps(0)
            drain_to("hy_x1", KT)
            hyena_taps(1)
            drain("hy_x2", lambda j, bank, s: dve.tensor_copy(pj[:, ds(j * 2 + 2 * KT, 2), :], bank),
                  {1: lambda: filter_angle(0), 3: lambda: filter_angle(1)})
            hyena_taps(2)
            hyena_vector()
            drain_x("hy_out")
            norm("ffn2")
            gated("ffn2")
            norm("mix3")
            drain_to("a_in1", 0)
            short_conv(1)
            drain_x("a_out1")
            norm("ffn3")
            gated("ffn3")

    return nc


def reduce_angle(dve, link, angle, k):
    ALU = mybir.AluOpType
    link(dve.tensor_scalar(k, angle, 1.0 / (2 * math.pi), ROUND, ALU.mult, ALU.add))
    link(dve.tensor_scalar(k, k, -ROUND, None, ALU.add))
    for part in (TWO_PI_1, TWO_PI_2, TWO_PI_3):
        link(dve.scalar_tensor_tensor(out=angle, in0=k, scalar=-part, in1=angle, op0=ALU.mult, op1=ALU.add))


INPUTS = ["x", "p", "positions", "attn_norm_w", "w_in", "conv_w", "conv_b", "dt_bias", "a_log", "d_skip", "ssd_norm_w",
          "w_ssd_out", "w_attn_out", "w_out", "moe_norm_w", "w_router_group", "b_router_group", "w_router_expert",
          "b_router_expert", "w_exp_gate", "w_exp_up", "w_exp_down", "ple_norm_w", "w_ple", "w_ple_gate",
          "final_norm_w", "norm_mix_g_2", "norm_ffn_g_2", "a_w_in_2", "a_conv_w_2", "a_w_out_2", "b_w_qkv_2",
          "b_q_norm_g_2", "b_k_norm_g_2", "b_rpb_2", "b_w_out_2", "c_w_in_2", "c_short_w_2", "c_short_b_2",
          "c_f_w1_2", "c_f_b1_2", "c_f_w2_2", "c_f_b2_2", "c_f_w3_2", "c_f_freq_2", "c_f_skip_2", "c_w_out_2",
          "f_w13_2", "f_w2_2"]


def kernel(**inputs):
    import numpy as _np
    import concourse.bacc as _bacc
    from concourse import mybir as _mybir
    from concourse.bass_utils import run_bass_kernel_spmd as _run

    nc = _bacc.Bacc("TRN2", target_bir_lowering=False, num_devices=1)
    arrays, views = {}, {}
    for name, a in [(n, _np.asarray(inputs[n])) for n in INPUTS] + list(constants().items()):
        a = _np.ascontiguousarray(a)
        arrays[f"in_{name}_dram"] = a
        views[name] = nc.dram_tensor(f"in_{name}_dram", a.shape, _mybir.dt.from_np(a.dtype), kind="ExternalInput").ap()
    out = nc.dram_tensor("out_0_dram", (1, SEQ, D), _mybir.dt.float32, kind="ExternalOutput").ap()
    build(nc, views, out)
    r = _run(nc, [arrays], core_ids=[0])
    return r.results[0]["out_0_dram"]
```

```python
import math
from contextlib import ExitStack

import numpy as np
import concourse.bass as bass
from concourse import mybir

P = 128
SEQ, D = 256, 1024
TT = SEQ // P
KT = D // P
COLS = 256
RING = 3
POOL_SLOT = 0
CHUNK = KT * COLS
HEADS, HD = 16, 64
PAIRS = HEADS // 2
SSD_GROUPS, SSD_STATE, SSD_TAPS = 2, 64, 4
SSD_INNER = HEADS * HD
SSD_CHANNELS = SSD_INNER + 2 * SSD_GROUPS * SSD_STATE
XBC_TILES = SSD_CHANNELS // P
DT_COL = SSD_INNER + SSD_CHANNELS
MIXER_DMAS = 11
N_GROUPS, GROUP_EXPERTS = 4, 8
EXPERTS = N_GROUPS * GROUP_EXPERTS
D_EXPERT = 256
FFN = ((8 * D + 3 * 256 - 1) // (3 * 256)) * 256
LAYERS = 4
HALF = 512
GRID_W, NA_ROWS, NA_COLS = 64, 8, 16
ORDER, BANDS, EMB, HIDDEN = 2, 16, 33, 64
EPS = 1e-6
NEG = -1e30
CREDIT = 1
TRI = P + SEQ

MLP_CHUNKS = 3 * (FFN // COLS)
STREAM = [("in_zx", 9), ("in_qk", 8), ("in_v", 4), ("in_g", 8), ("ssd_out", 4), ("attn_out", 4), ("mix_out", 4), ("experts", 3 * EXPERTS),
          ("ple", 1), ("ple_gate", 4),
          ("a_bc0", 8), ("a_u0", 4), ("a_out0", 4), ("ffn0", MLP_CHUNKS),
          ("b_qk", 8), ("b_v", 4), ("na_out", 4), ("ffn1", MLP_CHUNKS),
          ("hy_v", 4), ("hy_x1", 4), ("hy_x2", 4), ("hy_out", 4), ("ffn2", MLP_CHUNKS),
          ("a_bc1", 8), ("a_u1", 4), ("a_out1", 4), ("ffn3", MLP_CHUNKS)]
FIRST = {}
_c = 0
for _name, _n in STREAM:
    FIRST[_name] = (_c, _n)
    _c += _n
TOTAL = _c
BANKED = [n for n, _ in STREAM if n not in ("experts", "ple") and not n.startswith("ffn")]
DRAINED = {}
_c = 0
for _name in BANKED:
    DRAINED[_name] = _c
    _c += dict(STREAM)[_name]
LATE_DMAS, ROUTER_DMAS, HYENA_DMAS = 9, 5, 10
X_STATES = ["input", "mix_out", "experts", "ple", "final", "a_out0", "ffn0", "na_out", "ffn1", "hy_out",
            "ffn2", "a_out1", "ffn3"]
OPERANDS = ["attn", "ssd", "attention", "merged", "moe", "ple", "mix0", "conv0", "ffn0", "mix1", "na",
            "ffn1", "mix2", "hyena", "ffn2", "mix3", "conv1", "ffn3"]
NORMS = [("attn", "input", "attn_norm_w", 0), ("moe", "mix_out", "moe_norm_w", 0),
         ("ple", "experts", "ple_norm_w", 0)]
for _i, _a, _b in ((0, "final", "a_out0"), (1, "ffn0", "na_out"), (2, "ffn1", "hy_out"), (3, "ffn2", "a_out1")):
    NORMS += [(f"mix{_i}", _a, "norm_mix_g_2", 8 * _i), (f"ffn{_i}", _b, "norm_ffn_g_2", 8 * _i)]
NORM_OF = {_o: _k for _k, (_o, *_r) in enumerate(NORMS)}
SQUARED = [_o for _o, *_r in NORMS]
SQUARED.insert(3, "final")
GATED = ["experts", "ffn0", "ffn1", "ffn2", "ffn3"]
BEFORE = {"moe": "mix_out", "ple": "experts", "final": "ple_gate", "ffn0": "a_out0", "mix1": "ffn0",
          "ffn1": "na_out", "mix2": "ffn1", "ffn2": "hy_out", "mix3": "ffn2", "ffn3": "a_out1"}
ROUNDS = {"experts": 0}
for _i in range(LAYERS):
    ROUNDS[f"ffn{_i}"] = EXPERTS + _i * (FFN // COLS)

PARAMS = [("attn_norm_w", 8), ("moe_norm_w", 8), ("ple_norm_w", 8), ("ssd_norm_w", 8),
          ("conv_w", 40), ("conv_b", 10), ("norm_mix_g_2", 32), ("norm_ffn_g_2", 32),
          ("a_conv_w_2", 48), ("c_short_w_2", 72), ("c_short_b_2", 24), ("c_f_skip_2", 16)]
ROW = {}
_c = 0
for _name, _n in PARAMS:
    ROW[_name] = _c
    _c += _n
PARAM_ROWS = _c
PARAM_TILES = -(-PARAM_ROWS // P)


TWO_PI_1 = 6.28125
TWO_PI_2 = float(np.float32(np.round((2 * math.pi - TWO_PI_1) * 2 ** 20) / 2 ** 20))
TWO_PI_3 = float(np.float32(2 * math.pi - TWO_PI_1 - TWO_PI_2))
ROUND = 1.5 * 2 ** 23


def constants():
    f32 = np.float32
    c = {}
    c["ident"] = np.eye(P, dtype=f32)
    tri = np.zeros((P, TT, SEQ), f32)
    for t in range(TT):
        tri[:, t] = (np.arange(P)[:, None] + P * t) <= np.arange(SEQ)[None]
    c["tri"] = tri.reshape(P, TT * SEQ)
    q = np.arange(P)[:, None]
    c["causal"] = np.concatenate([np.where(np.arange(P)[None] <= q, 0, NEG),
                                  np.where(np.arange(SEQ)[None] <= q + P, 0, NEG)], 1).astype(f32)
    half = HD // 2
    rot = np.zeros((P, P), f32)
    for m in range(P):
        if m % HD < half:
            rot[m + half, m] = -1
        else:
            rot[m - half, m] = 1
    c["rot"] = rot
    inv = f32(10000.0) ** (-np.arange(half, dtype=f32) / f32(half))
    c["inv_freq"] = np.tile(inv, P // half).reshape(P, 1).astype(f32)
    c["diag16"] = np.eye(HEADS, dtype=f32)
    c["iota8"] = np.tile(np.arange(8, dtype=f32), (P, 1))
    c["headones"] = np.kron(np.eye(2, dtype=f32), np.ones((HD, HD), f32))
    c["flip"] = np.kron(np.eye(2, dtype=f32), np.eye(GRID_W, dtype=f32)[::-1])
    col = np.arange(SEQ) % GRID_W
    start = np.clip(col - NA_COLS // 2, 0, GRID_W - NA_COLS)
    ok = (col[None] >= start[:, None]) & (col[None] < start[:, None] + NA_COLS)
    c["na_mask"] = np.where(ok, 0, NEG).astype(f32).reshape(TT, P, SEQ).transpose(1, 0, 2).reshape(P, -1)
    t = np.linspace(0.0, 1.0, SEQ, dtype=f32)[:, None]
    bands = np.linspace(1e-4, BANDS - 1, BANDS, dtype=f32)
    ang = (f32(2.0 * math.pi) * np.arange(SEQ, dtype=f32)[:, None] / f32(SEQ) * bands).astype(f32)
    z = np.concatenate([t, np.cos(ang), -np.sin(ang)], -1).astype(f32)
    c["embed"] = np.ascontiguousarray(z.T)
    lt = math.log(1e-2)
    deltas = np.abs(np.linspace(lt / 1.5, lt / 0.3, D, dtype=f32))
    c["decay"] = np.exp(-t * deltas).astype(f32)
    n = 2 * SEQ
    tt = np.arange(SEQ)[:, None]
    f = np.arange(SEQ)[None]
    cos, sin = np.cos(2 * np.pi * tt * f / n), -np.sin(2 * np.pi * tt * f / n)
    nyq = np.cos(np.pi * np.arange(SEQ))
    sinn = sin.copy()
    sinn[:, 0] = nyq
    cosn = cos.copy()
    cosn[:, 0] = nyq
    c["dft"] = np.concatenate([cos, sinn, sin, cosn[:, :P]], 1).astype(f32)
    w = np.full(SEQ, 2.0)
    w[0] = 1.0
    icos = (w[:, None] * np.cos(2 * np.pi * f.T * tt.T / n)) / n
    isin = (-w[:, None] * np.sin(2 * np.pi * f.T * tt.T / n)) / n
    isin[0] = nyq / n
    c["idft"] = np.concatenate([icos, isin], 0).astype(f32)
    return c


class Chunk:

    def __init__(self, number, group=0):
        self.c = group * RING + number
        self.slot = number % RING
        self.turn = group + number // RING
        self.first = number < RING and isinstance(group, int)
        self.more = not (isinstance(group, int) and number + RING * group + RING >= TOTAL)

    def ahead(self):
        new = Chunk.__new__(Chunk)
        new.c, new.slot, new.turn, new.first, new.more = self.c + RING, self.slot, self.turn + 1, False, True
        return new


def last_chunk(name):
    return Chunk(sum(FIRST[name]) - 1)


def in_norm(name, j):
    return name in BEFORE.values() and isinstance(j, int) and j == FIRST[name][1] - 1


def chunks(eng, name):
    c0, n = FIRST[name]
    j = 0
    if c0 == 0:
        for j in range(RING):
            yield j, Chunk(j)
        j = RING
    groups = min(n - j, TOTAL - RING - c0 - j) // RING
    if groups > 1:
        with eng.Fori(0, groups) as g:
            for r in range(RING):
                yield g * RING + (j + r), Chunk(c0 + j + r, g)
        j += groups * RING
    for r in range(j, n):
        yield r, Chunk(c0 + r)


def mlp_rounds(eng, name):
    c0, n = FIRST[name]
    rounds = n // 3 - 1
    peel = 1 if c0 + n == TOTAL else 0
    with eng.Fori(0, rounds - peel) as g:
        yield g, c0 + 2, g
    for i in range(rounds - peel, rounds):
        yield i, c0 + 2 + 3 * i, 0


class Chain:

    def __init__(self, eng, sem):
        self.eng, self.sem, self.count, self.extra = eng, sem, 0, 0

    def link(self, ins):
        self.count += 1
        ins.then_inc(self.sem, 1)
        self.eng.wait_ge(self.sem, self.extra + self.count)

    def begin(self, i, per_round):
        self.start, self.per_round = self.count, per_round
        self.extra = i * per_round

    def end(self, rounds):
        assert self.count - self.start == self.per_round, (self.count - self.start, self.per_round)
        self.count = self.start + rounds * self.per_round
        self.extra = 0


def flat(ap, n):
    dims = " ".join(f"d{i}" for i in range(len(ap.shape)))
    return ap.rearrange(f"{dims} -> ({dims})").rearrange("(r n) -> r n", n=n)


def build(nc, A, out):
    f32, f32r, i32, u32 = mybir.dt.float32, mybir.dt.float32r, mybir.dt.int32, mybir.dt.uint32
    ALU, ACT, AX = mybir.AluOpType, mybir.ActivationFunctionType, mybir.AxisListType
    SUB, ADD, MUL = ALU.subtract, ALU.add, ALU.mult
    ds = bass.ds
    ctx = ExitStack()
    with ctx:
        def sb(name, shape, dt=f32):
            return ctx.enter_context(nc.sbuf_tensor(name, shape, dt))

        def sem(name):
            return ctx.enter_context(nc.semaphore(name))

        raw = [sb(f"raw{i}", [P, CHUNK]) for i in range(RING)]
        w_hi = [sb(f"w_hi{i}", [P, CHUNK], f32r) for i in range(RING)]
        w_lo = [sb(f"w_lo{i}", [P, CHUNK], f32r) for i in range(RING)]
        x = sb("x_res", [P, TT, D])
        h_hi = sb("h_hi", [P, KT, SEQ], f32r)
        h_lo = sb("h_lo", [P, KT, SEQ], f32r)
        ident = sb("ident_sb", [P, P])
        ones = sb("ones", [P, P])
        params = sb("params", [P, PARAM_TILES * P])
        ssq = sb("ssq", [P, TT])
        ms = sb("ms", [P, TT])
        inv = sb("inv", [P, TT])
        neg_half = sb("neg_half", [P, TT])
        eps_col = sb("eps_col", [P, 1])

        work0 = -(-nc.sbuf_base // 32) * 32
        limit = nc.sbuf_usable_end - work0

        def at(name, shape, offset, dt=f32):
            size = int(np.prod(shape[1:])) * 4
            assert offset + size <= limit, (name, offset + size, limit)
            return nc.alloc_sbuf_tensor_at(name, shape, dt, offset=work0 + offset)

        KB = 1024
        x_scaled = at("x_scaled", [P, TT, D], 0)
        param_rows = at("param_rows", [P, PARAM_TILES, P], 8 * KB)
        Z0, XBC0, Q0, GS0, GA0 = 0, 8, 18, 34, 42
        pj = at("pj", [P, 50, SEQ], 0)
        v_t = at("v_t", [P, TT, D], 50 * KB)
        conv = at("conv", [P, 10, SEQ], 58 * KB)
        xs_t = at("xs_t", [P, TT, D], 8 * KB)
        cb = at("cb", [P, SSD_GROUPS, TRI], 68 * KB)
        cum_diag = at("cum_diag", [HEADS, HEADS, SEQ], 71 * KB)
        decay = [at(f"decay_w{u}", [P, 2, TRI], (87 * KB, 100 * KB + 512)[u]) for u in range(2)]
        xdt = [at(f"xdt{u}", [P, TT, 2 * HD], (90, 16)[u] * KB) for u in range(2)]
        tri = at("tri_sb", [P, TT, SEQ], 91 * KB)
        S1 = 93 * KB
        diag16 = at("diag16_sb", [HEADS, HEADS], S1)
        dt_bias = at("dt_bias_sb", [P, HEADS], S1 + 64)
        a_rate = at("a_rate", [P, HEADS], S1 + 128)
        w_dt = at("w_dt", [P, KT, HEADS], S1 + 192)
        dt_x = at("dt_x", [P, TT, HEADS], S1 + 704)
        dt_n = at("dt_n", [P, TT, HEADS], S1 + 832)
        dt_u = at("dt_u", [P, TT, HEADS], S1 + 960)
        dt_w = at("dt_w", [P, TT, HEADS], S1 + 1088)
        dt_l = at("dt_l", [P, TT, HEADS], S1 + 1216)
        dt_r = at("dt_r", [P, TT, HEADS], S1 + 1344)
        dt_t = at("dt_t", [P, TT, HEADS], S1 + 1472)
        dA = at("dA", [P, TT, HEADS], S1 + 1600)
        cum_t = at("cum_t", [P, TT, HEADS], S1 + 1728)
        d_col = at("d_col", [P, PAIRS], S1 + 1856)
        inv_freq = at("inv_freq_sb", [P, 1], S1 + 1888)
        a_log_b = at("a_log_b", [P, HEADS], S1 + 1952)
        cum_f = at("cum_f", [HEADS, SEQ], 95 * KB + 256)
        rot = at("rot_sb", [P, P], 96 * KB + 512)
        causal = at("causal_sb", [P, TRI], 97 * KB)
        cos_f = at("cos_f", [P, SEQ], 98 * KB + 512)
        sin_f = at("sin_f", [P, SEQ], 99 * KB + 512)
        ang = at("ang", [P, SEQ], 100 * KB + 512)
        ang_k = at("ang_k", [P, SEQ], 101 * KB + 512)
        pos_i = at("pos_i", [P, SEQ], 102 * KB + 512, i32)
        y_sum = at("y_sum", [P, SEQ], 103 * KB + 512)
        sq_buf = at("sq_buf", [P, 4, SEQ], 71 * KB)
        ynorm = at("ynorm", [P, 4, SEQ], 75 * KB)
        rstd = at("rstd", [P, SEQ], 79 * KB)
        rope_t = at("rope_t", [P, 2, SEQ], 58 * KB)
        rope_u = at("rope_u", [P, 2, SEQ], 60 * KB)
        qk_st = [at(f"qk_st{u}", [P, 2, SEQ], (62, 87)[u] * KB) for u in range(2)]
        v_st = [at(f"v_st{u}", [P, TT, 2 * HD], (64, 89)[u] * KB) for u in range(2)]
        probs = [at(f"probs{u}", [P, 2, TT * SEQ], (65, 78)[u] * KB) for u in range(2)]
        probs_t = [at(f"probs_t{u}", [P, 2, TT * SEQ], (69, 82)[u] * KB) for u in range(2)]
        at_max = [at(f"at_max{u}", [P, 2, TT], 73 * KB + 96 * u) for u in range(2)]
        at_sum = [at(f"at_sum{u}", [P, 2, TT], 73 * KB + 96 * u + 32) for u in range(2)]
        at_inv = [at(f"at_inv{u}", [P, 2, TT], 73 * KB + 96 * u + 64) for u in range(2)]
        merge_t = at("merge_t", [P, 2, SEQ], 74 * KB)
        na_mask = at("na_mask_sb", [P, TT * SEQ], 76 * KB)
        na_bias = [at(f"na_bias{b}", [P, 2, TT * SEQ], (24 + 4 * b) * KB) for b in range(2)]
        headones = at("headones_sb", [P, P], 86 * KB)
        qk_gain = at("qk_gain", [P, 2], 86 * KB + 512)
        flip = at("flip_sb", [P, P], 91 * KB)
        na_sq = at("na_sq", [P, KT, SEQ], 32 * KB)
        qk_rms = at("qk_rms", [P, 2, TT, HEADS], 16 * KB)
        head_cols = at("head_cols", [HEADS, PAIRS, P], 19 * KB)
        rms_f = at("rms_f", [HEADS, 2, SEQ], 17 * KB)
        comb = at("comb", [P, EXPERTS, SEQ], 8 * KB)
        silu_g = at("silu_g", [P, 2 * SEQ], 40 * KB)
        hid = at("hid", [P, 2, SEQ], 42 * KB)
        hid_hi = at("hid_hi", [P, 2, SEQ], 44 * KB, f32r)
        hid_lo = at("hid_lo", [P, 2, SEQ], 46 * KB, f32r)
        R0 = 48 * KB
        NL = N_GROUPS + EXPERTS
        w_route = at("w_route", [P, KT, NL], 105 * KB)
        b_route = at("b_route", [P, NL], 106 * KB + 128)
        logits = at("logits", [P, TT, NL], R0 + 1344)
        g_pad = at("g_pad", [P, TT, 8], R0 + 1664)
        g_top = at("g_top", [P, TT, 8], R0 + 1728)
        g_idx = at("g_idx", [P, TT, 8], R0 + 1792, u32)
        g_idxf = at("g_idxf", [P, TT], R0 + 1856)
        g_hot = at("g_hot", [P, TT, N_GROUPS], R0 + 1920)
        g_neg = at("g_neg", [P, TT], R0 + 1952)
        g_exp = at("g_exp", [P, TT, N_GROUPS], R0 + 1984)
        g_sum = at("g_sum", [P, TT], R0 + 2016)
        g_w = at("g_w", [P, TT], R0 + 2048)
        e_prod = at("e_prod", [P, TT, EXPERTS], R0 + 2080)
        e_sel = at("e_sel", [P, TT, GROUP_EXPERTS], R0 + 2336)
        e_top = at("e_top", [P, TT, 8], R0 + 2400)
        e_idx = at("e_idx", [P, TT, 8], R0 + 2464, u32)
        e_idxf = at("e_idxf", [P, TT, 2], R0 + 2528)
        e_hot = at("e_hot", [P, TT, 2, 8], R0 + 2592)
        e_gap = at("e_gap", [P, TT], R0 + 2720)
        e_exp = at("e_exp", [P, TT], R0 + 2752)
        e_den = at("e_den", [P, TT], R0 + 2784)
        e_w = at("e_w", [P, TT, 2], R0 + 2816)
        e_wt = at("e_wt", [P, TT, 8], R0 + 2880)
        comb_t = at("comb_t", [P, TT, N_GROUPS, GROUP_EXPERTS], R0 + 3008)
        comb_f = at("comb_f", [EXPERTS, SEQ], R0 + 3264)
        iota8 = at("iota8_sb", [P, 8], 106 * KB + 288)
        p_t = at("p_t", [P, TT, SEQ], R0 + 5 * KB)
        gate_s = at("gate_s", [P, TT, COLS], R0 + 7 * KB)
        gate_m = at("gate_m", [P, TT, COLS], R0 + 9 * KB)
        final_w = at("final_w", [P, D], R0 + 11 * KB)
        cu = at("cu", [P, KT, SEQ], 24 * KB)
        acv = at("acv", [P, KT, SEQ], 32 * KB)
        hc = at("hc", [P, 3 * KT, SEQ], 24 * KB)
        f_w3 = at("f_w3", [HIDDEN, ORDER * 2 * D], 48 * KB)
        dft = at("dft_sb", [P, TT, 3 * SEQ + P], 64 * KB)
        idft = at("idft_sb", [P, 2 * TT, SEQ], 71 * KB)
        f_decay = at("f_decay", [P, TT, D], 75 * KB)
        embed = at("embed_sb", [EMB, SEQ], 83 * KB)
        f_hid = at("f_hid", [HIDDEN, SEQ], 84 * KB)
        f_k = at("f_k", [HIDDEN, SEQ], 85 * KB)
        f_w1 = at("f_w1", [EMB, HIDDEN], 86 * KB)
        f_w2 = at("f_w2", [HIDDEN, HIDDEN], 86 * KB + 256)
        f_b1 = at("f_b1", [HIDDEN, 1], 86 * KB + 512)
        f_b2 = at("f_b2", [HIDDEN, 1], 86 * KB + 544)
        f_freq = at("f_freq", [HIDDEN, 1], 86 * KB + 576)
        f_rev = at("f_rev", [P, TT, HALF], 0)
        f_even = at("f_even", [P, TT, HALF], 4 * KB)
        f_odd = at("f_odd", [P, TT, HALF], 8 * KB)
        hs_re = at("hs_re", [P, TT, HALF], 12 * KB)
        hs_im = at("hs_im", [P, TT, HALF], 16 * KB)
        u_t = at("u_t", [P, TT, HALF], 20 * KB)
        hs_re2 = at("hs_re2", [P, HALF], 88 * KB)
        f_inv = at("f_inv", [P, HALF], 90 * KB)
        u_st = at("u_st", [P, KT // 2, SEQ], 92 * KB)
        ys = at("ys", [P, 2 * TT, HALF], 96 * KB)
        ys_t = at("ys_t", [P, TT, HALF], 104 * KB)
        f_abs = at("f_abs", [P, 2, TT, HALF], 96 * KB)

        proj = ctx.enter_context(nc.psum_tensor("proj", [P, RING, HALF], f32))
        acc = ctx.enter_context(nc.psum_tensor("acc", [P, TT * 2, HALF], f32))
        misc = ctx.enter_context(nc.psum_tensor("misc", [P, HALF], f32))

        scores = [acc[:, 0:2, :], acc[:, 2:4, :]]
        turned_p = [[proj[:, 0, :], proj[:, 1, :]], [proj[:, 2, :], misc[:, :]]]

        def pair(b):
            return pair_of(proj[:, b, :])

        def pair_of(bank):
            return bank.rearrange("p (a n) -> p a n", a=2)

        side = [pair(0), pair_of(misc[:, :])]

        raw_loaded = [sem(f"raw_loaded{i}") for i in range(RING)]
        hi_ready = sem("hi_ready")
        lo_pool, lo_dve = sem("lo_pool"), sem("lo_dve")
        chunk_used = sem("chunk_used")
        drained = sem("drained")
        acc_top = sem("acc_top")
        x_top = sem("x_top")
        x_loaded, x_ready = sem("x_loaded"), sem("x_ready")
        ssq_ready, inv_ready, scaled_ready = sem("ssq_ready"), sem("inv_ready"), sem("scaled_ready")
        turned, turned_read, fhi_ready, h_ready = sem("turned"), sem("turned_read"), sem("fhi_ready"), sem("h_ready")
        small = sem("small")
        ident_loaded, params_loaded = sem("ident_loaded"), sem("params_loaded")
        rows_cleared, params_turned, params_ready = sem("rows_cleared"), sem("params_turned"), sem("params_ready")
        act_chain, dve_chain, pool_chain = sem("act_chain"), sem("dve_chain"), sem("pool_chain")
        silu_ready, banks_read, hid_ready = sem("silu_ready"), sem("banks_read"), sem("hid_ready")
        out_stored = sem("out_stored")
        mixer_tables = sem("mixer_tables")
        z_ready, taps_done, conv_first, conv_done, conv_ready = (
            sem("z_ready"), sem("taps_done"), sem("conv_first"), sem("conv_done"), sem("conv_ready"))
        gates_ready, dt_summed, dt_step, dt_exped = sem("gates_ready"), sem("dt_summed"), sem("dt_step"), sem("dt_exped")
        angles, sines, rates, dA_ready, cum_summed, cum_ready = (
            sem("angles"), sem("sines"), sem("rates"), sem("dA_ready"), sem("cum_summed"), sem("cum_ready"))
        xs_turned, xs_read, cb_summed, cb_ready = sem("xs_turned"), sem("xs_read"), sem("cb_summed"), sem("cb_ready")
        cum_spread, gaps_ready, decay_ready, scores_ready = (
            sem("cum_spread"), sem("gaps_ready"), sem("decay_ready"), sem("scores_ready"))
        y_ready, y_read, y_squared, y_ssq, y_root, y_normed = (
            sem("y_ready"), sem("y_read"), sem("y_squared"), sem("y_ssq"), sem("y_root"), sem("y_normed"))
        rotated, roped, qk_scored, masked, max_ready, exped, normed = (
            sem("rotated"), sem("roped"), sem("qk_scored"), sem("masked"), sem("max_ready"), sem("exped"), sem("normed"))
        v_staged, p_turned, pt_act, pt_dve, o_ready, o_hi, o_read = (
            sem("v_staged"), sem("p_turned"), sem("pt_act"), sem("pt_dve"), sem("o_ready"), sem("o_hi"), sem("o_read"))

        router_tables, late_tables = sem("router_tables"), sem("late_tables")
        routed, comb_made, comb_turned, comb_f_ready, comb_spread, comb_act, comb_dve = (
            sem("routed"), sem("comb_made"), sem("comb_turned"), sem("comb_f_ready"), sem("comb_spread"),
            sem("comb_act"), sem("comb_dve"))
        p_low = sem("p_low")
        gaps_e, exp_e = sem("gaps_e"), sem("exp_e")
        p_turned_ple, p_split, gate_sig = sem("p_turned_ple"), sem("p_split"), sem("gate_sig")
        a_first, a_taps, a_split = sem("a_first"), sem("a_taps"), sem("a_split")
        qk_squared, qk_summed, qk_root, qk_normed = sem("qk_squared"), sem("qk_summed"), sem("qk_root"), sem("qk_normed")
        bias_loaded = [sem(f"bias_loaded{b}") for b in range(2)]
        q_staged, qk_inverted, rms_turned, rms_copied, rms_spread = (
            sem("q_staged"), sem("qk_inverted"), sem("rms_turned"), sem("rms_copied"), sem("rms_spread"))
        xdt_ready, y_gated = sem("xdt_ready"), sem("y_gated")
        hyena_tables = sem("hyena_tables")
        f_summed, f_angle, f_sine = sem("f_summed"), sem("f_angle"), sem("f_sine")
        hc_first, hc_taps = sem("hc_first"), sem("hc_taps")
        filt_summed, rev_copied, parity_ready, abs_ready, mag_ready, norm_summed, h_summed, h_scaled = (
            sem("filt_summed"), sem("rev_copied"), sem("parity_ready"), sem("abs_ready"), sem("mag_ready"),
            sem("norm_summed"), sem("h_summed"), sem("h_scaled"))
        u_staged, u_turned, ut_ready, u_summed, ys_ready, y_summed, z_made = (
            sem("u_staged"), sem("u_turned"), sem("ut_ready"), sem("u_summed"), sem("ys_ready"), sem("y_summed"), sem("z_made"))

        credited = [gaps_ready, y_gated, y_read, roped, pt_act, pt_dve, o_read, ys_ready, z_made, o_ready,
                    parity_ready, u_summed, y_summed, y_ready, qk_scored, p_turned, h_summed, abs_ready]

        block = ctx.enter_context(nc.Block())

        SCORE_COLS = {True: ((0, P), (P, SEQ)), False: ((0, SEQ), (SEQ, SEQ))}

        @block.sync
        def _(sp):
            def load(s, src, k):
                if not s.first:
                    if s.slot == POOL_SLOT:
                        sp.wait_ge(lo_pool, s.turn)
                    else:
                        sp.wait_ge(lo_dve, s.turn * (RING - 1) + (s.slot - (RING - 1)))
                dst = raw[s.slot][:, :].rearrange("p (k n) -> p k n", k=k)
                sp.dma_start(dst, src).then_inc(raw_loaded[s.slot], 16)

            def load_cols(name, w, first_col, after=()):
                view = w.rearrange("(k p) n -> p k n", p=P)
                for j, s in chunks(sp, name):
                    load(s, view[:, :, ds(j * COLS + first_col, COLS)], KT)
                    if isinstance(j, int) and j in after:
                        after[j]()

            def load_late_tables():
                sp.wait_ge(drained, DRAINED["mix_out"] + FIRST["mix_out"][1])
                for dst, src in ((p_t[:, :, :], A["p"][0, 0].rearrange("(t p) n -> p t n", p=P)),
                                 (final_w[:, :], A["final_norm_w"].partition_broadcast(P)),
                                 (na_mask[:, :], A["na_mask"]), (headones[:, :], A["headones"]), (flip[:, :], A["flip"]),
                                 (qk_gain[0:HD, 0:1], flat(A["b_q_norm_g_2"], 1)), (qk_gain[HD:P, 0:1], flat(A["b_q_norm_g_2"], 1)),
                                 (qk_gain[0:HD, 1:2], flat(A["b_k_norm_g_2"], 1)), (qk_gain[HD:P, 1:2], flat(A["b_k_norm_g_2"], 1))):
                    sp.dma_start(dst, src, allow_slow_non_contiguous=True).then_inc(late_tables, 16)

            def load_mlp(name, gate, up, down):
                c0, n = FIRST[name]
                load(Chunk(c0), gate(0), KT)
                load(Chunk(c0 + 1), up(0), KT)
                for i, c, g in mlp_rounds(sp, name):
                    load(Chunk(c, g), gate(i + 1), KT)
                    load(Chunk(c + 1, g), up(i + 1), KT)
                    load(Chunk(c + 2, g), down(i), 2)
                load(Chunk(c0 + n - 1), down(n // 3 - 1), 2)

            def load_hyena_tables():
                sp.wait_ge(drained, DRAINED["na_out"] + FIRST["na_out"][1])
                for dst, src in ((f_w3[:, :], A["c_f_w3_2"][0]), (f_w1[:, :], A["c_f_w1_2"][0]), (f_w2[:, :], A["c_f_w2_2"][0]),
                                 (f_b1[:, :], flat(A["c_f_b1_2"], 1)), (f_b2[:, :], flat(A["c_f_b2_2"], 1)),
                                 (f_freq[:, :], flat(A["c_f_freq_2"], 1)), (embed[:, :], A["embed"]),
                                 (dft[:, :, :], A["dft"].rearrange("(t p) n -> p t n", p=P)),
                                 (idft[:, :, :], A["idft"].rearrange("(t p) n -> p t n", p=P)),
                                 (f_decay[:, :, :], A["decay"].rearrange("(t p) n -> p t n", p=P))):
                    sp.dma_start(dst, src, allow_slow_non_contiguous=True).then_inc(hyena_tables, 16)

            def load_ffn(layer):
                w13 = A["f_w13_2"][layer].rearrange("(k p) n -> p k n", p=P)
                w2 = A["f_w2_2"][layer].rearrange("(k p) n -> p k n", p=P)
                load_mlp(f"ffn{layer}", lambda i: w13[:, :, ds(i * COLS, COLS)],
                         lambda i: w13[:, :, ds(i * COLS + FFN, COLS)],
                         lambda i: w2[:, ds(i * 2, 2), :])

            sp.dma_start(x[:, :, :], A["x"][0].rearrange("(t p) n -> p t n", p=P)).then_inc(x_loaded, 16)
            sp.dma_start(ident[:, :], A["ident"]).then_inc(ident_loaded, 16)

            def load_params():
                sp.wait_ge(rows_cleared, 1)
                for name, rows in PARAMS:
                    src, done = flat(A[name], P), 0
                    while done < rows:
                        tile, row = divmod(ROW[name] + done, P)
                        n = min(rows - done, P - row)
                        sp.dma_start(param_rows[row:row + n, tile, :], src[done:done + n, :]).then_inc(params_loaded, 16)
                        done += n
            load_cols("in_zx", A["w_in"][0], 0, {0: load_params})
            for dst, src in ((tri[:, :, :], A["tri"].rearrange("p (t n) -> p t n", t=TT)), (diag16[:, :], A["diag16"]),
                             (dt_bias[:, :], A["dt_bias"][0].partition_broadcast(P)),
                             (a_log_b[:, :], A["a_log"][0].partition_broadcast(P)),
                             (w_dt[:, :, :], A["w_in"][0].rearrange("(k p) n -> p k n", p=P)[:, :, DT_COL:DT_COL + HEADS]),
                             (d_col[0:HD, :], A["d_skip"][0].rearrange("(i a) -> a i", a=2)[0].partition_broadcast(HD)),
                             (d_col[HD:P, :], A["d_skip"][0].rearrange("(i a) -> a i", a=2)[1].partition_broadcast(HD)),
                             (inv_freq[:, :], A["inv_freq"]), (rot[:, :], A["rot"]), (causal[:, :], A["causal"]),
                             (pos_i[:, :], A["positions"][0].partition_broadcast(P))):
                sp.dma_start(dst, src, allow_slow_non_contiguous=True).then_inc(mixer_tables, 16)
            for dst, src in ((w_route[:, :, 0:N_GROUPS], A["w_router_group"][0].rearrange("(k p) n -> p k n", p=P)),
                             (w_route[:, :, N_GROUPS:], A["w_router_expert"][0].rearrange("(k p) n -> p k n", p=P)),
                             (b_route[:, 0:N_GROUPS], A["b_router_group"][0].partition_broadcast(P)),
                             (b_route[:, N_GROUPS:], A["b_router_expert"][0].partition_broadcast(P)),
                             (iota8[:, :], A["iota8"])):
                sp.dma_start(dst, src).then_inc(router_tables, 16)
            inner = SSD_INNER + SSD_CHANNELS + HEADS
            load_cols("in_qk", A["w_in"][0], inner)
            load_cols("in_v", A["w_in"][0], inner + 2 * D)
            load_cols("in_g", A["w_in"][0], inner + 3 * D)
            load_cols("ssd_out", A["w_ssd_out"][0], 0)
            load_cols("attn_out", A["w_attn_out"][0], 0)
            load_cols("mix_out", A["w_out"][0], 0)
            by_expert = {n: A[n][0].rearrange("g e (k p) f -> p (g e) k f", p=P)
                         for n in ("w_exp_gate", "w_exp_up", "w_exp_down")}
            load_mlp("experts", *[lambda i, v=v: v[:, ds(i, 1), :, :].rearrange("p e k f -> p (e k) f")
                                  for v in by_expert.values()])
            load_late_tables()
            load(Chunk(FIRST["ple"][0]), A["w_ple"][0].rearrange("(k p) n -> p k n", p=P), 2)
            load_cols("ple_gate", A["w_ple_gate"][0], 0)
            load_cols("a_bc0", A["a_w_in_2"][0], 0)
            load_cols("a_u0", A["a_w_in_2"][0], 2 * D)
            load_cols("a_out0", A["a_w_out_2"][0], 0)
            load_ffn(0)
            load_cols("b_qk", A["b_w_qkv_2"][0], 0)
            load_cols("b_v", A["b_w_qkv_2"][0], 2 * D)
            load_cols("na_out", A["b_w_out_2"][0], 0)
            rpb = A["b_rpb_2"]
            head, row = (2 * NA_ROWS - 1) * (2 * NA_COLS - 1), 2 * NA_COLS - 1
            with sp.Fori(0, PAIRS // 2) as ii:
                for b in range(2):
                    i = ii * 2 + b
                    sp.wait_ge(qk_scored, i + (PAIRS - 1) + CREDIT)
                    for h in range(2):
                        for r in range(SEQ // GRID_W):
                            t, half = divmod(r, 2)
                            src = bass.AP(rpb.tensor, i * (2 * head) + (h * head + (NA_ROWS - 1 - r) * row + NA_COLS - GRID_W),
                                          [[1, GRID_W], [row, SEQ // GRID_W], [1, GRID_W]])
                            dst = na_bias[b][half * GRID_W:(half + 1) * GRID_W, h, t * SEQ:(t + 1) * SEQ]
                            sp.dma_start(dst.rearrange("p (a b) -> p a b", b=GRID_W), src).then_inc(bias_loaded[b], 16)
            load_ffn(1)
            load_cols("hy_v", A["c_w_in_2"][0], 0)
            load_cols("hy_x1", A["c_w_in_2"][0], D)
            load_hyena_tables()
            load_cols("hy_x2", A["c_w_in_2"][0], 2 * D)
            load_cols("hy_out", A["c_w_out_2"][0], 0)
            load_ffn(2)
            load_cols("a_bc1", A["a_w_in_2"][1], 0)
            load_cols("a_u1", A["a_w_in_2"][1], 2 * D)
            load_cols("a_out1", A["a_w_out_2"][1], 0)
            load_ffn(3)
            sp.wait_ge(x_ready, len(X_STATES) - 1)
            sp.dma_start(out[0].rearrange("(t p) n -> p t n", p=P), x[:, :, :]).then_inc(out_stored, 16)
            sp.wait_ge(out_stored, 16)

        PARAM_DMAS = sum(len({(ROW[n] + r) // P for r in range(k)}) for n, k in PARAMS)

        @block.tensor
        def _(pe):
            def wait_parts(s):
                if s.slot == POOL_SLOT:
                    pe.wait_ge(lo_pool, s.turn + 1)
                else:
                    pe.wait_ge(lo_dve, s.turn * (RING - 1) + s.slot)

            def product_f(s, operand=None):
                hi = w_hi[s.slot][:, :].rearrange("p (k n) -> p k n", k=KT)
                lo = w_lo[s.slot][:, :].rearrange("p (k n) -> p k n", k=KT)
                for a in range(2):
                    for k in range(KT):
                        if a == 0 and operand:
                            wait_operand(operand, k)
                        for w, h in ((hi, h_hi), (hi, h_lo), (lo, h_hi)):
                            last = pe.matmul(pair(s.slot)[:, a, :], w[:, k, a * P:(a + 1) * P], h[:, k, :],
                                             start=(k == 0 and w is hi and h is h_hi),
                                             stop=(k == KT - 1 and w is lo))
                last.then_inc(chunk_used, 1)

            def product_t(s, operand=None):
                hi = w_hi[s.slot][:, :].rearrange("p (k n) -> p k n", k=KT)
                lo = w_lo[s.slot][:, :].rearrange("p (k n) -> p k n", k=KT)
                for t in range(TT):
                    for k in range(KT):
                        if t == 0 and operand:
                            wait_operand(operand, k)
                        for h, w in ((h_hi, hi), (h_hi, lo), (h_lo, hi)):
                            last = pe.matmul(pair(s.slot)[:, t, :], h[:, k, t * P:(t + 1) * P], w[:, k, :],
                                             start=(k == 0 and w is hi and h is h_hi),
                                             stop=(k == KT - 1 and h is h_lo))
                last.then_inc(chunk_used, 1)

            def project(name, product, operand, after=()):
                slot = None
                for j, s in chunks(pe, name):
                    slot = s.slot if slot is None else slot
                    wait_parts(s)
                    if isinstance(j, int) and DRAINED[name] + j < RING:
                        pass
                    else:
                        pe.wait_ge(drained, j + (DRAINED[name] - RING + 1))
                    product(s, operand if s.slot == slot else None)
                    if j in after:
                        after[j]()

            def norm_turn(operand):
                for t in range(TT):
                    pe.wait_ge(scaled_ready, TT * SQUARED.index(operand) + t + 1)
                    for k in range(KT):
                        last = pe.transpose(pair_of(acc[:, k // 2, :])[:, k % 2, t * P:(t + 1) * P],
                                            x_scaled[:, t, k * P:(k + 1) * P], ident[:, :])
                        if t == TT - 1 and k % 2:
                            last.then_inc(turned, 1)

            def wait_operand(operand, k):
                if operand in NORM_OF:
                    if k % 2 == 0:
                        pe.wait_ge(turned_read, NORM_OF[operand] * (KT // 2) + k // 2 + 1)
                elif operand.startswith("conv"):
                    if k in (0, KT - 2):
                        pe.wait_ge(a_split, 2 * int(operand[-1]) + (2 if k else 1))
                elif k == 0:
                    pe.wait_ge(h_ready, OPERANDS.index(operand) + 1)

            def sum_decays():
                pe.wait_ge(dA_ready, 1)
                for t in range(TT):
                    for s in range(t + 1):
                        pe.matmul(misc[:, 64 + t * HEADS:64 + (t + 1) * HEADS], tri[:, s, t * P:(t + 1) * P],
                                  dA[:, s, :], start=(s == 0), stop=(s == t))
                for s in range(TT):
                    last = pe.matmul(misc[0:HEADS, SEQ:2 * SEQ], dA[:, s, :], tri[:, s, :],
                                     start=(s == 0), stop=(s == TT - 1))
                last.then_inc(cum_summed, 1)

            def ssd():
                pe.wait_ge(conv_ready, 1)
                pe.wait_ge(drained, DRAINED["ssd_out"])
                for kk in range(KT // 2):
                    if kk >= RING:
                        pe.wait_ge(xs_read, kk - RING + 1)
                    for t in range(TT):
                        for a in range(2):
                            last = pe.transpose(pair(kk % RING)[:, t, a * P:(a + 1) * P],
                                                conv[:, 2 * kk + a, t * P:(t + 1) * P], ident[:, :])
                    last.then_inc(xs_turned, 1)
                for g in range(SSD_GROUPS):
                    r = slice(g * SSD_STATE, (g + 1) * SSD_STATE)
                    pe.matmul(acc[:, 2 + g, 0:SEQ], conv[r, 8, 0:P], conv[r, 9, :], start=True, stop=True)
                    last = pe.matmul(acc[:, 2 + g, SEQ:TRI], conv[r, 8, P:SEQ], conv[r, 9, P:SEQ], start=True, stop=True)
                last.then_inc(cb_summed, 1)
                pe.wait_ge(cum_ready, 1)
                n = PAIRS // 2
                with pe.Fori(0, n) as ii:
                    for u in range(2):
                        i = ii * 2 + u
                        pe.wait_ge(gaps_ready, ii * 2 + CREDIT)
                        for h in range(2):
                            last = pe.matmul(acc[:, u, h * SEQ:(h + 1) * SEQ], ones[0:HEADS, :],
                                             cum_diag[:, 2 * i + h, :], start=True, stop=True)
                        last.then_inc(cum_spread, 1)
                    for u in range(2):
                        i = ii * 2 + u
                        pe.wait_ge(scores_ready, i + 1)
                        pe.wait_ge(y_read, ii * 2 + CREDIT)
                        for h in range(2):
                            o = acc[h * HD:(h + 1) * HD, 2 + u, :]
                            pe.matmul(o[:, 0:SEQ], xdt[u][:, 0, h * HD:(h + 1) * HD], decay[u][:, h, 0:SEQ],
                                      start=True, stop=False)
                            last = pe.matmul(o[:, P:SEQ], xdt[u][:, 1, h * HD:(h + 1) * HD], decay[u][:, h, SEQ:TRI],
                                             start=False, stop=True)
                        last.then_inc(y_ready, 1)
                for g in range(SSD_GROUPS):
                    pe.wait_ge(y_squared, g + 1)
                    for a in range(4):
                        last = pe.matmul(acc[:, g, 0:SEQ], ones[:, :], sq_buf[:, a, :], start=(a == 0), stop=(a == 3))
                    last.then_inc(y_ssq, 1)

            def attention():
                pe.wait_ge(drained, DRAINED["attn_out"])
                with pe.Fori(0, PAIRS // 2) as ii:
                    for u in range(2):
                        i = ii * 2 + u
                        pe.wait_ge(pt_act, ii * 2 + CREDIT)
                        for a in range(2):
                            last = pe.matmul(turned_p[u][0][:, a * SEQ:(a + 1) * SEQ], rot[:, :],
                                             pj[:, i + (Q0 + a * KT), :], start=True, stop=True)
                        last.then_inc(rotated, 1)
                    for u in range(2):
                        i = ii * 2 + u
                        pe.wait_ge(roped, i + 1 + CREDIT)
                        pe.wait_ge(o_read, ii * 2 + CREDIT)
                        for h in range(2):
                            r = slice(h * HD, (h + 1) * HD)
                            for t, (c, n) in enumerate(SCORE_COLS[True]):
                                last = pe.matmul(scores[u][:, h, c:c + n], qk_st[u][r, 0, t * P:(t + 1) * P],
                                                 qk_st[u][r, 1, 0:n], start=True, stop=True)
                        last.then_inc(qk_scored, 1)
                    attention_out(ii, 0, True)

            def attention_out(ii, base, causal_):
                for u in range(2):
                    i = ii * 2 + u
                    pe.wait_ge(normed, i + (base + 1))
                    if not causal_:
                        pe.wait_ge(pt_act, ii * 2 + base + CREDIT)
                        pe.wait_ge(pt_dve, ii * 2 + base + CREDIT)
                    elif u == 0:
                        pe.wait_ge(pt_dve, ii * 2 + base + CREDIT)
                    for h in range(2):
                        for t, (c, n) in enumerate(SCORE_COLS[causal_]):
                            for kt in range(n // P):
                                to = t * P if kt == 0 else SEQ + (t * P if not causal_ else 0)
                                last = pe.transpose(turned_p[u][h][:, to:to + P],
                                                    probs[u][:, h, c + kt * P:c + (kt + 1) * P], ident[:, :])
                    last.then_inc(p_turned, 1)
                for u in range(2):
                    i = ii * 2 + u
                    pe.wait_ge(pt_act, i + (base + 1) + CREDIT)
                    pe.wait_ge(pt_dve, i + (base + 1) + CREDIT)
                    pe.wait_ge(v_staged, i + (base + 1))
                    for h in range(2):
                        o = scores[u][h * HD:(h + 1) * HD, 0, :]
                        pe.matmul(o[:, 0:SEQ], v_st[u][:, 0, h * HD:(h + 1) * HD], probs_t[u][:, h, 0:SEQ],
                                  start=True, stop=False)
                        q0 = P if causal_ else 0
                        last = pe.matmul(o[:, q0:SEQ], v_st[u][:, 1, h * HD:(h + 1) * HD],
                                         probs_t[u][:, h, SEQ:2 * SEQ - q0], start=False, stop=True)
                    last.then_inc(o_ready, 1)

            def down(s, start, stop):
                hi = w_hi[s.slot][:, :].rearrange("p (k n) -> p k n", k=2)
                lo = w_lo[s.slot][:, :].rearrange("p (k n) -> p k n", k=2)
                for k, t in ([(k, t) for t in range(TT) for k in range(2)] if stop else
                             [(k, t) for k in range(2) for t in range(TT)]):
                    for h, w in ((hid_hi, hi), (hid_hi, lo), (hid_lo, hi)):
                        for m in range(2):
                            last = pe.matmul(acc[:, 2 * t + m, :], h[:, k, t * P:(t + 1) * P],
                                             w[:, k, m * HALF:(m + 1) * HALF],
                                             start=(start and k == 0 and h is hid_hi and w is hi),
                                             stop=(stop and k == 1 and h is hid_lo), skip_group_check=True)
                    if stop and t == 0 and k == 1:
                        last.then_inc(acc_top, 1)
                last.then_inc(chunk_used, 1)

            def mlp(name, operand, before=None):
                c0, n = FIRST[name]
                base = ROUNDS[name]
                if before:
                    before[0]()
                for r in range(2):
                    wait_parts(Chunk(c0 + r))
                    product_f(Chunk(c0 + r), operand if r == 0 else None)
                if before:
                    before[1]()
                for t in range(TT):
                    pe.wait_ge(turned_read, (NORM_OF[operand] + 1) * (KT // 2))
                    for m in range(2):
                        pe.matmul(acc[:, 2 * t + m, :], ident[:, :], x[:, t, m * HALF:(m + 1) * HALF],
                                  start=True, stop=False, skip_group_check=True)
                for i, c, g in mlp_rounds(pe, name):
                    wait_parts(Chunk(c, g))
                    pe.wait_ge(banks_read, i + (base + 1))
                    product_f(Chunk(c, g))
                    wait_parts(Chunk(c + 1, g))
                    product_f(Chunk(c + 1, g))
                    wait_parts(Chunk(c + 2, g))
                    pe.wait_ge(hid_ready, i + (base + 1))
                    down(Chunk(c + 2, g), False, False)
                wait_parts(Chunk(c0 + n - 1))
                pe.wait_ge(hid_ready, base + n // 3)
                down(Chunk(c0 + n - 1), False, True)

            def route():
                pe.wait_ge(h_ready, OPERANDS.index("moe") + 1)
                pe.wait_ge(router_tables, 16 * ROUTER_DMAS)
                for t in range(TT):
                    for k in range(KT):
                        for h in (h_hi, h_lo):
                            last = pe.matmul(misc[:, t * NL:(t + 1) * NL], h[:, k, t * P:(t + 1) * P].bitcast(f32),
                                             w_route[:, k, :], start=(k == 0 and h is h_hi),
                                             stop=(k == KT - 1 and h is h_lo))
                last.then_inc(routed, 1)

            def spread_weights():
                pe.wait_ge(comb_made, 1)
                for t in range(TT):
                    last = pe.transpose(misc[0:EXPERTS, SEQ + t * P:SEQ + (t + 1) * P],
                                        comb_t[:, t, :, :].rearrange("p g e -> p (g e)"), ident[:, :])
                last.then_inc(comb_turned, 1)
                pe.wait_ge(comb_f_ready, 1)
                for k in range(EXPERTS // 2):
                    if k >= 4:
                        pe.wait_ge(comb_dve if k % 2 else comb_act, (k - 4) // 2 + 1)
                    for a in range(2):
                        e = 2 * k + a
                        last = pe.matmul(pair_of(acc[:, k % 4, :])[:, a, :], ident[0:EXPERTS, e:e + 1].to_broadcast([EXPERTS, P]),
                                         comb_f[:, :], start=True, stop=True)
                    last.then_inc(comb_spread, 1)
                pe.wait_ge(comb_act, EXPERTS // 4)
                pe.wait_ge(comb_dve, EXPERTS // 4)

            def sum_squares(a):
                pe.wait_ge(late_tables, 16 * LATE_DMAS)
                pe.wait_ge(qk_squared, a + 1)
                for t in range(TT):
                    for i in range(PAIRS):
                        c = (a * TT + t) * HEADS + 2 * i
                        last = pe.matmul(misc[:, c:c + 2], na_sq[:, i, t * P:(t + 1) * P], headones[:, 0:P:HD],
                                         start=True, stop=True)
                last.then_inc(qk_summed, 1)

            def turn_rms(a):
                pe.wait_ge(qk_inverted, a + 1)
                for t in range(TT):
                    o = misc[0:HEADS, SEQ + t * P:SEQ + (t + 1) * P] if a else acc[0:HEADS, 3, t * P:(t + 1) * P]
                    last = pe.transpose(o, qk_rms[:, a, t, :], ident[:, :])
                last.then_inc(rms_turned, 1)

            def spread_rms(a):
                pe.wait_ge(rms_copied, a + 1)
                if a:
                    pe.wait_ge(qk_normed, a)
                for i in range(PAIRS):
                    last = pe.matmul(pair_of(acc[:, i // 2, :])[:, i % 2, :], head_cols[:, i, :], rms_f[:, a, :],
                                     start=True, stop=True)
                last.then_inc(rms_spread, 1)

            def na_attention():
                pe.wait_ge(drained, DRAINED["na_out"])
                pe.wait_ge(qk_normed, 2)
                with pe.Fori(0, PAIRS // 2) as ii:
                    for u in range(2):
                        i = ii * 2 + u
                        pe.wait_ge(q_staged, i + 1)
                        pe.wait_ge(o_read, ii * 2 + PAIRS + CREDIT)
                        pe.wait_ge(bias_loaded[u], ii * (8 * 16) + 8 * 16)
                        for h in range(2):
                            r = slice(h * HD, (h + 1) * HD)
                            for t in range(TT):
                                o = scores[u][:, h, t * SEQ:(t + 1) * SEQ]
                                pe.matmul(o, qk_st[u][r, 0, t * P:(t + 1) * P], qk_st[u][r, 1, :], start=True, stop=False)
                                last = pe.matmul(o, flip[:, :], na_bias[u][:, h, t * SEQ:(t + 1) * SEQ],
                                                 start=False, stop=True)
                        last.then_inc(qk_scored, 1)
                    attention_out(ii, PAIRS, False)

            def filter_layer(layer):
                if layer == 0:
                    pe.wait_ge(hyena_tables, 16 * HYENA_DMAS)
                    pe.matmul(misc[0:HIDDEN, 0:SEQ], f_w1[:, :], embed[:, :], start=True, stop=True).then_inc(f_summed, 1)
                else:
                    pe.wait_ge(f_sine, 1)
                    pe.matmul(misc[0:HIDDEN, SEQ:2 * SEQ], f_w2[:, :], f_hid[:, :], start=True, stop=True).then_inc(f_summed, 1)

            def hyena():
                pe.wait_ge(f_sine, 2)
                pe.wait_ge(drained, DRAINED["hy_out"])
                with pe.Fori(0, D // HALF) as half:
                    for n in range(ORDER):
                        b = half * ORDER + n
                        for v in range(2):
                            pe.wait_ge(ys_ready, b * 2 + CREDIT)
                            for way in range(2):
                                for t in range(TT):
                                    last = pe.matmul(pair_of(acc[:, 2 * v + way, :])[:, t, :], f_hid[:, t * P:(t + 1) * P],
                                                     f_w3[:, ds(half * HALF + (2 * n + way) * D + v * COLS, COLS)],
                                                     start=True, stop=True)
                            last.then_inc(filt_summed, 1)
                        for v in range(2):
                            pe.wait_ge(u_staged, half + 1)
                            pe.wait_ge(z_made, b * 2 + CREDIT)
                            for t in range(TT):
                                for m in range(2):
                                    last = pe.transpose(pair(1 + v)[:, t, m * P:(m + 1) * P],
                                                        u_st[:, 2 * v + m, t * P:(t + 1) * P], ident[:, :])
                            last.then_inc(u_turned, 1)
                        for v in range(2):
                            cols = slice(v * COLS, (v + 1) * COLS)
                            pe.wait_ge(parity_ready, b * 2 + (v + 1) + CREDIT)
                            for bank, part_, first in [(pair_of(acc[:, 2 * v, :])[:, f, :], f_even, f * P) for f in range(TT)] + \
                                    [(pair_of(acc[:, 2 * v + 1, :])[:, f, :], f_odd, 2 * SEQ + f * P) for f in range(TT)] + \
                                    [(side[v][:, 0, :], f_even, 3 * SEQ)]:
                                for t in range(TT):
                                    last = pe.matmul(bank, dft[:, t, first:first + P], part_[:, t, cols], start=(t == 0), stop=(t == 1))
                            last.then_inc(h_summed, 1)
                        for v in range(2):
                            pe.wait_ge(mag_ready, b * 2 + (v + 1))
                            for t in range(TT):
                                last = pe.matmul(side[v][:, 1, :], ones[:, :], f_abs[:, 0, t, v * COLS:(v + 1) * COLS],
                                                 start=(t == 0), stop=(t == 1))
                            last.then_inc(norm_summed, 1)
                        for v in range(2):
                            pe.wait_ge(ut_ready, b * 2 + (v + 1))
                            pe.wait_ge(h_scaled, b * 2 + (v + 1))
                            for f in range(2 * TT):
                                for t in range(TT):
                                    last = pe.matmul(pair_of(acc[:, 2 * v + f // 2, :])[:, f % 2, :], dft[:, t, f * P:(f + 1) * P],
                                                     u_t[:, t, v * COLS:(v + 1) * COLS], start=(t == 0), stop=(t == 1))
                            last.then_inc(u_summed, 1)
                        for v in range(2):
                            pe.wait_ge(ys_ready, b * 2 + (v + 1) + CREDIT)
                            for m in range(2):
                                for f in range(2 * TT):
                                    last = pe.matmul(pair(1 + v)[:, m, :], ys[:, f, (2 * v + m) * P:(2 * v + m + 1) * P],
                                                     idft[:, f, :], start=(f == 0), stop=(f == 2 * TT - 1))
                            last.then_inc(y_summed, 1)
                pe.wait_ge(z_made, 4 * ORDER + CREDIT)

            pe.wait_ge(ident_loaded, 16)
            norm_turn("attn")
            pe.wait_ge(params_loaded, 16 * PARAM_DMAS)
            for i in range(PARAM_TILES):
                last = pe.transpose(misc[:, i * P:(i + 1) * P], param_rows[:, i, :], ident[:, :])
            last.then_inc(params_turned, 1)
            project("in_zx", product_f, "attn")
            project("in_qk", product_f, "attn")
            pe.wait_ge(mixer_tables, MIXER_DMAS * 16)
            pe.wait_ge(params_ready, 1)
            for t in range(TT):
                for k in range(KT):
                    for h in (h_hi, h_lo):
                        last = pe.matmul(misc[:, t * HEADS:(t + 1) * HEADS],
                                         h[:, k, t * P:(t + 1) * P].bitcast(f32), w_dt[:, k, :],
                                         start=(k == 0 and h is h_hi), stop=(k == KT - 1 and h is h_lo))
            last.then_inc(dt_summed, 1)
            project("in_v", product_t, "attn")
            sum_decays()
            project("in_g", product_f, "attn")
            ssd()
            project("ssd_out", product_f, "ssd")
            attention()
            project("attn_out", product_f, "attention")
            project("mix_out", product_t, "merged")
            norm_turn("moe")
            mlp("experts", "moe", (route, spread_weights))
            norm_turn("ple")
            pe.wait_ge(late_tables, 16 * LATE_DMAS)
            for a in range(2):
                for t in range(TT):
                    last = pe.transpose(misc[:, a * SEQ + t * P:a * SEQ + (t + 1) * P],
                                        p_t[:, t, a * P:(a + 1) * P], ident[:, :])
            last.then_inc(p_turned_ple, 1)
            s = Chunk(FIRST["ple"][0])
            wait_parts(s)
            pe.wait_ge(p_low, 1)
            down(s, True, True)
            project("ple_gate", product_t, "ple")
            norm_turn("mix0")
            project("a_bc0", product_f, "mix0")
            project("a_u0", product_f, "mix0")
            project("a_out0", product_t, "conv0")
            norm_turn("ffn0")
            mlp("ffn0", "ffn0")
            norm_turn("mix1")
            project("b_qk", product_f, "mix1")
            project("b_v", product_t, "mix1", {
                0: lambda: sum_squares(0), 1: lambda: (turn_rms(0), sum_squares(1)),
                2: lambda: (spread_rms(0), turn_rms(1)), 3: lambda: spread_rms(1)})
            na_attention()
            project("na_out", product_t, "na")
            norm_turn("ffn1")
            mlp("ffn1", "ffn1")
            norm_turn("mix2")
            project("hy_v", product_f, "mix2")
            project("hy_x1", product_f, "mix2")
            project("hy_x2", product_f, "mix2", {0: lambda: filter_layer(0), 2: lambda: filter_layer(1)})
            hyena()
            project("hy_out", product_t, "hyena")
            norm_turn("ffn2")
            mlp("ffn2", "ffn2")
            norm_turn("mix3")
            project("a_bc1", product_f, "mix3")
            project("a_u1", product_f, "mix3")
            project("a_out1", product_t, "conv1")
            norm_turn("ffn3")
            mlp("ffn3", "ffn3")

        @block.gpsimd
        def _(pool):
            chain = Chain(pool, pool_chain)

            def part(s):
                if s.more and s.slot == POOL_SLOT:
                    low(s.ahead())

            def low(n):
                pool.wait_ge(hi_ready, n.c + 1)
                pool.tensor_tensor(w_lo[n.slot][:, :], raw[n.slot][:, :], w_hi[n.slot][:, :].bitcast(f32), SUB)\
                    .then_inc(lo_pool, 1)

            def parts(name, after=()):
                for j, s in chunks(pool, name):
                    if not in_norm(name, j):
                        part(s)
                    if j in after:
                        after[j]()

            def parts_mlp(name):
                c0, n = FIRST[name]
                part(Chunk(c0))
                part(Chunk(c0 + 1))
                for i, c, g in mlp_rounds(pool, name):
                    for r in range(3):
                        part(Chunk(c + r, g))

            def norm_root(operand):
                n = SQUARED.index(operand)
                for t in range(TT):
                    pool.wait_ge(ssq_ready, TT * n + t + 1)
                    if n:
                        pool.wait_ge(scaled_ready, TT * n)
                    chain.link(pool.tensor_scalar(ms[:, t:t + 1], ssq[:, t:t + 1], 1.0 / D, EPS, MUL, ADD))
                    pool.tensor_tensor(inv[:, t:t + 1], ms[:, t:t + 1], neg_half[:, t:t + 1], ALU.pow).then_inc(inv_ready, 1)
                if operand in BEFORE:
                    part(last_chunk(BEFORE[operand]))

            pool.memset(param_rows[:, :, :], 0.0).then_inc(rows_cleared, 1)
            for s in credited:
                pool.sem_inc(s, CREDIT)
            pool.memset(neg_half[:, :], -0.5).then_inc(small, 1)
            pool.memset(ones[:, :], 1.0).then_inc(small, 1)
            pool.memset(eps_col[:, :], EPS).then_inc(small, 1)
            pool.wait_ge(small, 3)
            norm_root("attn")
            low(Chunk(POOL_SLOT))
            parts("in_zx")
            parts("in_qk")
            parts("in_v")
            parts("in_g")
            parts("ssd_out")
            parts("attn_out")
            parts("mix_out")
            norm_root("moe")
            parts_mlp("experts")
            norm_root("ple")
            parts("ple")
            parts("ple_gate")
            norm_root("final")
            norm_root("mix0")
            parts("a_bc0")
            parts("a_u0")
            parts("a_out0")
            norm_root("ffn0")
            parts_mlp("ffn0")
            norm_root("mix1")
            parts("b_qk")

            parts("b_v")
            parts("na_out")
            norm_root("ffn1")
            parts_mlp("ffn1")
            norm_root("mix2")
            parts("hy_v")
            parts("hy_x1")
            parts("hy_x2")
            parts("hy_out")
            norm_root("ffn2")
            parts_mlp("ffn2")
            norm_root("mix3")
            parts("a_bc1")
            parts("a_u1")
            parts("a_out1")
            norm_root("ffn3")
            parts_mlp("ffn3")

        @block.scalar
        def _(act):
            def part(s):
                if s.more:
                    act.wait_ge(chunk_used, s.c + 1)
                    high(s.ahead())

            def high(n):
                act.wait_ge(raw_loaded[n.slot], (n.turn + 1) * 16)
                act.activation(w_hi[n.slot][:, :], raw[n.slot][:, :], ACT.Copy).then_inc(hi_ready, 1)

            def parts(name, after=(), urgent=False):
                for j, s in chunks(act, name):
                    if urgent and j in after:
                        after[j]()
                    if not in_norm(name, j):
                        part(s)
                    if not urgent and j in after:
                        after[j]()

            def norm(operand):
                n = NORM_OF[operand]
                state, gain, row = X_STATES.index(NORMS[n][1]), NORMS[n][2], NORMS[n][3]
                squares(SQUARED.index(operand), state)
                if n == 0:
                    high(Chunk(0))
                    act.wait_ge(params_ready, 1)
                for kk in range(KT // 2):
                    act.wait_ge(turned, n * (KT // 2) + kk + 1)
                    for a in range(2):
                        col = ROW[gain] + row + 2 * kk + a
                        act.activation(h_hi[:, 2 * kk + a, :], pair_of(acc[:, kk, :])[:, a, :], ACT.Copy,
                                       scale=params[:, col:col + 1]).then_inc(fhi_ready, 1)
                if n == 0:
                    for c in range(1, RING):
                        high(Chunk(c))

            def squares(n, state):
                if state == 0:
                    act.wait_ge(x_loaded, 16)
                elif X_STATES[state] not in GATED:
                    act.wait_ge(x_ready, state)
                if n:
                    act.wait_ge(inv_ready, TT * n)
                for t in range(TT):
                    if X_STATES[state] in GATED:
                        act.wait_ge(x_ready if t else x_top, state if t else GATED.index(X_STATES[state]) + 1)
                    if t or n:
                        act.wait_ge(ssq_ready, TT * n + t)
                    act.activation(x_scaled[:, t, :], x[:, t, :], ACT.Square, accum_out=ssq[:, t:t + 1])\
                        .then_inc(ssq_ready, 1)
                if SQUARED[n] in BEFORE:
                    part(last_chunk(BEFORE[SQUARED[n]]))

            def softmax_exp(ii, base, causal_):
                for u in range(2):
                    act.wait_ge(max_ready, ii * 2 + (base + u + 1))
                    for h in range(2):
                        for t, (c, n) in enumerate(SCORE_COLS[causal_]):
                            act.activation(probs[u][:, h, c:c + n], probs[u][:, h, c:c + n], ACT.Exp,
                                           bias=at_max[u][:, h, t:t + 1], accum_out=at_sum[u][:, h, t:t + 1]).then_inc(exped, 1)
                n = TRI if causal_ else 2 * SEQ
                for u in range(2):
                    act.wait_ge(p_turned, ii * 2 + (base + u + 1) + CREDIT)
                    act.activation(probs_t[u][:, 0, 0:n], turned_p[u][0][:, 0:n], ACT.Copy).then_inc(pt_act, 1)
                for u in range(2):
                    act.wait_ge(o_ready, ii * 2 + (base + u + 1) + CREDIT)
                    act.activation(h_hi[:, ii * 2 + u, :], scores[u][:, 0, 0:SEQ], ACT.Copy).then_inc(o_hi, 1)

            def stage_v(ii, u, base):
                act.wait_ge(o_ready, ii * 2 + base + CREDIT)
                act.activation(v_st[u][:, :, :], v_t[:, :, ds((ii * 2 + u) * P, P)], ACT.Copy).then_inc(v_staged, 1)

            def silu_gate(base, i, c):
                act.wait_ge(chunk_used, c.c + 1)
                if not (isinstance(i, int) and base + i == 0):
                    act.wait_ge(banks_read, i + base)
                act.activation(silu_g[:, :], proj[:, c.slot, :], ACT.Silu).then_inc(silu_ready, 1)

            def parts_mlp(name):
                c0, n = FIRST[name]
                base = ROUNDS[name]
                silu_gate(base, 0, Chunk(c0))
                part(Chunk(c0))
                part(Chunk(c0 + 1))
                for i, c, g in mlp_rounds(act, name):
                    silu_gate(base, i + 1, Chunk(c, g))
                    for r in range(3):
                        part(Chunk(c + r, g))

            def short_conv(layer):
                def tap(j):
                    act.wait_ge(drained, DRAINED[f"a_u{layer}"] + j + 1)
                    for m in (2 * j, 2 * j + 1):
                        col = ROW["a_conv_w_2"] + (layer * 3 + 1) * KT + m
                        act.activation(acv[:, m, :], cu[:, m, :], ACT.Copy, scale=params[:, col:col + 1]).then_inc(a_first, 1)
                return {j: lambda j=j: tap(j) for j in range(KT // 2)}

            def hyena_tap(first, end):
                act.wait_ge(drained, DRAINED["hy_v"] + end // 2)
                w, b0 = ROW["c_short_w_2"] + 3 * KT, ROW["c_short_b_2"]
                with act.Fori(first, end) as m:
                    act.activation(hc[:, ds(m, 1), :].rearrange("p o n -> p (o n)"),
                                   pj[:, ds(m, 1), :].rearrange("p o n -> p (o n)"), ACT.Identity,
                                   bias=params[:, ds(m + b0, 1)], scale=params[:, ds(m + w, 1)]).then_inc(hc_first, 1)

            def filter_sine(layer):
                act.wait_ge(f_angle, layer + 1)
                act.activation(f_hid[:, :], f_hid[:, :], ACT.Sin).then_inc(f_sine, 1)

            def hyena_scalar():
                act.wait_ge(hc_taps, 6 * KT)
                with act.Fori(0, D // HALF) as half:
                    for n in range(ORDER):
                        b = half * ORDER + n
                        if n == 0:
                            act.wait_ge(z_made, b * 2 + CREDIT)
                            act.activation(u_st[:, :, :], hc[:, ds(half * (KT // 2), KT // 2), :], ACT.Copy).then_inc(u_staged, 1)
                        for v in range(2):
                            act.wait_ge(filt_summed, b * 2 + (v + 1))
                            act.wait_ge(parity_ready, b * 2 + CREDIT)
                            act.activation(f_rev[:, :, v * COLS:(v + 1) * COLS], pair_of(acc[:, 2 * v + 1, :]), ACT.Copy)\
                                .then_inc(rev_copied, 1)
                        for v in range(2):
                            act.wait_ge(u_turned, b * 2 + (v + 1))
                            act.wait_ge(u_summed, b * 2 + CREDIT)
                            act.activation(u_t[:, :, v * COLS:(v + 1) * COLS], pair(1 + v), ACT.Copy).then_inc(ut_ready, 1)
                        for v in range(2):
                            cols = slice(v * COLS, (v + 1) * COLS)
                            act.wait_ge(parity_ready, b * 2 + (v + 1) + CREDIT)
                            act.wait_ge(y_summed, b * 2 + CREDIT)
                            act.activation(f_abs[:, 0, :, cols], f_even[:, :, cols], ACT.Abs).then_inc(abs_ready, 1)
                            act.activation(f_abs[:, 1, :, cols], f_odd[:, :, cols], ACT.Abs).then_inc(abs_ready, 1)

            norm("attn")
            parts("in_zx")
            parts("in_qk")
            act.wait_ge(mixer_tables, MIXER_DMAS * 16)
            act.activation(a_rate[:, :], a_log_b[:, :], ACT.Exp).then_inc(dt_exped, 1)
            act.wait_ge(dt_step, 2)
            act.activation(dt_u[:, :, :], dt_n[:, :, :], ACT.Exp, scale=-1.0).then_inc(dt_exped, 1)
            act.wait_ge(dt_step, 3)
            act.activation(dt_l[:, :, :], dt_w[:, :, :], ACT.Ln).then_inc(dt_exped, 1)
            act.wait_ge(drained, DRAINED["in_qk"])
            w0, b0 = ROW["conv_w"] + 3 * XBC_TILES, ROW["conv_b"]
            for m in range(XBC_TILES):
                act.activation(conv[:, m, :], pj[:, XBC0 + m, :], ACT.Identity, bias=params[:, b0 + m:b0 + m + 1],
                               scale=params[:, w0 + m:w0 + m + 1]).then_inc(conv_first, 1)
            parts("in_v")
            act.wait_ge(taps_done, 3 * XBC_TILES)
            act.activation(conv[:, :, :], conv[:, :, :], ACT.Silu).then_inc(conv_ready, 1)
            act.activation(pj[:, Z0:Z0 + KT, :], pj[:, Z0:Z0 + KT, :], ACT.Silu).then_inc(z_ready, 1)
            for dst, scale in ((sin_f, 1.0), (cos_f, 0.5)):
                act.wait_ge(angles, 1)
                act.activation(dst[:, :], ang[:, :], ACT.Sin, scale=scale).then_inc(sines, 1)
            parts("in_g")
            act.wait_ge(drained, DRAINED["ssd_out"])
            act.activation(pj[:, GS0:GS0 + 2 * KT, :], pj[:, GS0:GS0 + 2 * KT, :], ACT.Sigmoid).then_inc(gates_ready, 1)
            with act.Fori(0, PAIRS // 2) as ii:
                for u in range(2):
                    act.wait_ge(gaps_ready, ii * 2 + (u + 1) + CREDIT)
                    act.activation(decay[u][:, :, :], decay[u][:, :, :], ACT.Exp).then_inc(decay_ready, 1)
            for g in range(SSD_GROUPS):
                if g:
                    act.wait_ge(y_ssq, g)
                else:
                    act.wait_ge(y_gated, PAIRS + CREDIT)
                act.activation(sq_buf[:, :, :], pj[:, Z0 + 4 * g:Z0 + 4 * g + 4, :], ACT.Square).then_inc(y_squared, 1)
                act.wait_ge(y_ssq, g + 1)
                if g:
                    act.wait_ge(y_normed, g)
                act.activation(rstd[:, :], acc[:, g, 0:SEQ], ACT.Sqrt, bias=eps_col[:, 0:1],
                               scale=1.0 / (SSD_INNER // SSD_GROUPS)).then_inc(y_root, 1)
            parts("ssd_out")
            with act.Fori(0, PAIRS // 2) as ii:
                for u in range(2):
                    stage_v(ii, u, 0)
                softmax_exp(ii, 0, True)
            parts("attn_out")
            parts("mix_out")
            norm("moe")
            for t in range(TT):
                act.wait_ge(gaps_e, 1)
                act.activation(g_exp[:, t, :], logits[:, t, 0:N_GROUPS], ACT.Exp, bias=g_neg[:, t:t + 1],
                               accum_out=g_sum[:, t:t + 1]).then_inc(exp_e, 1)
            act.wait_ge(gaps_e, 2)
            act.activation(e_exp[:, :], e_gap[:, :], ACT.Exp).then_inc(exp_e, 1)
            for k in range(0, EXPERTS // 2, 2):
                act.wait_ge(comb_spread, k + 1)
                act.activation(comb[:, 2 * k:2 * k + 2, :], pair_of(acc[:, k % 4, :]), ACT.Copy).then_inc(comb_act, 1)
            parts_mlp("experts")
            norm("ple")
            act.wait_ge(p_turned_ple, 1)
            act.activation(hid_hi[:, :, :], misc[:, :].rearrange("p (a n) -> p a n", a=2), ACT.Copy).then_inc(p_split, 1)
            parts("ple")
            for j, s in chunks(act, "ple_gate"):
                act.wait_ge(chunk_used, s.c + 1)
                act.wait_ge(drained, j + DRAINED["ple_gate"])
                act.activation(gate_s[:, :, :], pair(s.slot), ACT.Sigmoid).then_inc(gate_sig, 1)
                if not in_norm("ple_gate", j):
                    part(s)
            squares(SQUARED.index("final"), X_STATES.index("ple"))
            norm("mix0")
            parts("a_bc0")
            parts("a_u0", short_conv(0), urgent=True)
            parts("a_out0")
            norm("ffn0")
            parts_mlp("ffn0")
            norm("mix1")
            parts("b_qk")
            def square(a):
                if a:
                    act.wait_ge(qk_summed, a)
                act.activation(na_sq[:, :, :], pj[:, a * KT:(a + 1) * KT, :], ACT.Square).then_inc(qk_squared, 1)

            def root(a):
                act.wait_ge(qk_summed, a + 1)
                act.activation(qk_rms[:, a, :, :], misc[:, a * TT * HEADS:(a + 1) * TT * HEADS].rearrange("p (t h) -> p t h", t=TT),
                               ACT.Sqrt, bias=eps_col[:, 0:1], scale=1.0 / HD).then_inc(qk_root, 1)

            def copy_rms(a):
                act.wait_ge(rms_turned, a + 1)
                act.activation(rms_f[:, a, :], misc[0:HEADS, SEQ:2 * SEQ] if a else acc[0:HEADS, 3, 0:SEQ], ACT.Copy)\
                    .then_inc(rms_copied, 1)
            act.wait_ge(drained, DRAINED["b_v"])
            square(0)
            parts("b_v", {0: lambda: (root(0), square(1)), 1: lambda: (copy_rms(0), root(1)), 2: lambda: copy_rms(1)})
            act.wait_ge(drained, DRAINED["na_out"])
            act.wait_ge(late_tables, 16 * LATE_DMAS)
            act.wait_ge(qk_normed, 2)
            with act.Fori(0, PAIRS // 2) as ii:
                for u in range(2):
                    i = ii * 2 + u
                    act.wait_ge(qk_scored, ii * 2 + PAIRS + CREDIT)
                    act.activation(qk_st[u][:, :, :], pj[:, 0:2 * KT, :].rearrange("p (a e) n -> p a e n", a=2)[:, :, i, :],
                                   ACT.Copy).then_inc(q_staged, 1)
                for u in range(2):
                    stage_v(ii, u, PAIRS)
                softmax_exp(ii, PAIRS, False)
            parts("na_out")
            norm("ffn1")
            parts_mlp("ffn1")
            norm("mix2")
            parts("hy_v")
            hyena_tap(0, KT)
            parts("hy_x1")
            hyena_tap(KT, 2 * KT)

            def rest(j):
                hyena_tap(2 * KT + 2 * j, 2 * KT + 2 * j + 2)
                if j in (0, 2):
                    filter_sine(j // 2)
            parts("hy_x2", {j: lambda j=j: rest(j) for j in range(KT // 2)})
            hyena_scalar()
            parts("hy_out")
            norm("ffn2")
            parts_mlp("ffn2")
            norm("mix3")
            parts("a_bc1")
            parts("a_u1", short_conv(1), urgent=True)
            parts("a_out1")
            norm("ffn3")
            parts_mlp("ffn3")

        @block.vector
        def _(dve):
            chain = Chain(dve, dve_chain)
            link = chain.link

            def part(s):
                if s.more and s.slot != POOL_SLOT:
                    low(s.ahead())

            def low(n):
                dve.wait_ge(hi_ready, n.c + 1)
                dve.tensor_tensor(w_lo[n.slot][:, :], raw[n.slot][:, :], w_hi[n.slot][:, :].bitcast(f32), SUB)\
                    .then_inc(lo_dve, 1)

            def drain(name, read, after=(), urgent=False):
                for j, s in chunks(dve, name):
                    dve.wait_ge(chunk_used, s.c + 1)
                    read(j, pair(s.slot), s).then_inc(drained, 1)
                    if urgent and j in after:
                        after[j]()
                    if not in_norm(name, j):
                        part(s)
                    if not urgent and j in after:
                        after[j]()

            def drain_to(name, tile):
                drain(name, lambda j, bank, s: dve.tensor_copy(pj[:, ds(j * 2 + tile, 2), :], bank))

            def drain_x(name):
                def read(j, bank, s):
                    xs = x[:, :, ds(j * COLS, COLS)]
                    return dve.tensor_tensor(xs, xs, bank, ADD)
                drain(name, read)
                dve.wait_ge(drained, DRAINED[name] + FIRST[name][1])
                signal(x_ready)

            def signal(s):
                dve.engine_nop().then_inc(s, 1)

            def scale_x(operand):
                n = SQUARED.index(operand)
                for t in range(TT):
                    dve.wait_ge(inv_ready, TT * n + t + 1)
                    dve.tensor_scalar(x_scaled[:, t, :], x[:, t, :], inv[:, t:t + 1], None, MUL).then_inc(scaled_ready, 1)

            def norm(operand):
                n = NORM_OF[operand]
                gain, row = NORMS[n][2], NORMS[n][3]
                scale_x(operand)
                if operand in BEFORE:
                    part(last_chunk(BEFORE[operand]))
                if n == 0:
                    dve.wait_ge(params_turned, 1)
                    dve.tensor_copy(params[:, :], misc[:, 0:PARAM_TILES * P]).then_inc(params_ready, 1)
                    dve.wait_ge(params_ready, 1)
                for kk in range(KT // 2):
                    for a in range(2):
                        k = 2 * kk + a
                        col = ROW[gain] + row + k
                        dve.wait_ge(fhi_ready, n * KT + 2 * kk + 2)
                        last = dve.scalar_tensor_tensor(out=h_lo[:, k, :], in0=pair_of(acc[:, kk, :])[:, a, :],
                                                        scalar=params[:, col:col + 1], in1=h_hi[:, k, :].bitcast(f32),
                                                        op0=MUL, op1=SUB)
                        if a:
                            last.then_inc(turned_read, 1)
                dve.wait_ge(turned_read, (n + 1) * (KT // 2))
                signal(h_ready)
                if n == 0:
                    for c in range(RING):
                        if c != POOL_SLOT:
                            low(Chunk(c))

            def split_h(src, tiles=KT):
                link(dve.tensor_copy(h_hi[:, 0:tiles, :], src))
                link(dve.tensor_tensor(h_lo[:, 0:tiles, :], src, h_hi[:, 0:tiles, :].bitcast(f32), SUB))
                signal(h_ready)

            norm("attn")
            drain_to("in_zx", 0)
            drain_to("in_qk", Q0)
            dve.wait_ge(mixer_tables, MIXER_DMAS * 16)
            dve.wait_ge(dt_summed, 1)
            dve.tensor_tensor(dt_x[:, :, :], misc[:, 0:TT * HEADS].rearrange("p (t h) -> p t h", t=TT),
                              dt_bias[:, :].unsqueeze(1).to_broadcast([P, TT, HEADS]), ADD).then_inc(dt_step, 1)
            dve.wait_ge(dt_step, 1)
            dve.scalar_tensor_tensor(out=dt_n[:, :, :], in0=dt_x[:, :, :], scalar=-1.0, in1=dt_x[:, :, :],
                                     op0=MUL, op1=ALU.max).then_inc(dt_step, 1)
            dve.wait_ge(dt_exped, 2)
            dve.tensor_scalar(dt_w[:, :, :], dt_u[:, :, :], 1.0, None, ADD).then_inc(dt_step, 1)
            dve.wait_ge(dt_step, 3)
            link(dve.tensor_scalar(dt_r[:, :, :], dt_w[:, :, :], -1.0, 1e-30, ADD, ADD))
            link(dve.reciprocal(dt_r[:, :, :], dt_r[:, :, :]))
            link(dve.tensor_tensor(dt_r[:, :, :], dt_r[:, :, :], dt_u[:, :, :], MUL))
            dve.wait_ge(dt_exped, 3)
            link(dve.tensor_scalar(dt_n[:, :, :], dt_l[:, :, :], 1e-30, None, ADD))
            link(dve.tensor_tensor(dt_r[:, :, :], dt_r[:, :, :], dt_n[:, :, :], MUL))
            link(dve.scalar_tensor_tensor(out=dt_t[:, :, :], in0=dt_x[:, :, :], scalar=0.0, in1=dt_r[:, :, :],
                                          op0=ALU.max, op1=ADD))
            dve.scalar_tensor_tensor(out=dA[:, :, :], in0=dt_t[:, :, :], scalar=-1.0,
                                     in1=a_rate[:, :].unsqueeze(1).to_broadcast([P, TT, HEADS]),
                                     op0=MUL, op1=MUL).then_inc(dA_ready, 1)
            for shift in range(1, SSD_TAPS):
                w = ROW["conv_w"] + (SSD_TAPS - 1 - shift) * XBC_TILES
                for m in range(XBC_TILES):
                    dve.wait_ge(conv_first, m + 1)
                    if shift > 1:
                        dve.wait_ge(taps_done, (shift - 2) * XBC_TILES + m + 1)
                    dve.scalar_tensor_tensor(out=conv[:, m, shift:], in0=pj[:, XBC0 + m, 0:SEQ - shift],
                                             scalar=params[:, w + m:w + m + 1], in1=conv[:, m, shift:],
                                             op0=MUL, op1=ADD).then_inc(taps_done, 1)
            drain("in_v", lambda j, bank, s: dve.tensor_copy(v_t[:, :, ds(j * COLS, COLS)], bank))
            dve.wait_ge(cum_summed, 1)
            link(dve.tensor_copy(cum_t[:, :, :], misc[:, 64:64 + TT * HEADS].rearrange("p (t h) -> p t h", t=TT)))
            link(dve.tensor_copy(cum_f[:, :], misc[0:HEADS, SEQ:2 * SEQ]))
            dve.tensor_tensor(cum_diag[:, :, :], cum_f[:, :].unsqueeze(1).to_broadcast([HEADS, HEADS, SEQ]),
                              diag16[:, :].unsqueeze(2).to_broadcast([HEADS, HEADS, SEQ]), MUL).then_inc(cum_ready, 1)
            dve.tensor_copy(ang_k[:, :], pos_i[:, :]).then_inc(dve_chain, 1)
            chain.count += 1
            dve.wait_ge(dve_chain, chain.count)
            link(dve.tensor_scalar(ang[:, :], ang_k[:, :], inv_freq[:, 0:1], None, MUL))
            reduce_angle(dve, link, ang[:, :], ang_k[:, :])
            signal(angles)
            drain_to("in_g", GS0)
            dve.wait_ge(sines, 2)
            link(dve.tensor_tensor(cos_f[:, :], cos_f[:, :], cos_f[:, :], MUL))
            link(dve.tensor_scalar(cos_f[:, :], cos_f[:, :], -2.0, 1.0, MUL, ADD))
            for kk in range(KT // 2):
                dve.wait_ge(xs_turned, kk + 1)
                dve.tensor_copy(xs_t[:, :, kk * COLS:(kk + 1) * COLS], pair(kk % RING)).then_inc(xs_read, 1)
            dve.wait_ge(cb_summed, 1)
            for g in range(SSD_GROUPS):
                link(dve.tensor_tensor(cb[:, g, 0:SEQ], acc[:, 2 + g, 0:SEQ], tri[:, 0, :], MUL))
                link(dve.tensor_tensor(cb[:, g, SEQ:TRI], acc[:, 2 + g, SEQ:TRI], tri[:, 1, P:SEQ], MUL))
            dve.wait_ge(xs_read, KT // 2)
            dve.wait_ge(z_ready, 1)
            for g in range(SSD_GROUPS):
                n = PAIRS // SSD_GROUPS // 2
                with dve.Fori(g * n, (g + 1) * n) as ii:
                    for u in range(2):
                        i = ii * 2 + u
                        dve.wait_ge(y_ready, ii * 2 + CREDIT)
                        dve.tensor_tensor(xdt[u][:, :, :].rearrange("p t (h c) -> p t h c", h=2),
                                          xs_t[:, :, ds(i * P, P)].rearrange("p t (h c) -> p t h c", h=2),
                                          dt_t[:, :, ds(i * 2, 2)].unsqueeze(3).to_broadcast([P, TT, 2, HD]), MUL)\
                            .then_inc(xdt_ready, 1)
                    for u in range(2):
                        i = ii * 2 + u
                        dve.wait_ge(cum_spread, i + 1)
                        for h in range(2):
                            for t, (a, b, q0) in enumerate(((0, SEQ, 0), (SEQ, TRI, P))):
                                last = dve.tensor_scalar(decay[u][:, h, a:b], acc[:, u, h * SEQ + q0:(h + 1) * SEQ],
                                                         cum_t[:, t, ds(i * 2 + h, 1)], 0.0, SUB, ALU.min)
                        last.then_inc(gaps_ready, 1)
                    for u in range(2):
                        i = ii * 2 + u
                        dve.wait_ge(decay_ready, i + 1)
                        dve.wait_ge(xdt_ready, i + 1)
                        dve.tensor_tensor(decay[u][:, :, :], decay[u][:, :, :],
                                          cb[:, g, :].unsqueeze(1).to_broadcast([P, 2, TRI]), MUL).then_inc(scores_ready, 1)
                    for u in range(2):
                        i = ii * 2 + u
                        dve.wait_ge(y_ready, i + 1 + CREDIT)
                        dve.wait_ge(y_gated, i + CREDIT)
                        dve.scalar_tensor_tensor(out=y_sum[:, :], in0=conv[:, i, :], scalar=d_col[:, ds(i, 1)],
                                                 in1=acc[:, 2 + u, 0:SEQ], op0=MUL, op1=ADD).then_inc(y_read, 1)
                        dve.wait_ge(y_read, i + 1 + CREDIT)
                        dve.tensor_tensor(pj[:, i, :], pj[:, i, :], y_sum[:, :], MUL).then_inc(y_gated, 1)
            for g in range(SSD_GROUPS):
                dve.wait_ge(y_gated, PAIRS + CREDIT)
                dve.wait_ge(y_root, g + 1)
                link(dve.reciprocal(rstd[:, :], rstd[:, :]))
                for a in range(4):
                    col = ROW["ssd_norm_w"] + 4 * g + a
                    last = dve.scalar_tensor_tensor(out=ynorm[:, a, :], in0=pj[:, 4 * g + a, :],
                                                    scalar=params[:, col:col + 1], in1=rstd[:, :],
                                                    op0=MUL, op1=MUL)
                last.then_inc(y_normed, 1)
                dve.wait_ge(y_normed, g + 1)
                link(dve.tensor_copy(h_hi[:, 4 * g:4 * g + 4, :], ynorm[:, :, :]))
                link(dve.tensor_tensor(h_lo[:, 4 * g:4 * g + 4, :], ynorm[:, :, :],
                                       h_hi[:, 4 * g:4 * g + 4, :].bitcast(f32), SUB))
            signal(h_ready)
            dve.wait_ge(gates_ready, 1)
            drain("ssd_out", lambda j, bank, s: dve.tensor_tensor(
                pj[:, ds(j * 2, 2), :], bank, pj[:, ds(j * 2 + GS0, 2), :], MUL))

            def softmax_rows(ii, base, causal_):
                cols = SCORE_COLS[causal_]
                for u in range(2):
                    i = ii * 2 + u
                    dve.wait_ge(qk_scored, i + (base + 1) + CREDIT)
                    dve.wait_ge(p_turned, ii * 2 + base + CREDIT)
                    if causal_:
                        dve.scalar_tensor_tensor(out=probs[u][:, :, 0:TRI], in0=scores[u][:, :, 0:TRI], scalar=HD ** -0.5,
                                                 in1=causal[:, :].unsqueeze(1).to_broadcast([P, 2, TRI]),
                                                 op0=MUL, op1=ADD).then_inc(masked, 1)
                    else:
                        dve.tensor_tensor(probs[u][:, :, :], scores[u],
                                          na_mask[:, :].unsqueeze(1).to_broadcast([P, 2, TT * SEQ]), ADD).then_inc(masked, 1)
                    dve.wait_ge(masked, i + (base + 1))
                    if causal_:
                        for t, (c, n) in enumerate(cols):
                            last = dve.tensor_reduce(at_max[u][:, :, t:t + 1].rearrange("p h o -> p (h o)"),
                                                     probs[u][:, :, c:c + n], AX.X, ALU.max, negate=True)
                    else:
                        last = dve.tensor_reduce(at_max[u][:, :, :], probs[u][:, :, :].rearrange("p h (t k) -> p h t k", t=TT),
                                                 AX.X, ALU.max, negate=True)
                    last.then_inc(max_ready, 1)
                for u in range(2):
                    dve.wait_ge(exped, ii * 8 + (base * 4 + 4 * u + 4))
                    link(dve.reciprocal(at_inv[u][:, :, :], at_sum[u][:, :, :]))
                    for h in range(2):
                        for t, (c, n) in enumerate(cols):
                            last = dve.tensor_scalar(probs[u][:, h, c:c + n], probs[u][:, h, c:c + n],
                                                     at_inv[u][:, h, t:t + 1], None, MUL)
                    last.then_inc(normed, 1)
                n = TRI if causal_ else 2 * SEQ
                for u in range(2):
                    dve.wait_ge(p_turned, ii * 2 + (base + u + 1) + CREDIT)
                    dve.tensor_copy(probs_t[u][:, 1, 0:n], turned_p[u][1][:, 0:n]).then_inc(pt_dve, 1)
                for u in range(2):
                    i = ii * 2 + u
                    dve.wait_ge(o_hi, i + (base + 1))
                    dve.tensor_tensor(h_lo[:, i, :], scores[u][:, 0, 0:SEQ], h_hi[:, i, :].bitcast(f32), SUB).then_inc(o_read, 1)

            with dve.Fori(0, PAIRS // 2) as ii:
                chain.begin(ii, 6)
                for u in range(2):
                    i = ii * 2 + u
                    qk = pj[:, Q0:Q0 + 2 * KT, :].rearrange("p (a e) n -> p a e n", a=2)[:, :, i, :]
                    dve.wait_ge(roped, i + CREDIT)
                    link(dve.tensor_tensor(rope_t[:, :, :], qk, cos_f[:, :].unsqueeze(1).to_broadcast([P, 2, SEQ]), MUL))
                    dve.wait_ge(rotated, i + 1)
                    link(dve.tensor_tensor(rope_u[:, :, :], turned_p[u][0].rearrange("p (a n) -> p a n", a=2),
                                           sin_f[:, :].unsqueeze(1).to_broadcast([P, 2, SEQ]), MUL))
                    dve.wait_ge(qk_scored, ii * 2 + CREDIT)
                    dve.tensor_tensor(qk_st[u][:, :, :], rope_t[:, :, :], rope_u[:, :, :], ADD).then_inc(roped, 1)
                softmax_rows(ii, 0, True)
            chain.end(PAIRS // 2)
            dve.wait_ge(o_read, PAIRS + CREDIT)
            signal(h_ready)
            def merge(j, bank, s):
                dve.wait_ge(drained, j + DRAINED["attn_out"])
                link(dve.tensor_tensor(merge_t[:, :, :], bank, pj[:, ds(j * 2 + GA0, 2), :], MUL))
                return dve.tensor_tensor(pj[:, ds(j * 2, 2), :], pj[:, ds(j * 2, 2), :], merge_t[:, :, :], ADD)
            drain("attn_out", merge)
            dve.wait_ge(drained, DRAINED["attn_out"] + 4)
            split_h(pj[:, 0:KT, :])
            drain_x("mix_out")
            def gated(name, weighted=False):
                c0, n = FIRST[name]
                base = ROUNDS[name]

                def product(i, c):
                    dve.wait_ge(silu_ready, i + (base + 1))
                    dve.wait_ge(hid_ready, i + base)
                    dve.wait_ge(chunk_used, c.c + 1)
                    dve.tensor_tensor(hid[:, :, :], silu_g[:, :].rearrange("p (a n) -> p a n", a=2), pair(c.slot), MUL)\
                        .then_inc(banks_read, 1)
                    dve.wait_ge(banks_read, i + (base + 1))
                    if weighted:
                        link(dve.tensor_tensor(hid[:, :, :], hid[:, :, :], comb[:, ds(i, 1), :].to_broadcast([P, 2, SEQ]), MUL))

                def split(i):
                    link(dve.tensor_copy(hid_hi[:, :, :], hid[:, :, :]))
                    dve.tensor_tensor(hid_lo[:, :, :], hid[:, :, :], hid_hi[:, :, :].bitcast(f32), SUB).then_inc(hid_ready, 1)

                dve.wait_ge(chunk_used, c0 + 1)
                part(Chunk(c0))
                product(0, Chunk(c0 + 1))
                part(Chunk(c0 + 1))
                split(0)
                rounds = n // 3 - 1
                looped = rounds - (1 if c0 + n == TOTAL else 0)
                for i, c, g in mlp_rounds(dve, name):
                    if g is i:
                        chain.begin(i, 2 if weighted else 1)
                    dve.wait_ge(chunk_used, Chunk(c, g).c + 1)
                    part(Chunk(c, g))
                    product(i + 1, Chunk(c + 1, g))
                    part(Chunk(c + 1, g))
                    dve.wait_ge(chunk_used, Chunk(c + 2, g).c + 1)
                    split(i + 1)
                    part(Chunk(c + 2, g))
                    if g is i:
                        chain.end(looped)
                for t in range(TT):
                    dve.wait_ge(chunk_used if t else acc_top, c0 + n if t else GATED.index(name) + (2 if name != "experts" else 1))
                    dve.tensor_copy(x[:, t, :], acc[:, 2 * t:2 * t + 2, :].rearrange("p m n -> p (m n)"))\
                        .then_inc(x_ready if t else x_top, 1)

            def short_conv(layer):
                cols = ROW["a_conv_w_2"] + layer * 3 * KT

                def rest(j):
                    tiles = slice(2 * j, 2 * j + 2)
                    if j == KT // 2 - 1:
                        split(slice(0, 2 * j))
                    for m in (2 * j, 2 * j + 1):
                        dve.wait_ge(a_first, layer * KT + m + 1)
                        dve.scalar_tensor_tensor(out=acv[:, m, 1:], in0=cu[:, m, 0:SEQ - 1], scalar=params[:, cols + m:cols + m + 1],
                                                 in1=acv[:, m, 1:], op0=MUL, op1=ADD).then_inc(a_taps, 1)
                    for k, m in enumerate((2 * j, 2 * j + 1)):
                        dve.wait_ge(a_taps, 2 * KT * layer + 4 * j + k + 1)
                        w = cols + 2 * KT + m
                        dve.scalar_tensor_tensor(out=acv[:, m, 0:SEQ - 1], in0=cu[:, m, 1:], scalar=params[:, w:w + 1],
                                                 in1=acv[:, m, 0:SEQ - 1], op0=MUL, op1=ADD).then_inc(a_taps, 1)
                    dve.wait_ge(a_taps, 2 * KT * layer + 4 * j + 4)
                    link(dve.tensor_tensor(acv[:, tiles, :], acv[:, tiles, :], pj[:, tiles, :], MUL))
                    if j == KT // 2 - 1:
                        split(slice(2 * j, KT))
                        signal(h_ready)

                def split(tiles):
                    link(dve.tensor_copy(h_hi[:, tiles, :], acv[:, tiles, :]))
                    dve.tensor_tensor(h_lo[:, tiles, :], acv[:, tiles, :], h_hi[:, tiles, :].bitcast(f32), SUB).then_inc(a_split, 1)
                drain(f"a_u{layer}", lambda j, bank, s: dve.tensor_tensor(
                    cu[:, 2 * j:2 * j + 2, :], bank, pj[:, KT + 2 * j:KT + 2 * j + 2, :], MUL),
                      {j: lambda j=j: rest(j) for j in range(KT // 2)}, urgent=True)

            def filter_angle(layer):
                dve.wait_ge(hyena_tables, 16 * HYENA_DMAS)
                dve.wait_ge(f_summed, layer + 1)
                link(dve.tensor_scalar(f_hid[:, :], misc[0:HIDDEN, layer * SEQ:(layer + 1) * SEQ], (f_b1, f_b2)[layer][:, 0:1],
                                       f_freq[:, 0:1], ADD, MUL))
                reduce_angle(dve, link, f_hid[:, :], f_k[:, :])
                signal(f_angle)

            def hyena_taps(first, end):
                w = ROW["c_short_w_2"]
                with dve.Fori(first, end) as m:
                    dve.wait_ge(hc_first, m + 1)
                    tile, src = [a[:, ds(m, 1), :].rearrange("p o n -> p (o n)") for a in (hc, pj)]
                    dve.scalar_tensor_tensor(out=tile[:, 1:], in0=src[:, 0:SEQ - 1], scalar=params[:, ds(m + w, 1)],
                                             in1=tile[:, 1:], op0=MUL, op1=ADD).then_inc(hc_taps, 1)
                    dve.wait_ge(hc_taps, m * 2 + 1)
                    dve.scalar_tensor_tensor(out=tile[:, 0:SEQ - 1], in0=src[:, 1:], scalar=params[:, ds(m + (w + 6 * KT), 1)],
                                             in1=tile[:, 0:SEQ - 1], op0=MUL, op1=ADD).then_inc(hc_taps, 1)

            def hyena_vector():
                dve.wait_ge(hc_taps, 6 * KT)
                with dve.Fori(0, D // HALF) as half:
                    chain.begin(half, ORDER * 28)
                    for n in range(ORDER):
                        b = half * ORDER + n
                        for v in range(2):
                            cols = slice(v * COLS, (v + 1) * COLS)
                            even, odd, forward = f_even[:, :, cols], f_odd[:, :, cols], pair_of(acc[:, 2 * v, :])
                            decay_v = f_decay[:, :, ds(half * HALF + v * COLS, COLS)]
                            dve.wait_ge(rev_copied, b * 2 + (v + 1))
                            dve.wait_ge(h_summed, b * 2 + CREDIT)
                            dve.wait_ge(abs_ready, b * 4 + CREDIT)
                            link(dve.tensor_tensor(even, forward, f_rev[:, :, cols], ADD))
                            link(dve.tensor_tensor(odd, forward, f_rev[:, :, cols], SUB))
                            link(dve.tensor_tensor(even, even, decay_v, MUL))
                            link(dve.tensor_tensor(odd, odd, decay_v, MUL))
                            dve.memset(f_odd[0:1, 0, cols], 0.0).then_inc(parity_ready, 1)
                        for v in range(2):
                            cols = slice(v * COLS, (v + 1) * COLS)
                            dve.wait_ge(abs_ready, b * 4 + (2 * v + 2) + CREDIT)
                            dve.tensor_tensor(f_abs[:, 0, :, cols], f_abs[:, 0, :, cols], f_abs[:, 1, :, cols], ALU.max)\
                                .then_inc(mag_ready, 1)
                        for v in range(2):
                            cols = slice(v * COLS, (v + 1) * COLS)
                            dve.wait_ge(norm_summed, b * 2 + (v + 1))
                            link(dve.reciprocal(f_inv[:, cols], side[v][:, 1, :]))
                            dve.wait_ge(h_summed, b * 2 + (v + 1) + CREDIT)
                            norm_v = f_inv[:, cols].unsqueeze(1).to_broadcast([P, TT, COLS])
                            link(dve.tensor_tensor(hs_re[:, :, cols], pair_of(acc[:, 2 * v, :]), norm_v, MUL))
                            link(dve.tensor_tensor(hs_im[:, :, cols], pair_of(acc[:, 2 * v + 1, :]), norm_v, MUL))
                            dve.tensor_tensor(hs_re2[:, cols], side[v][:, 0, :], f_inv[:, cols], MUL).then_inc(h_scaled, 1)
                        for v in range(2):
                            cols = slice(v * COLS, (v + 1) * COLS)
                            re, im, tmp = ys[:, 0:2, cols], ys[:, 2:4, cols], ys_t[:, :, cols]
                            u_re, u_im = pair_of(acc[:, 2 * v, :]), pair_of(acc[:, 2 * v + 1, :])
                            dve.wait_ge(u_summed, b * 2 + (v + 1) + CREDIT)
                            dve.wait_ge(h_scaled, b * 2 + (v + 1))
                            link(dve.tensor_tensor(re, u_re, hs_re[:, :, cols], MUL))
                            link(dve.tensor_tensor(tmp, u_im, hs_im[:, :, cols], MUL))
                            link(dve.tensor_tensor(re, re, tmp, SUB))
                            link(dve.tensor_tensor(im, u_re, hs_im[:, :, cols], MUL))
                            link(dve.tensor_tensor(ys_t[:, 0, cols], u_im[:, 0, :], hs_re2[:, cols], MUL))
                            link(dve.tensor_tensor(ys_t[:, 1, cols], u_im[:, 1, :], hs_re[:, 1, cols], MUL))
                            dve.tensor_tensor(im, im, tmp, ADD).then_inc(ys_ready, 1)
                        for v in range(2):
                            dve.wait_ge(y_summed, b * 2 + (v + 1) + CREDIT)
                            dve.wait_ge(ys_ready, b * 2 + 2 + CREDIT)
                            dve.wait_ge(z_made, b * 2 + v + CREDIT)
                            z = ys_t[:, v, :].rearrange("p (m n) -> p m n", n=SEQ)
                            for m in range(2):
                                skip = params[:, ds(half * (KT // 2) + (ROW["c_f_skip_2"] + n * KT + 2 * v + m), 1)]
                                last = dve.scalar_tensor_tensor(out=z[:, m, :], in0=u_st[:, 2 * v + m, :], scalar=skip,
                                                                in1=pair(1 + v)[:, m, :], op0=MUL, op1=ADD)
                            link(last)
                            gate = hc[:, ds(half * (KT // 2) + ((n + 1) * KT + 2 * v), 2), :]
                            dest = hc[:, ds(half * (KT // 2) + 2 * v, 2), :] if n == ORDER - 1 else u_st[:, 2 * v:2 * v + 2, :]
                            dve.tensor_tensor(dest, z[:, :, :], gate, MUL).then_inc(z_made, 1)
                chain.end(D // HALF)
                dve.wait_ge(z_made, 4 * ORDER + CREDIT)
                split_h(hc[:, 0:KT, :])

            norm("moe")
            dve.wait_ge(router_tables, 16 * ROUTER_DMAS)
            link(dve.memset(g_pad[:, :, :], -3e38))
            dve.wait_ge(routed, 1)
            link(dve.tensor_tensor(logits[:, :, :], misc[:, 0:TT * NL].rearrange("p (t n) -> p t n", t=TT),
                                   b_route[:, :].unsqueeze(1).to_broadcast([P, TT, NL]), ADD))
            link(dve.tensor_copy(g_pad[:, :, 0:N_GROUPS], logits[:, :, 0:N_GROUPS]))
            for t in range(TT):
                link(dve.max(g_top[:, t, :], g_pad[:, t, :]))
            dve.tensor_scalar(g_neg[:, :], g_top[:, :, 0], -1.0, None, MUL).then_inc(gaps_e, 1)
            for t in range(TT):
                link(dve.max_index(out=g_idx[:, t, :], in_max=g_top[:, t, :], in_values=g_pad[:, t, :]))
            link(dve.tensor_copy(g_idxf[:, :], g_idx[:, :, 0]))
            for t in range(TT):
                link(dve.tensor_scalar(g_hot[:, t, :], iota8[:, 0:N_GROUPS], g_idxf[:, t:t + 1], None, ALU.is_equal))
            for t in range(TT):
                link(dve.tensor_tensor(e_prod[:, t, :].rearrange("p (g e) -> p g e", g=N_GROUPS),
                                       logits[:, t, N_GROUPS:].rearrange("p (g e) -> p g e", g=N_GROUPS),
                                       g_hot[:, t, :].unsqueeze(2).to_broadcast([P, N_GROUPS, GROUP_EXPERTS]), MUL))
            for t in range(TT):
                link(dve.tensor_reduce(e_sel[:, t, :], e_prod[:, t, :].rearrange("p (g e) -> p e g", g=N_GROUPS), AX.X, ADD))
            for t in range(TT):
                link(dve.max(e_top[:, t, :], e_sel[:, t, :]))
            dve.tensor_tensor(e_gap[:, :], e_top[:, :, 1], e_top[:, :, 0], SUB).then_inc(gaps_e, 1)
            for t in range(TT):
                link(dve.max_index(out=e_idx[:, t, :], in_max=e_top[:, t, :], in_values=e_sel[:, t, :]))
            link(dve.tensor_copy(e_idxf[:, :, :], e_idx[:, :, 0:2]))
            for t in range(TT):
                for k in range(2):
                    link(dve.tensor_scalar(e_hot[:, t, k, :], iota8[:, :], e_idxf[:, t, k:k + 1], None, ALU.is_equal))
            dve.wait_ge(exp_e, 3)
            link(dve.reciprocal(g_w[:, :], g_sum[:, :]))
            link(dve.tensor_scalar(e_den[:, :], e_exp[:, :], 1.0, None, ADD))
            link(dve.reciprocal(e_den[:, :], e_den[:, :]))
            link(dve.tensor_tensor(e_w[:, :, 0], e_den[:, :], g_w[:, :], MUL))
            link(dve.tensor_tensor(e_w[:, :, 1], e_w[:, :, 0], e_exp[:, :], MUL))
            for t in range(TT):
                link(dve.tensor_scalar(e_wt[:, t, :], e_hot[:, t, 0, :], e_w[:, t, 0:1], None, MUL))
                link(dve.scalar_tensor_tensor(out=e_wt[:, t, :], in0=e_hot[:, t, 1, :], scalar=e_w[:, t, 1:2],
                                              in1=e_wt[:, t, :], op0=MUL, op1=ADD))
            for t in range(TT):
                link(dve.tensor_tensor(comb_t[:, t, :, :], g_hot[:, t, :].unsqueeze(2).to_broadcast([P, N_GROUPS, GROUP_EXPERTS]),
                                       e_wt[:, t, :].unsqueeze(1).to_broadcast([P, N_GROUPS, GROUP_EXPERTS]), MUL))
            signal(comb_made)
            dve.wait_ge(comb_turned, 1)
            dve.tensor_copy(comb_f[:, :], misc[0:EXPERTS, SEQ:2 * SEQ]).then_inc(comb_f_ready, 1)
            for k in range(1, EXPERTS // 2, 2):
                dve.wait_ge(comb_spread, k + 1)
                dve.tensor_copy(comb[:, 2 * k:2 * k + 2, :], pair_of(acc[:, k % 4, :])).then_inc(comb_dve, 1)
            dve.wait_ge(comb_act, EXPERTS // 4)
            dve.wait_ge(comb_dve, EXPERTS // 4)
            gated("experts", True)
            norm("ple")
            dve.wait_ge(p_split, 1)
            dve.tensor_tensor(hid_lo[:, :, :], misc[:, :].rearrange("p (a n) -> p a n", a=2),
                              hid_hi[:, :, :].bitcast(f32), SUB).then_inc(p_low, 1)
            c = Chunk(FIRST["ple"][0])
            dve.wait_ge(chunk_used, c.c + 1)
            part(c)

            def add_ple(j, bank, s):
                dve.wait_ge(gate_sig, j + 1)
                dve.wait_ge(drained, j + DRAINED["ple_gate"])
                xs = x[:, :, ds(j * COLS, COLS)]
                link(dve.tensor_tensor(gate_m[:, :, :], gate_s[:, :, :],
                                       acc[:, :, :].rearrange("p (t m) n -> p t (m n)", t=TT)[:, :, ds(j * COLS, COLS)], MUL))
                return dve.tensor_tensor(xs, xs, gate_m[:, :, :], ADD)
            drain("ple_gate", add_ple)
            dve.wait_ge(drained, DRAINED["ple_gate"] + FIRST["ple_gate"][1])
            signal(x_ready)
            dve.wait_ge(late_tables, 16 * LATE_DMAS)
            for t in range(TT):
                dve.wait_ge(inv_ready, TT * SQUARED.index("final") + t + 1)
                dve.scalar_tensor_tensor(out=x[:, t, :], in0=x[:, t, :], scalar=inv[:, t:t + 1], in1=final_w[:, :],
                                         op0=MUL, op1=MUL).then_inc(scaled_ready, 1)
            dve.wait_ge(scaled_ready, TT * (SQUARED.index("final") + 1))
            signal(x_ready)
            part(last_chunk(BEFORE["final"]))
            norm("mix0")
            drain_to("a_bc0", 0)
            short_conv(0)
            drain_x("a_out0")
            norm("ffn0")
            gated("ffn0")
            norm("mix1")
            drain_to("b_qk", 0)
            dve.wait_ge(late_tables, 16 * LATE_DMAS)
            link(dve.tensor_scalar(qk_gain[:, 0:1], qk_gain[:, 0:1], HD ** -0.5, None, MUL))
            link(dve.tensor_copy(head_cols[:, :, :].rearrange("k i (h c) -> k i h c", h=2),
                                 ident[0:HEADS, 0:HEADS].rearrange("k (i h) -> k i h", h=2).unsqueeze(3)
                                 .to_broadcast([HEADS, PAIRS, 2, HD])))

            def invert(a):
                dve.wait_ge(qk_root, a + 1)
                dve.reciprocal(qk_rms[:, a, :, :], qk_rms[:, a, :, :]).then_inc(qk_inverted, 1)

            def normalize(a):
                dve.wait_ge(rms_spread, a + 1)
                qk = pj[:, a * KT:(a + 1) * KT, :]
                dve.scalar_tensor_tensor(out=qk, in0=qk, scalar=qk_gain[:, a:a + 1],
                                         in1=acc[:, :, :].rearrange("p m (a n) -> p (m a) n", a=2),
                                         op0=MUL, op1=MUL).then_inc(qk_normed, 1)
            drain("b_v", lambda j, bank, s: dve.tensor_copy(v_t[:, :, ds(j * COLS, COLS)], bank),
                  {0: lambda: invert(0), 1: lambda: invert(1), 2: lambda: normalize(0), 3: lambda: normalize(1)})
            with dve.Fori(0, PAIRS // 2) as ii:
                chain.begin(ii, 2)
                softmax_rows(ii, PAIRS, False)
            chain.end(PAIRS // 2)
            dve.wait_ge(o_read, 2 * PAIRS + CREDIT)
            signal(h_ready)
            drain_x("na_out")
            norm("ffn1")
            gated("ffn1")
            norm("mix2")
            drain_to("hy_v", 0)
            hyena_taps(0, KT)
            drain_to("hy_x1", KT)
            hyena_taps(KT, 2 * KT)

            def rest(j):
                hyena_taps(2 * KT + 2 * j, 2 * KT + 2 * j + 2)
                if j in (0, 2):
                    filter_angle(j // 2)
            drain("hy_x2", lambda j, bank, s: dve.tensor_copy(pj[:, ds(j * 2 + 2 * KT, 2), :], bank),
                  {j: lambda j=j: rest(j) for j in range(KT // 2)})
            hyena_vector()
            drain_x("hy_out")
            norm("ffn2")
            gated("ffn2")
            norm("mix3")
            drain_to("a_bc1", 0)
            short_conv(1)
            drain_x("a_out1")
            norm("ffn3")
            gated("ffn3")

    return nc


def reduce_angle(dve, link, angle, k):
    ALU = mybir.AluOpType
    link(dve.tensor_scalar(k, angle, 1.0 / (2 * math.pi), ROUND, ALU.mult, ALU.add))
    link(dve.tensor_scalar(k, k, -ROUND, None, ALU.add))
    for part in (TWO_PI_1, TWO_PI_2, TWO_PI_3):
        link(dve.scalar_tensor_tensor(out=angle, in0=k, scalar=-part, in1=angle, op0=ALU.mult, op1=ALU.add))


INPUTS = ["x", "p", "positions", "attn_norm_w", "w_in", "conv_w", "conv_b", "dt_bias", "a_log", "d_skip", "ssd_norm_w",
          "w_ssd_out", "w_attn_out", "w_out", "moe_norm_w", "w_router_group", "b_router_group", "w_router_expert",
          "b_router_expert", "w_exp_gate", "w_exp_up", "w_exp_down", "ple_norm_w", "w_ple", "w_ple_gate",
          "final_norm_w", "norm_mix_g_2", "norm_ffn_g_2", "a_w_in_2", "a_conv_w_2", "a_w_out_2", "b_w_qkv_2",
          "b_q_norm_g_2", "b_k_norm_g_2", "b_rpb_2", "b_w_out_2", "c_w_in_2", "c_short_w_2", "c_short_b_2",
          "c_f_w1_2", "c_f_b1_2", "c_f_w2_2", "c_f_b2_2", "c_f_w3_2", "c_f_freq_2", "c_f_skip_2", "c_w_out_2",
          "f_w13_2", "f_w2_2"]


def kernel(**inputs):
    import numpy as _np
    import concourse.bacc as _bacc
    from concourse import mybir as _mybir
    from concourse.bass_utils import run_bass_kernel_spmd as _run

    nc = _bacc.Bacc("TRN2", target_bir_lowering=False, num_devices=1)
    arrays, views = {}, {}
    for name, a in [(n, _np.asarray(inputs[n])) for n in INPUTS] + list(constants().items()):
        a = _np.ascontiguousarray(a)
        arrays[f"in_{name}_dram"] = a
        views[name] = nc.dram_tensor(f"in_{name}_dram", a.shape, _mybir.dt.from_np(a.dtype), kind="ExternalInput").ap()
    out = nc.dram_tensor("out_0_dram", (1, SEQ, D), _mybir.dt.float32, kind="ExternalOutput").ap()
    build(nc, views, out)
    r = _run(nc, [arrays], core_ids=[0])
    return r.results[0]["out_0_dram"]
```
